# Optimizing a Trainium2 kernel written in Bass

```python
import math
import jax, jax.numpy as jnp
from jax import lax
import numpy as np

D_MODEL = 1024
BATCH = 1
SEQ = 256
DEPTH = 2

N_MIXERS = 2
D_FF = 2816
NORM_EPS = 1e-6
N_NORMS = 6
MACARON_WEIGHT = 0.5

GLA_HEADS = 4
GLA_DK = D_MODEL // 2
GLA_DV = D_MODEL
GLA_HK = GLA_DK // GLA_HEADS
GLA_HV = GLA_DV // GLA_HEADS
GLA_RANK = 16
GLA_GATE_NORMALIZER = 16.0
GLA_CHUNK = 64
GLA_IN = 2 * GLA_DK + 2 * GLA_DV + GLA_RANK

SSD_EXPAND = 2
SSD_DI = SSD_EXPAND * D_MODEL
SSD_HEADDIM = 64
SSD_HEADS = SSD_DI // SSD_HEADDIM
SSD_STATE = 128
SSD_GROUPS = 8
SSD_HPG = SSD_HEADS // SSD_GROUPS
SSD_CONV = 4
SSD_CHUNK = 64
SSD_CONV_DIM = SSD_DI + 2 * SSD_GROUPS * SSD_STATE
SSD_IN = SSD_DI + SSD_CONV_DIM + SSD_HEADS

kernel_name = 'hybrid_gla_ssd_macaron_sandwich'

def rmsnorm(x, g):
    xf = x.astype(jnp.float32)
    y = xf * lax.rsqrt(jnp.mean(xf * xf, axis=-1, keepdims=True) + NORM_EPS)
    return (y * g.astype(jnp.float32)).astype(x.dtype)

def swiglu(h, w_gate, w_up, w_down):
    return (jax.nn.silu(h @ w_gate) * (h @ w_up)) @ w_down

def gla_mixer(h, w_in, w_gk2, b_gk, g_norm, w_out):
    f32 = jnp.float32
    bsz, t_len, _ = h.shape
    n = t_len // GLA_CHUNK
    proj = h @ w_in
    q, k, v, r, lr = jnp.split(proj, [GLA_DK, 2 * GLA_DK, 2 * GLA_DK + GLA_DV, 2 * GLA_DK + 2 * GLA_DV], axis=-1)
    gk = jax.nn.log_sigmoid((lr @ w_gk2 + b_gk).astype(f32)) / GLA_GATE_NORMALIZER
    qc = q.astype(f32).reshape(bsz, n, GLA_CHUNK, GLA_HEADS, GLA_HK) * (GLA_HK ** -0.5)
    kc = k.astype(f32).reshape(bsz, n, GLA_CHUNK, GLA_HEADS, GLA_HK)
    vc = v.astype(f32).reshape(bsz, n, GLA_CHUNK, GLA_HEADS, GLA_HV)
    gc = gk.reshape(bsz, n, GLA_CHUNK, GLA_HEADS, GLA_HK)
    b = jnp.cumsum(gc, axis=2)
    b_mid = b[:, :, GLA_CHUNK // 2:GLA_CHUNK // 2 + 1]
    q_in = qc * jnp.exp(b - b_mid)
    k_in = kc * jnp.exp(b_mid - b)
    causal = jnp.tril(jnp.ones((GLA_CHUNK, GLA_CHUNK), dtype=bool))
    scores = jnp.einsum('bcihd,bcjhd->bchij', q_in, k_in)
    scores = jnp.where(causal, scores, 0.0)
    o_intra = jnp.einsum('bchij,bcjhv->bcihv', scores, vc)
    b_last = b[:, :, -1]
    q_inter = qc * jnp.exp(b)
    k_state = kc * jnp.exp(b_last[:, :, None] - b)

    def step(state, xs):
        q_i, k_i, v_i, dec = xs
        o_i = jnp.einsum('bihd,bhdv->bihv', q_i, state)
        state = state * jnp.exp(dec)[..., None] + jnp.einsum('bjhd,bjhv->bhdv', k_i, v_i)
        return state, o_i

    s0 = jnp.zeros((bsz, GLA_HEADS, GLA_HK, GLA_HV), f32)
    xs = (jnp.moveaxis(q_inter, 1, 0), jnp.moveaxis(k_state, 1, 0), jnp.moveaxis(vc, 1, 0), jnp.moveaxis(b_last, 1, 0))
    _, o_inter = lax.scan(step, s0, xs)
    o = (o_intra + jnp.moveaxis(o_inter, 0, 1)).reshape(bsz, t_len, GLA_HEADS, GLA_HV)
    o = rmsnorm(o, g_norm.reshape(GLA_HEADS, GLA_HV)).reshape(bsz, t_len, GLA_DV)
    o = o.astype(h.dtype) * jax.nn.silu(r)
    return o @ w_out

def ssd_mixer(h, w_in, conv_w, conv_b, dt_bias, a_log, d_skip, g_norm, w_out):
    f32 = jnp.float32
    bsz, t_len, _ = h.shape
    n = t_len // SSD_CHUNK
    proj = h @ w_in
    z, xbc, dt = jnp.split(proj, [SSD_DI, SSD_DI + SSD_CONV_DIM], axis=-1)
    xbc = lax.conv_general_dilated(xbc, conv_w[:, None, :].astype(xbc.dtype), window_strides=(1,),
                                   padding=[(SSD_CONV - 1, 0)], dimension_numbers=('NWC', 'WIO', 'NWC'),
                                   feature_group_count=SSD_CONV_DIM)
    xbc = jax.nn.silu(xbc + conv_b)
    xs_, bm, cm = jnp.split(xbc, [SSD_DI, SSD_DI + SSD_GROUPS * SSD_STATE], axis=-1)
    dt = jax.nn.softplus(dt.astype(f32) + dt_bias.astype(f32))
    a = -jnp.exp(a_log.astype(f32)).reshape(SSD_GROUPS, SSD_HPG)
    x_c = xs_.astype(f32).reshape(bsz, n, SSD_CHUNK, SSD_GROUPS, SSD_HPG, SSD_HEADDIM)
    b_c = bm.astype(f32).reshape(bsz, n, SSD_CHUNK, SSD_GROUPS, SSD_STATE)
    c_c = cm.astype(f32).reshape(bsz, n, SSD_CHUNK, SSD_GROUPS, SSD_STATE)
    dt_c = dt.reshape(bsz, n, SSD_CHUNK, SSD_GROUPS, SSD_HPG)
    cs = jnp.cumsum(dt_c * a, axis=2)
    causal = jnp.tril(jnp.ones((SSD_CHUNK, SSD_CHUNK), dtype=bool))[:, :, None, None]
    seg = cs[:, :, :, None] - cs[:, :, None, :]
    decay = jnp.exp(jnp.where(causal, seg, -jnp.inf))
    cb = jnp.einsum('bcigs,bcjgs->bcijg', c_c, b_c)
    wmat = cb[..., None] * decay * dt_c[:, :, None]
    y_diag = jnp.einsum('bcijgh,bcjghp->bcighp', wmat, x_c)
    cs_last = cs[:, :, -1]
    w_state = jnp.exp(cs_last[:, :, None] - cs) * dt_c
    c_dec = jnp.exp(cs)

    def step(state, xs):
        c_i, cd_i, b_i, w_i, x_i, dl = xs
        y_i = jnp.einsum('blgs,bghps,blgh->blghp', c_i, state, cd_i)
        state = state * jnp.exp(dl)[..., None, None] + jnp.einsum('blgs,blgh,blghp->bghps', b_i, w_i, x_i)
        return state, y_i

    s0 = jnp.zeros((bsz, SSD_GROUPS, SSD_HPG, SSD_HEADDIM, SSD_STATE), f32)
    xs = (jnp.moveaxis(c_c, 1, 0), jnp.moveaxis(c_dec, 1, 0), jnp.moveaxis(b_c, 1, 0),
          jnp.moveaxis(w_state, 1, 0), jnp.moveaxis(x_c, 1, 0), jnp.moveaxis(cs_last, 1, 0))
    _, y_off = lax.scan(step, s0, xs)
    y = y_diag + jnp.moveaxis(y_off, 0, 1) + d_skip.astype(f32).reshape(SSD_GROUPS, SSD_HPG)[..., None] * x_c
    y = y.reshape(bsz, t_len, SSD_DI)
    y = y * jax.nn.silu(z.astype(f32))
    y = rmsnorm(y.reshape(bsz, t_len, SSD_GROUPS, SSD_DI // SSD_GROUPS),
                g_norm.reshape(SSD_GROUPS, SSD_DI // SSD_GROUPS)).reshape(bsz, t_len, SSD_DI)
    return y.astype(h.dtype) @ w_out

def setup_inputs(seed: int = 0) -> dict:
    key = jax.random.key(seed)
    ks = jax.random.split(key, 20)
    f32 = jnp.float32
    n_gla = (DEPTH + 1) // 2
    n_ssd = DEPTH // 2

    def nrm(k, shape, scale):
        return jax.random.normal(k, shape, f32) * scale

    x = nrm(ks[0], (BATCH, SEQ, D_MODEL), 1.0)
    ffn_w_gate = nrm(ks[1], (DEPTH, 2, D_MODEL, D_FF), D_MODEL ** -0.5)
    ffn_w_up = nrm(ks[2], (DEPTH, 2, D_MODEL, D_FF), D_MODEL ** -0.5)
    ffn_w_down = nrm(ks[3], (DEPTH, 2, D_FF, D_MODEL), D_FF ** -0.5)
    norm_gain = 1.0 + nrm(ks[4], (DEPTH, N_NORMS, D_MODEL), 0.05)
    gla_w_in = nrm(ks[5], (n_gla, D_MODEL, GLA_IN), D_MODEL ** -0.5)
    gla_w_gk2 = nrm(ks[6], (n_gla, GLA_RANK, GLA_DK), GLA_RANK ** -0.5)
    gla_b_gk = nrm(ks[7], (n_gla, GLA_DK), 0.1)
    gla_norm = 1.0 + nrm(ks[8], (n_gla, GLA_DV), 0.05)
    gla_w_out = nrm(ks[9], (n_gla, GLA_DV, D_MODEL), GLA_DV ** -0.5)
    ssd_w_in = nrm(ks[10], (n_ssd, D_MODEL, SSD_IN), D_MODEL ** -0.5)
    ssd_conv_w = nrm(ks[11], (n_ssd, SSD_CONV, SSD_CONV_DIM), SSD_CONV ** -0.5)
    ssd_conv_b = nrm(ks[12], (n_ssd, SSD_CONV_DIM), 0.05)
    dt0 = jnp.exp(jax.random.uniform(ks[13], (n_ssd, SSD_HEADS), f32, math.log(1e-3), math.log(0.1)))
    ssd_dt_bias = dt0 + jnp.log(-jnp.expm1(-dt0))
    ssd_A_log = jnp.log(jax.random.uniform(ks[14], (n_ssd, SSD_HEADS), f32, 1.0, 16.0))
    ssd_D = 1.0 + nrm(ks[15], (n_ssd, SSD_HEADS), 0.1)
    ssd_norm = 1.0 + nrm(ks[16], (n_ssd, SSD_DI), 0.05)
    ssd_w_out = nrm(ks[17], (n_ssd, SSD_DI, D_MODEL), SSD_DI ** -0.5)
    return {'x': x, 'ffn_w_gate': ffn_w_gate, 'ffn_w_up': ffn_w_up, 'ffn_w_down': ffn_w_down,
            'norm_gain': norm_gain, 'gla_w_in': gla_w_in, 'gla_w_gk2': gla_w_gk2, 'gla_b_gk': gla_b_gk,
            'gla_norm': gla_norm, 'gla_w_out': gla_w_out, 'ssd_w_in': ssd_w_in, 'ssd_conv_w': ssd_conv_w,
            'ssd_conv_b': ssd_conv_b, 'ssd_dt_bias': ssd_dt_bias, 'ssd_A_log': ssd_A_log, 'ssd_D': ssd_D,
            'ssd_norm': ssd_norm, 'ssd_w_out': ssd_w_out}

def reference(x, ffn_w_gate, ffn_w_up, ffn_w_down, norm_gain, gla_w_in, gla_w_gk2, gla_b_gk, gla_norm,
              gla_w_out, ssd_w_in, ssd_conv_w, ssd_conv_b, ssd_dt_bias, ssd_A_log, ssd_D, ssd_norm, ssd_w_out):
    for i in range(DEPTH):
        g = norm_gain[i]
        h = swiglu(rmsnorm(x, g[0]), ffn_w_gate[i, 0], ffn_w_up[i, 0], ffn_w_down[i, 0])
        x = x + MACARON_WEIGHT * rmsnorm(h, g[1])
        h = rmsnorm(x, g[2])
        j = i // N_MIXERS
        if i % N_MIXERS == 0:
            h = gla_mixer(h, gla_w_in[j], gla_w_gk2[j], gla_b_gk[j], gla_norm[j], gla_w_out[j])
        else:
            h = ssd_mixer(h, ssd_w_in[j], ssd_conv_w[j], ssd_conv_b[j], ssd_dt_bias[j], ssd_A_log[j],
                          ssd_D[j], ssd_norm[j], ssd_w_out[j])
        x = x + rmsnorm(h, g[3])
        h = swiglu(rmsnorm(x, g[4]), ffn_w_gate[i, 1], ffn_w_up[i, 1], ffn_w_down[i, 1])
        x = x + MACARON_WEIGHT * rmsnorm(h, g[5])
    return x


_drawn_inputs = setup_inputs


def setup_inputs(seed=0):
    import zlib

    import numpy as np

    out = dict(_drawn_inputs(seed))
    spreads = {}
    factors = {}
    for name, (base, spread) in spreads.items():
        noise = np.random.default_rng([zlib.crc32(name.encode()), seed]).standard_normal(out[name].shape)
        drawn = base * np.exp(spread * noise) if base else spread * noise
        out[name] = __import__('jax').numpy.asarray(drawn.astype(out[name].dtype))
    for name, factor in factors.items():
        out[name] = (out[name] * factor).astype(out[name].dtype)
    return out
```

```python
from contextlib import ExitStack

import concourse.bass as bass
from concourse import mybir

ALU = mybir.AluOpType
ACT = mybir.ActivationFunctionType
F32 = mybir.dt.float32
F32R = mybir.dt.float32r
I32 = mybir.dt.int32

P = 128
T = 256
NT = T // P
D = 1024
KD = D // P
D_FF = 2816
UW = 256
UNIT = KD * UW
NF = D_FF // UW
EPS = 1e-6
CH = 64
HPG = 4
HD = 64
GLA_H = 4
GLA_RANK = 16
SSD_G = 8
SSD_H = 32
DI = 2048
CONV = 4
MAGIC = float(0x5F3759DF)
SLOT_P1, SLOT_P2, SLOT_P3, SLOT_O = 0, 1, 2, 3
SLOT_GATE, SLOT_UP, SLOT_DOWN = 0, 1, 2
CONST_IDENT, CONST_ALL = 3, 16
SSD_WEIGHTS = 4
SSD_STEPS, GLA_STEPS = 32, 12

PHASES = [("ffn", 0, 0), ("gla", 0, 0), ("ffn", 0, 1), ("ffn", 1, 0), ("ssd", 0, 0), ("ffn", 1, 1)]
NPH = len(PHASES)


def uses_in(kind, slot):
    if kind == "ffn":
        return NF if slot < 3 else 0
    return GLA_H if kind == "gla" else SSD_G


def used_before(phase, slot):
    return sum(uses_in(PHASES[q][0], slot) for q in range(phase))


def groups_before(kind):
    return 0 if kind == "gla" else GLA_H


def ffns_before(phase):
    return sum(PHASES[q][0] == "ffn" for q in range(phase))


def pipeline(eng, n, body):
    body(0, True, False, False)
    body(1, True, True, False)
    with eng.Fori(2, n) as g:
        body(g, True, True, True)
    body(n, False, True, True)
    body(n + 1, False, False, True)


class Links:

    def __init__(self, eng, sem):
        self.eng, self.sem, self.base, self.k = eng, sem, 0, 0

    def __call__(self, ins):
        self.k += 1
        ins.then_inc(self.sem, 1)
        self.eng.wait_ge(self.sem, self.base + self.k)

    def body(self, i, start, per):
        self.before = self.base + self.k
        self.base, self.k = i * per + (self.before - start * per), 0

    def after(self, n, per):
        assert self.k == per, (self.k, per)
        self.base, self.k = self.before + n * per, 0


def trunk(nc, x, ffn_w_gate, ffn_w_up, ffn_w_down, norm_gain, gla_w_in, gla_w_gk2, gla_b_gk,
          gla_norm, gla_w_out, ssd_w_in, ssd_conv_w, ssd_conv_b, ssd_dt_bias, ssd_A_log, ssd_D,
          ssd_norm, ssd_w_out, out):
    with ExitStack() as ctx:
        def sb(name, shape, dt=F32):
            return ctx.enter_context(nc.sbuf_tensor(name, shape, dt))

        def sem(name):
            return ctx.enter_context(nc.semaphore(name))

        raw = sb("raw", [P, 4, UNIT])
        ws = sb("ws", [P, 4, 2, UNIT], F32R)
        xres = sb("xres", [P, NT, D])
        xT = sb("xT", [P, KD, 2, T], F32R)
        hT = sb("hT", [P, 2, 2, T], F32R)
        exps = sb("exps", [P, 4096])
        scr = sb("scr", [P, 2, 2048])
        gpost = sb("gpost", [P, D])
        gpre = sb("gpre", [P, D])
        lo2 = sb("lo2", [P, 2, T])
        feat = sb("feat", [P, 4, CONV - 1 + T])
        ca = sb("ca", [P, 4, T])
        fm = sb("fm", [P, 4, T])
        xdt = sb("xdt", [P, NT, 256])
        xw = sb("xw", [P, NT, 256])
        dx = sb("dx", [P, NT, 256])
        wm = sb("wm", [P, NT, HPG, CH])
        zf = sb("zf", [P, NT, 256])
        zs = sb("zs", [P, NT, 256])
        vs = sb("vs", [P, NT, 256])
        yn = sb("yn", [P, NT, 256])
        dtw = sb("dtw", [P, KD, SSD_H])
        sw = sb("sw", [P, KD, 2, SSD_H], F32R)
        ident = sb("ident", [P, P])
        tri = sb("tri", [P, P])
        blk = sb("blk", [P, P])
        half = sb("half", [P, 2, P])
        mask = sb("mask", [P, CH])
        zr = sb("zr", [P, P], F32R)
        pcol = sb("pcol", [P, 2, P])
        xtok = scr[:, 0, 0:512].rearrange("p (t n) -> p t n", t=NT)
        st = scr[:, 0, 512:1280].rearrange("p (c n) -> p c n", c=3)
        bcb = scr[:, 0, 1280:1664]
        prow = scr[:, 1, 0:2 * P].rearrange("p (a n) -> p a n", a=2)
        lrw = exps[:, 0:KD * GLA_RANK].rearrange("p (k n) -> p k n", k=KD)
        wgk = xdt[0:GLA_RANK, :, :].rearrange("p t n -> p (t n)")
        lrT = dx[0:GLA_RANK, 0, :]
        lrt = sb("lrt", [P, NT, GLA_RANK])
        hb = sb("hb", [P, 3, SSD_H])
        dtv = sb("dtv", [P, 8, NT, SSD_H])
        edl = sb("edl", [P, 4, SSD_H])
        sm = sb("sm", [P, 32])
        ps = ctx.enter_context(nc.psum_tensor("ps", [P, 8, 512], F32))

        JUNK = scr[:, 1, 0:D]
        NORMED = scr[:, 0, :].rearrange("p (t d) -> p t d", t=NT)
        T1 = scr[:, 1, D:2 * D]
        DT, DA, CS, CSL, WST, CDEC, TA, TB = range(8)
        A, B, C, E = 4, 5, 6, 7
        CW0, CB0 = 0, 0
        GG0, GS0, GB0 = 32, 40, 56

        loaded = [sem(f"loaded{s}") for s in range(4)]
        hi_done = [sem(f"hi_done{s}") for s in range(4)]
        lo_done = [sem(f"lo_done{s}") for s in range(4)]
        tile_mm = [sem(f"tile_mm{s}") for s in range(4)]
        params_in, x_in = sem("params_in"), sem("x_in")
        gpre_in, gpost_in = sem("gpre_in"), sem("gpost_in")
        stored = sem("stored")
        consts = sem("consts")
        cols_T, cols_done = sem("cols_T"), sem("cols_done")
        dve_step = sem("dve_step")
        sq_post, sq_pre = sem("sq_post"), sem("sq_pre")
        post_read = sem("post_read")
        x_ready, xn_ready = sem("x_ready"), sem("xn_ready")
        xnT = sem("xnT")
        xT_hi, xT_lo = sem("xT_hi"), sem("xT_lo")
        gate_lo, up_lo = sem("gate_lo"), sem("up_lo")
        gate_sum, silu_g, h_done, h_hi, hT_ready = (sem(n) for n in (
            "gate_sum", "silu_g", "h_done", "h_hi", "hT_ready"))
        up_sum = sem("up_sum")
        small_hi, small_lo, small_mm, small_lo_out = (sem(n) for n in (
            "small_hi", "small_lo", "small_mm", "small_lo_out"))
        gla_mm, gla_dve, gla_act = sem("gla_mm"), sem("gla_dve"), sem("gla_act")
        ssd_mm, ssd_dve, ssd_act = sem("ssd_mm"), sem("ssd_dve"), sem("ssd_act")
        p1_lo, p2_lo, p3_lo = sem("p1_lo"), sem("p2_lo"), sem("p3_lo")
        p1_sum, p2_sum, p3_sum = sem("p1_sum"), sem("p2_sum"), sem("p3_sum")
        conv_done, feat_done = sem("conv_done"), sem("feat_done")
        tok_T, tok_out, tok_mul = sem("tok_T"), sem("tok_out"), sem("tok_mul")
        e_mm, e_out, w_done = sem("e_mm"), sem("e_out"), sem("w_done")
        upd_mm, state_done = sem("upd_mm"), sem("state_done")
        in_mm, off_mm = sem("in_mm"), sem("off_mm")
        y_done, y_sq, yn_done = sem("y_done"), sem("y_sq"), sem("yn_done")
        zs_done = sem("zs_done")
        yT_mm, yT_hi, yT_lo = sem("yT_mm"), sem("yT_hi"), sem("yT_lo")

        block = ctx.enter_context(nc.Block())

        @block.sync
        def _(sp):
            def at(value):
                return value if isinstance(value, int) else sp.snap(value)

            def cols(w, col, n=UW):
                return w.rearrange("(k p) n -> p k n", p=P)[:, :, bass.ds(col, n)]

            def load_cols(slot, w, col, count):
                dst = raw[:, slot, :].rearrange("p (k n) -> p k n", k=KD)
                src = cols(w, at(col))
                if count is not None:
                    sp.wait_ge(lo_done[slot], count)
                for h in (1, 0):
                    ks = slice(h * KD // 2, (h + 1) * KD // 2)
                    sp.dma_start(dst[:, ks, :], src[:, ks, :]).then_inc(loaded[slot], 16)

            def load_two(slot, w, col0, col1, count):
                dst = raw[:, slot, :].rearrange("p (k c n) -> p k c n", k=KD, c=2)
                starts = at(col0), at(col1)
                sp.wait_ge(lo_done[slot], count)
                for c, col in enumerate(starts):
                    sp.dma_start(dst[:, :, c, :], cols(w, col, P)).then_inc(loaded[slot], 16)

            def load_rows(slot, w, row, count):
                dst = raw[:, slot, :].rearrange("p (j n) -> p j n", j=2)
                starts = at(row), at(row + P)
                if count is not None:
                    sp.wait_ge(lo_done[slot], count)
                for j in (1, 0):
                    sp.dma_start(dst[:, j, :], w[bass.ds(starts[j], P), :]).then_inc(loaded[slot], 16)

            for t in range(NT):
                sp.dma_start(xres[:, t, :], x[0, t * P:(t + 1) * P, :]).then_inc(x_in, 16)

            def load_first(ph):
                if ph == NPH:
                    return
                kind, layer, which = PHASES[ph]
                count = used_before(ph, 0) if ph else None
                if kind == "ffn":
                    load_cols(SLOT_GATE, ffn_w_gate[layer, which], 0, count)
                elif kind == "gla":
                    load_two(SLOT_P1, gla_w_in[0], 0, 512, count)
                else:
                    load_cols(SLOT_P1, ssd_w_in[0], DI, count)

            load_first(0)
            for ph, (kind, layer, which) in enumerate(PHASES):
                n0 = [used_before(ph, s) for s in range(4)]
                if kind == "ffn":
                    wg, wu, wd = (w[layer, which] for w in (ffn_w_gate, ffn_w_up, ffn_w_down))

                    def load_ffn(i, fresh=False):
                        load_cols(SLOT_UP, wu, i * UW, None if fresh else i + n0[SLOT_UP])
                        if isinstance(i, int) and i == NF - 1:
                            load_first(ph + 1)
                        else:
                            load_cols(SLOT_GATE, wg, i * UW + UW, i + n0[SLOT_GATE] + 1)
                        load_rows(SLOT_DOWN, wd, i * UW, None if fresh else i + n0[SLOT_DOWN])
                    if ph == 0:
                        load_ffn(0, True)
                    with sp.Fori(1 if ph == 0 else 0, NF - 1) as i:
                        load_ffn(i)
                    load_ffn(NF - 1)
                else:
                    ssd = kind == "ssd"
                    n = SSD_G if ssd else GLA_H
                    w, wo = (ssd_w_in[0], ssd_w_out[0]) if ssd else (gla_w_in[0], gla_w_out[0])

                    def load_group(g, first):
                        if ssd:
                            if not first:
                                load_cols(SLOT_P1, w, g * UW + DI, g + n0[SLOT_P1])
                            load_two(SLOT_P2, w, g * P + 2 * DI, g * P + 2 * DI + 1024, g + n0[SLOT_P2])
                            load_cols(SLOT_P3, w, g * UW, g + n0[SLOT_P3])
                        else:
                            if not first:
                                load_two(SLOT_P1, w, g * P, g * P + 512, g + n0[SLOT_P1])
                            load_cols(SLOT_P2, w, g * UW + 2048, g + n0[SLOT_P2])
                            load_cols(SLOT_P3, w, g * UW + 1024, g + n0[SLOT_P3])

                    def load_out(g):
                        fresh = isinstance(g, int) and g + n0[SLOT_O] == 0
                        load_rows(SLOT_O, wo, g * UW, None if fresh else g + n0[SLOT_O])
                    load_group(0, True)
                    load_group(1, False)
                    load_out(0)
                    with sp.Fori(2, n) as g:
                        load_group(g, False)
                        load_out(g - 1)
                    load_first(ph + 1)
                    load_out(n - 1)
            for t in range(NT):
                sp.wait_ge(x_ready, NPH * NT - NT + t + 1)
                sp.dma_start(out[0, t * P:(t + 1) * P, :], xres[:, t, :]).then_inc(stored, 16)
            sp.wait_ge(stored, 16 * NT)

        @block.gpsimd
        def _(pool):
            step = Links(pool, consts)
            gain = norm_gain.rearrange("l n d -> (l n) d")

            def load_gain(dst, j, arrived):
                pool.dma_start(dst, gain[j:j + 1, :].broadcast_to([P, D])).then_inc(arrived, 16)

            load_gain(gpre[:, :], 0, gpre_in)
            load_gain(gpost[:, :], 1, gpost_in)
            step(pool.memset(prow[:, 1, :], 0.0))
            rows = "(t c) -> t c"
            for dst, src in (
                    (prow[:, 0, :], ssd_conv_w[0].rearrange("k (t c) -> (k t) c", c=P)),
                    (prow[0:32, 1, :], ssd_conv_b[0].rearrange(rows, c=P)),
                    (prow[GG0:GG0 + 8, 1, :], gla_norm[0].rearrange(rows, c=P)),
                    (prow[GS0:GS0 + 16, 1, :], ssd_norm[0].rearrange(rows, c=P)),
                    (prow[GB0:GB0 + 4, 1, :], gla_b_gk[0].rearrange(rows, c=P)),
                    (hb[:, 0, :], ssd_A_log.broadcast_to([P, SSD_H])),
                    (hb[:, 1, :], ssd_D.broadcast_to([P, SSD_H])),
                    (hb[:, 2, :], ssd_dt_bias.broadcast_to([P, SSD_H])),
                    (wgk, gla_w_gk2[0]),
                    (lrw[:, :, :], gla_w_in[0].rearrange("(k p) n -> p k n", p=P)[:, :, 3072:3072 + GLA_RANK]),
                    (dtw[:, :, :], ssd_w_in[0].rearrange("(k p) n -> p k n", p=P)[:, :, 6144:6144 + SSD_H])):
                pool.dma_start(dst, src).then_inc(params_in, 16)
            step(pool.memset(ident[:, :], 0.0))
            step(pool.affine_select(out=ident[:, :], in_=ident[:, :], compare_op=ALU.not_equal, fill=1.0, base=0,
                                    pattern=[[-1, P]], channel_multiplier=1))
            assert step.k == CONST_IDENT
            step(pool.memset(zr[:, :].bitcast(F32), 0.0))
            step(pool.memset(tri[:, :], 1.0))
            step(pool.affine_select(out=tri[:, :], in_=tri[:, :], compare_op=ALU.is_ge, fill=0.0, base=0,
                                    pattern=[[1, P]], channel_multiplier=-1))
            step(pool.memset(tri[0:CH, CH:P], 0.0))
            step(pool.memset(blk[:, :], 0.0))
            step(pool.memset(half[:, :, :], 0.0))
            for c in range(2):
                r = slice(c * CH, (c + 1) * CH)
                step(pool.tensor_copy(mask[r, :], tri[r, r]))
                step(pool.memset(blk[r, r], 1.0))
                step(pool.memset(half[r, c, :], 1.0))
            step(pool.memset(feat[:, :, 0:CONV - 1], 0.0))
            assert step.k == CONST_ALL

            def side_products(g, proj, scan, outp):
                if not scan:
                    return
                G = groups_before("ssd")
                hs = bass.ds((g - 1) * HPG, HPG)

                def heads(ap, n):
                    return ap.rearrange("p t (h o) -> p t h o", o=1).broadcast_to([P, n, HPG, HD])

                def by_head(buf):
                    return buf[:, :, :].rearrange("p t (h d) -> p t h d", h=HPG)
                pool.wait_ge(tok_out, g - 1 + G + 1)
                pool.tensor_tensor(out=by_head(xw), in0=by_head(xtok), in1=heads(dtv[:, WST, :, hs], NT),
                                   op=ALU.mult).then_inc(tok_mul, 1)
                pool.tensor_tensor(out=by_head(xdt), in0=by_head(xtok), in1=heads(dtv[:, DT, :, hs], NT),
                                   op=ALU.mult).then_inc(tok_mul, 1)
                if not (isinstance(g, int) and g == 1):
                    pool.wait_ge(yn_done, 2 * (g - 1 + G))
                for t in range(NT):
                    pool.tensor_tensor(out=by_head(dx)[:, t], in0=by_head(xtok)[:, t],
                                       in1=hb[:, 1, hs].rearrange("p (h o) -> p h o", o=1).broadcast_to([P, HPG, HD]),
                                       op=ALU.mult).then_inc(tok_mul, 1)

            for b in range(NPH):
                pool.wait_ge(xn_ready, NT * (b + 1))
                if b > 0:
                    load_gain(gpost[:, :], 2 * b + 1, gpost_in)
                if b + 1 < NPH:
                    load_gain(gpre[:, :], 2 * (b + 1), gpre_in)
                if PHASES[b][0] == "ssd":
                    pool.wait_ge(ssd_dve, SSD_WEIGHTS)
                    pipeline(pool, SSD_G, side_products)

        @block.scalar
        def _(act):
            def hi(slot, count):
                act.wait_ge(loaded[slot], (count + 1) * 32)
                if not (isinstance(count, int) and count == 0):
                    act.wait_ge(tile_mm[slot], count * 2)
                act.activation(ws[:, slot, 0, :], raw[:, slot, :], ACT.Copy).then_inc(hi_done[slot], 1)

            def low_halves(slot, count, banks, done):
                for c in range(2):
                    act.wait_ge(tile_mm[slot], count * 2 + c + 1)
                    act.activation(lo2[:, c, :], ps[:, banks + c, T:2 * T], ACT.Copy).then_inc(done, 1)

            def norm(b):
                if b > 0:
                    slot = SLOT_DOWN if PHASES[b - 1][0] == "ffn" else SLOT_O
                    for t in range(NT):
                        act.wait_ge(tile_mm[slot], 2 * used_before(b, slot) - 1 + t)
                        act.activation(JUNK, ps[:, 2 * t:2 * t + 2, :].rearrange("p b n -> p (b n)"), ACT.Square,
                                       accum_out=sm[:, t:t + 1]).then_inc(sq_post, 1)
                        act.wait_ge(sq_post, NT * (b - 1) + t + 1)
                if b == NPH:
                    return
                for t in range(NT):
                    if b == 0:
                        act.wait_ge(x_in, 16 * NT)
                    else:
                        act.wait_ge(x_ready, NT * (b - 1) + t + 1)
                    act.activation(JUNK, xres[:, t, :], ACT.Square, accum_out=sm[:, 2 + t:3 + t]).then_inc(sq_pre, 1)
                    act.wait_ge(sq_pre, NT * b + t + 1)
                for t in range(NT):
                    for q in range(2):
                        act.wait_ge(xnT, 2 * NT * b + 2 * t + q + 1)
                        act.activation(xT[:, 4 * q:4 * q + 4, 0, t * P:(t + 1) * P],
                                       ps[:, A + 2 * t + q, :].rearrange("p (k n) -> p k n", k=4),
                                       ACT.Copy).then_inc(xT_hi, 1)

            def ffn(ph):
                f = ffns_before(ph) * NF * 2
                n0 = [used_before(ph, s) for s in range(4)]
                last = ph == NPH - 1

                def body(i, split_next):
                    hi(SLOT_UP, i + n0[SLOT_UP])
                    low_halves(SLOT_GATE, i + n0[SLOT_GATE], A, gate_lo)
                    if split_next:
                        hi(SLOT_GATE, i + n0[SLOT_GATE] + 1)
                    for c in range(2):
                        act.wait_ge(gate_sum, i * 2 + f + c + 1)
                        act.activation(fm[:, c, :], ca[:, c, :], ACT.Silu).then_inc(silu_g, 1)
                    hi(SLOT_DOWN, i + n0[SLOT_DOWN])
                    low_halves(SLOT_UP, i + n0[SLOT_UP], C, up_lo)
                    for c in range(2):
                        act.wait_ge(h_done, i * 2 + f + c + 1)
                        act.activation(hT[:, c, 0, :], fm[:, 2 + c, :], ACT.Copy).then_inc(h_hi, 1)
                if ph == 0:
                    body(0, True)
                with act.Fori(1 if ph == 0 else 0, NF - 1 if last else NF) as i:
                    body(i, True)
                if last:
                    body(NF - 1, False)

            def gla_start():
                act.wait_ge(params_in, 16 * 11)
                act.activation(sw[:, :, 0, 0:GLA_RANK], lrw[:, :, :], ACT.Copy).then_inc(small_hi, 1)
                act.wait_ge(small_mm, 2)
                act.activation(lrt[:, :, :], ps[:, C:E + 1, GLA_RANK:2 * GLA_RANK], ACT.Copy).then_inc(small_lo_out, 1)
                et = scr[:, 0, 1024:2048]
                act.wait_ge(gla_dve, 3)
                act.activation(et, et, ACT.Exp, scale=-1.0).then_inc(gla_act, 1)
                act.wait_ge(gla_act, 1)
                act.activation(et, et, ACT.Ln, bias=1.0).then_inc(gla_act, 1)
                b16, dm, de = scr[:, 0, 0:1024], scr[:, 0, 1024:2048], scr[:, 1, 0:1024]
                act.wait_ge(gla_dve, 7)
                nrm = 1.0 / 16.0
                act.activation(exps[:, 0:1024], dm, ACT.Exp, scale=nrm).then_inc(gla_act, 1)
                act.activation(exps[:, 1024:2048], dm, ACT.Exp, scale=-nrm).then_inc(gla_act, 1)
                act.activation(exps[:, 2048:3072], b16, ACT.Exp, scale=nrm).then_inc(gla_act, 1)
                act.activation(exps[:, 3072:4096], de, ACT.Exp, scale=nrm).then_inc(gla_act, 1)
                act.activation(edl[:, 0, 0:16], b16.rearrange("p (n i) -> p n i", i=CH)[:, :, CH - 1], ACT.Exp,
                               scale=nrm).then_inc(gla_act, 1)

            def ssd_start():
                act.activation(sw[:, :, 0, :], dtw[:, :, :], ACT.Copy).then_inc(small_hi, 1)
                act.activation(hb[:, 0, :], hb[:, 0, :], ACT.Exp).then_inc(ssd_act, 1)
                act.wait_ge(small_mm, 4)
                act.activation(dtv[:, TA, :, :], ps[:, C:E + 1, SSD_H:2 * SSD_H], ACT.Copy).then_inc(small_lo_out, 1)
                act.wait_ge(ssd_dve, 1)
                act.activation(dtv[:, TB, :, :], dtv[:, TB, :, :], ACT.Exp, scale=-1.0).then_inc(ssd_act, 1)
                act.wait_ge(ssd_dve, 3)
                act.activation(dtv[:, CDEC, :, :], dtv[:, CS, :, :], ACT.Exp).then_inc(ssd_act, 1)
                act.activation(dtv[:, TB, :, :], dtv[:, TA, :, :], ACT.Exp).then_inc(ssd_act, 1)
                act.activation(edl[:, :, :], edl[:, :, :], ACT.Exp).then_inc(ssd_act, 1)
                for t in range(NT):
                    act.wait_ge(ssd_dve, SSD_WEIGHTS + 2 * t + 2)
                    act.activation(exps[:, t * 2048:(t + 1) * 2048], scr[:, 1, :], ACT.Exp).then_inc(ssd_act, 1)

            def mixer(ph, kind, n):
                G = groups_before(kind)
                n0 = [used_before(ph, s) for s in range(4)]
                ssd = kind == "ssd"
                gain0 = GS0 if ssd else GG0

                def body(g, proj, scan, outp):
                    first = isinstance(g, int) and g == 1
                    if proj:
                        hi(SLOT_P2, g + n0[SLOT_P2])
                    if scan:
                        if not (first and kind == "gla"):
                            act.wait_ge(yn_done, 2 * (g - 1 + G))
                        act.wait_ge(p3_sum if ssd else p2_sum, 2 * (g - 1 + G) + 2)
                        act.activation(zs[:, :, :], zf[:, :, :], ACT.Silu).then_inc(zs_done, 1)
                    if proj:
                        if not (isinstance(g, int) and g == 0):
                            act.wait_ge(p3_sum, (g + G) * 2)
                        low_halves(SLOT_P1, g + n0[SLOT_P1], A, p1_lo)
                    if outp:
                        act.wait_ge(yT_mm, g - 2 + G + 1)
                        for j in range(2):
                            act.activation(hT[:, j, 0, :], ps[:, C, j * T:(j + 1) * T], ACT.Copy,
                                           scale=pcol[:, 1, bass.ds(2 * g + (gain0 - 4 + j), 1)]).then_inc(yT_hi, 1)
                    if scan:
                        act.wait_ge(tok_T, g - 1 + G + 1)
                        if ssd:
                            if not first:
                                act.wait_ge(tok_mul, 4 * (g - 1))
                            act.activation(xtok[:, :, :].rearrange("p t n -> p (t n)"), ps[:, E, :],
                                           ACT.Copy).then_inc(tok_out, 1)
                        else:
                            act.activation(xw[:, :, 0:P], ps[:, E, 0:2 * P].rearrange("p (t n) -> p t n", t=2),
                                           ACT.Copy).then_inc(tok_out, 1)
                    if proj:
                        hi(SLOT_P3, g + n0[SLOT_P3])
                        low_halves(SLOT_P2, g + n0[SLOT_P2], A, p2_lo)
                    if scan and ssd:
                        act.wait_ge(e_mm, g - 1 + G + 1)
                        act.activation(bcb[:, :], ps[:, C, 0:384], ACT.Copy).then_inc(e_out, 1)
                    if proj:
                        hi(SLOT_P1, g + n0[SLOT_P1] + 1)
                    if scan:
                        if ssd:
                            act.wait_ge(y_done, g)
                        else:
                            act.wait_ge(off_mm, g - 1 + G + 1)
                        for t in range(NT):
                            act.activation(JUNK[:, t * 256:(t + 1) * 256], yn[:, t, :] if ssd else ps[:, A + t, 0:256],
                                           ACT.Square, accum_out=sm[:, 8 + t:9 + t]).then_inc(y_sq, 1)
                    if proj:
                        low_halves(SLOT_P3, g + n0[SLOT_P3], C, p3_lo)
                    if scan:
                        hi(SLOT_O, g - 1 + n0[SLOT_O])
                    if proj and ssd:
                        act.wait_ge(conv_done, 4 * g + 4)
                        if scan:
                            act.wait_ge(off_mm, g - 1 + G + 1)
                        for c in range(4):
                            tile = 2 * g + c if c < 2 else g + 8 * c
                            act.activation(fm[:, c, :], ca[:, c, :], ACT.Silu,
                                           bias=pcol[:, 1, bass.ds(tile, 1)]).then_inc(feat_done, 1)
                pipeline(act, n, body)

            act.wait_ge(cols_T, 1)
            act.activation(pcol[:, :, :].rearrange("p a n -> p (a n)"), ps[:, C, 0:256], ACT.Copy).then_inc(cols_done, 1)
            norm(0)
            hi(SLOT_GATE, 0)
            for ph, (kind, layer, which) in enumerate(PHASES):
                if kind == "ffn":
                    ffn(ph)
                elif kind == "gla":
                    gla_start()
                    mixer(ph, kind, GLA_H)
                else:
                    ssd_start()
                    mixer(ph, kind, SSD_G)
                norm(ph + 1)

        @block.vector
        def _(dve):
            step = Links(dve, dve_step)

            def lo(slot, count):
                dve.wait_ge(hi_done[slot], count + 1)
                dve.tensor_tensor(ws[:, slot, 1, :], raw[:, slot, :], ws[:, slot, 0, :].bitcast(F32),
                                  ALU.subtract).then_inc(lo_done[slot], 1)

            def sums(low, count, banks, outs, done):
                for c in range(2):
                    dve.wait_ge(low, count + c + 1)
                    dve.tensor_tensor(outs[c], ps[:, banks + c, 0:T], lo2[:, c, :], ALU.add).then_inc(done, 1)

            def rsqrt(ss, n, width):
                m, y, a, mh = (sm[:, o:o + n] for o in (16, 18, 20, 22))
                step(dve.tensor_scalar(m, ss, 1.0 / width, EPS, ALU.mult, ALU.add))
                step(dve.tensor_scalar(y.bitcast(I32), m.bitcast(I32), 1, None, ALU.logical_shift_right))
                dve.tensor_scalar(mh, m, -0.5, None, ALU.mult)
                step(dve.tensor_scalar(y.bitcast(I32), y.bitcast(I32), -1.0, MAGIC, ALU.mult, ALU.add))
                for _ in range(3):
                    if n == 1:
                        step(dve.scalar_tensor_tensor(out=a, in0=y, scalar=mh, in1=y, op0=ALU.mult, op1=ALU.mult))
                    else:
                        step(dve.tensor_tensor(a, y, y, ALU.mult))
                        step(dve.tensor_tensor(a, a, mh, ALU.mult))
                    step(dve.scalar_tensor_tensor(out=y, in0=a, scalar=1.5, in1=y, op0=ALU.add, op1=ALU.mult))
                return y

            def norm(b):
                if b > 0:
                    weight = 0.5 if PHASES[b - 1][0] == "ffn" else 1.0
                    dve.wait_ge(gpost_in, 16 * b)
                    for t in range(NT):
                        dve.wait_ge(sq_post, NT * (b - 1) + t + 1)
                        r = rsqrt(sm[:, t:t + 1], 1, D)
                        dve.scalar_tensor_tensor(out=T1, in0=ps[:, 2 * t:2 * t + 2, :].rearrange("p b n -> p (b n)"),
                                                 scalar=r, in1=gpost[:, :], op0=ALU.mult, op1=ALU.mult).then_inc(post_read, 1)
                        dve.wait_ge(post_read, NT * (b - 1) + t + 1)
                        dve.scalar_tensor_tensor(out=xres[:, t, :], in0=T1, scalar=weight, in1=xres[:, t, :],
                                                 op0=ALU.mult, op1=ALU.add).then_inc(x_ready, 1)
                if b == NPH:
                    return
                dve.wait_ge(gpre_in, 16 * (b + 1))
                for t in range(NT):
                    dve.wait_ge(sq_pre, NT * b + t + 1)
                    r = rsqrt(sm[:, 2 + t:3 + t], 1, D)
                    dve.scalar_tensor_tensor(out=NORMED[:, t, :], in0=xres[:, t, :], scalar=r, in1=gpre[:, :],
                                             op0=ALU.mult, op1=ALU.mult).then_inc(xn_ready, 1)
                for t in range(NT):
                    for q in range(2):
                        dve.wait_ge(xT_hi, 2 * NT * b + 2 * t + q + 1)
                        cols = (slice(None), slice(4 * q, 4 * q + 4))
                        dve.tensor_tensor(xT[:, 4 * q:4 * q + 4, 1, t * P:(t + 1) * P],
                                          ps[:, A + 2 * t + q, :].rearrange("p (k n) -> p k n", k=4),
                                          xT[:, 4 * q:4 * q + 4, 0, t * P:(t + 1) * P].bitcast(F32),
                                          ALU.subtract).then_inc(xT_lo, 1)

            def ffn(ph):
                f = ffns_before(ph) * NF * 2
                n0 = [used_before(ph, s) for s in range(4)]
                last = ph == NPH - 1

                def body(i, split_next):
                    lo(SLOT_UP, i + n0[SLOT_UP])
                    sums(gate_lo, i * 2 + f, A, [ca[:, c, :] for c in range(2)], gate_sum)
                    if split_next:
                        lo(SLOT_GATE, i + n0[SLOT_GATE] + 1)
                    lo(SLOT_DOWN, i + n0[SLOT_DOWN])
                    sums(up_lo, i * 2 + f, C, [ca[:, 2 + c, :] for c in range(2)], up_sum)
                    for c in range(2):
                        dve.wait_ge(up_sum, i * 2 + f + c + 1)
                        dve.wait_ge(silu_g, i * 2 + f + c + 1)
                        dve.tensor_tensor(fm[:, 2 + c, :], fm[:, c, :], ca[:, 2 + c, :], ALU.mult).then_inc(h_done, 1)
                    for c in range(2):
                        dve.wait_ge(h_hi, i * 2 + f + c + 1)
                        dve.tensor_tensor(hT[:, c, 1, :], fm[:, 2 + c, :], hT[:, c, 0, :].bitcast(F32),
                                          ALU.subtract).then_inc(hT_ready, 1)
                with dve.Fori(0, NF - 1 if last else NF) as i:
                    body(i, True)
                if last:
                    body(NF - 1, False)

            def gla_start():
                dve.wait_ge(small_hi, 1)
                dve.tensor_tensor(sw[:, :, 1, 0:GLA_RANK], lrw[:, :, :], sw[:, :, 0, 0:GLA_RANK].bitcast(F32),
                                  ALU.subtract).then_inc(small_lo, 1)
                reset = scr[:, 1, 1024:2048]
                dve.wait_ge(xT_lo, 8)
                step(dve.memset(reset, 1.0))
                dve.memset(reset.rearrange("p (n i) -> p n i", i=CH)[:, :, 0:1], 0.0)
                dve.wait_ge(small_lo_out, 1)
                dve.tensor_tensor(lrt[:, :, :], lrt[:, :, :], ps[:, C:E + 1, 0:GLA_RANK], ALU.add).then_inc(gla_dve, 1)
                dve.wait_ge(gla_mm, 1)
                dve.tensor_copy(lrT, ps[0:GLA_RANK, C, 0:T]).then_inc(gla_dve, 1)
                z, et, g16 = scr[:, 0, 0:1024], scr[:, 0, 1024:2048], scr[:, 1, 0:1024]
                dve.wait_ge(gla_mm, 2)
                dve.wait_ge(cols_done, 1)
                for h in range(GLA_H):
                    step(dve.tensor_scalar(z[:, h * T:(h + 1) * T], ps[:, C + h // 2, (h % 2) * T:(h % 2 + 1) * T],
                                           pcol[:, 1, GB0 + h:GB0 + h + 1], None, ALU.add))
                dve.scalar_tensor_tensor(out=et, in0=z, scalar=-1.0, in1=z, op0=ALU.mult, op1=ALU.max).then_inc(gla_dve, 1)
                dve.wait_ge(gla_act, 2)
                dve.scalar_tensor_tensor(out=g16, in0=z, scalar=0.0, in1=et, op0=ALU.min, op1=ALU.subtract).then_inc(gla_dve, 1)
                dve.wait_ge(gla_dve, 4)
                dve.tensor_tensor_scan(out=z, data0=reset, data1=g16, initial=0.0, op0=ALU.mult,
                                       op1=ALU.add).then_inc(gla_dve, 1)
                dve.wait_ge(gla_dve, 5)

                def chunks(ap):
                    return ap.rearrange("p (n i) -> p n i", i=CH)
                dve.tensor_tensor(chunks(et), chunks(z), chunks(z)[:, :, CH // 2:CH // 2 + 1].broadcast_to([P, 16, CH]),
                                  ALU.subtract).then_inc(gla_dve, 1)
                dve.tensor_tensor(chunks(g16), chunks(z)[:, :, CH - 1:CH].broadcast_to([P, 16, CH]), chunks(z),
                                  ALU.subtract).then_inc(gla_dve, 1)

            def ssd_start():
                dve.wait_ge(small_hi, 2)
                dve.tensor_tensor(sw[:, :, 1, :], dtw[:, :, :], sw[:, :, 0, :].bitcast(F32),
                                  ALU.subtract).then_inc(small_lo, 1)
                v = [dtv[:, r, :, :] for r in range(8)]

                def over_t(ap):
                    return ap.rearrange("p (t h) -> p t h", t=1).broadcast_to([P, NT, SSD_H])
                dve.wait_ge(small_lo_out, 2)
                step(dve.tensor_tensor(v[TA], v[TA], ps[:, C:E + 1, 0:SSD_H], ALU.add))
                step(dve.tensor_tensor(v[TA], v[TA], over_t(hb[:, 2, :]), ALU.add))
                dve.scalar_tensor_tensor(out=v[TB], in0=v[TA], scalar=-1.0, in1=v[TA], op0=ALU.mult, op1=ALU.max).then_inc(ssd_dve, 1)
                e, den, s, s2, q = v[TB], v[DT], v[CS], v[CSL], v[WST]
                dve.wait_ge(ssd_act, 2)
                step(dve.tensor_scalar(den, e, 2.0, None, ALU.add))
                step(dve.reciprocal(den, den))
                step(dve.tensor_tensor(s, e, den, ALU.mult))
                step(dve.tensor_tensor(s2, s, s, ALU.mult))
                step(dve.tensor_scalar(q, s2, 1.0 / 15, None, ALU.mult))
                for c in (13, 11, 9, 7, 5, 3):
                    step(dve.scalar_tensor_tensor(out=q, in0=q, scalar=1.0 / c, in1=s2, op0=ALU.add, op1=ALU.mult))
                step(dve.scalar_tensor_tensor(out=q, in0=q, scalar=1.0, in1=s, op0=ALU.add, op1=ALU.mult))
                step(dve.tensor_scalar(v[TA], v[TA], 0.0, None, ALU.max))
                step(dve.scalar_tensor_tensor(out=v[DT], in0=q, scalar=2.0, in1=v[TA], op0=ALU.mult, op1=ALU.add))
                dve.scalar_tensor_tensor(out=v[DA], in0=v[DT], scalar=-1.0, in1=over_t(hb[:, 0, :]), op0=ALU.mult,
                                         op1=ALU.mult).then_inc(ssd_dve, 1)
                dve.wait_ge(ssd_mm, 1)
                step(dve.tensor_copy(dtv[:, CS:CSL + 1, :, :].rearrange("p a t h -> p (a t h)"), ps[:, C, 0:128]))
                step(dve.tensor_copy(edl[:, :, :].rearrange("p c h -> p (c h)"), ps[:, C, 128:256]))
                dve.tensor_tensor(v[TA], v[CSL], v[CS], ALU.subtract).then_inc(ssd_dve, 1)
                dve.wait_ge(ssd_act, 5)
                dve.tensor_tensor(v[WST], v[TB], v[DT], ALU.mult).then_inc(ssd_dve, 1)
                r, seg = scr[:, 0, :], scr[:, 1, :]
                hi_ = "p (h i) -> p h i"

                def over_i(ap):
                    return ap.rearrange("p (h i) -> p h i", i=1).broadcast_to([P, SSD_H, CH])
                for t in range(NT):
                    if t:
                        dve.wait_ge(ssd_mm, 1 + t)
                        dve.wait_ge(ssd_act, 5 + t)
                    dve.tensor_tensor(r.rearrange(hi_, i=CH), over_i(dtv[:, DA, t, :]),
                                      mask[:, :].rearrange("p (h i) -> p h i", h=1).broadcast_to([P, SSD_H, CH]),
                                      ALU.mult).then_inc(ssd_dve, 1)
                    dve.wait_ge(ssd_mm, 2 + t)
                    step(dve.tensor_tensor(seg.rearrange(hi_, i=CH), ps[:, A:E + 1, :].rearrange("p b (h i) -> p (b h) i", i=CH),
                                           over_i(dtv[:, CS, t, :]), ALU.subtract))
                    dve.tensor_scalar(seg, seg, 0.0, None, ALU.min).then_inc(ssd_dve, 1)

            def mixer(ph, kind, n):
                G = groups_before(kind)
                n0 = [used_before(ph, s) for s in range(4)]
                ssd = kind == "ssd"
                gain0 = GS0 if ssd else GG0

                def by_head(ap):
                    return ap.rearrange("p (h d) -> p h d", h=HPG)

                def heads(ap, rows=P):
                    return ap.rearrange("p (h d) -> p h d", d=1).broadcast_to([rows, HPG, HD])

                def body(g, proj, scan, outp):
                    first = isinstance(g, int) and g == 1
                    c0 = g * 2 + 2 * G
                    if proj:
                        lo(SLOT_P2, g + n0[SLOT_P2])
                        if ssd:
                            sums(p1_lo, c0, A, [feat[:, c, CONV - 1:] for c in range(2)], p1_sum)
                        else:
                            sums(p1_lo, c0, A, [ca[:, c, :] for c in range(2)], p1_sum)
                    if outp:
                        for j in range(2):
                            dve.wait_ge(yT_hi, 2 * (g - 2 + G) + 2)
                            dve.scalar_tensor_tensor(out=hT[:, j, 1, :], in0=ps[:, C, j * T:(j + 1) * T],
                                                     scalar=pcol[:, 1, bass.ds(2 * g + (gain0 - 4 + j), 1)],
                                                     in1=hT[:, j, 0, :].bitcast(F32), op0=ALU.mult,
                                                     op1=ALU.subtract).then_inc(yT_lo, 1)
                    if proj:
                        lo(SLOT_P3, g + n0[SLOT_P3])
                        if ssd:
                            sums(p2_lo, c0, A, [feat[:, 2 + c, CONV - 1:] for c in range(2)], p2_sum)
                        else:
                            if scan:
                                dve.wait_ge(zs_done, g - 1 + G + 1)
                            sums(p2_lo, c0, A, [zf[:, t, :] for t in range(2)], p2_sum)
                    if scan:
                        mk = mask[:, :].rearrange("p (t i) -> p t i", t=1).broadcast_to([P, NT, CH])
                        if ssd:
                            dve.wait_ge(e_out, g)
                            cb = bcb[:, 256:384].rearrange("p (t i) -> p t i", t=2)
                            step(dve.tensor_tensor(cb, cb, mk, ALU.mult))
                            for t in range(NT):
                                dve.tensor_tensor(
                                    wm[:, t, :, :],
                                    exps[:, bass.ds(g * HPG * CH + (t * 2048 - HPG * CH), HPG * CH)].rearrange("p (h i) -> p h i", h=HPG),
                                    cb[:, t, :].rearrange("p (h i) -> p h i", h=1).broadcast_to([P, HPG, CH]),
                                    ALU.mult).then_inc(w_done, 1)
                        else:
                            dve.wait_ge(e_mm, g - 1 + G + 1)
                            dve.tensor_tensor(wm[:, :, 0, :], ps[:, C, 0:P].rearrange("p (t i) -> p t i", t=2), mk,
                                              ALU.mult).then_inc(w_done, 2)
                    if proj:
                        lo(SLOT_P1, g + n0[SLOT_P1] + 1)
                    if scan:
                        bank = [(E, 0), (C, 0), (E, 256)]
                        for c in range(3):
                            dve.wait_ge(upd_mm, 2 * (g - 1 + G) + (1 if c == 0 else 2))
                            new = ps[:, bank[c][0], bank[c][1]:bank[c][1] + 256]
                            if c == 0:
                                dve.tensor_copy(st[:, 0, :], new).then_inc(state_done, 1)
                                continue
                            dve.wait_ge(state_done, 3 * (g - 1 + G) + c)
                            if ssd:
                                step(dve.tensor_tensor(by_head(st[:, c, :]), by_head(st[:, c - 1, :]),
                                                       heads(edl[:, c, bass.ds((g - 1) * HPG, HPG)]), ALU.mult))
                                dve.tensor_tensor(st[:, c, :], st[:, c, :], new, ALU.add).then_inc(state_done, 1)
                            else:
                                dve.scalar_tensor_tensor(out=st[:, c, :], in0=st[:, c - 1, :],
                                                         scalar=edl[:, 0, bass.ds(4 * g + (c - 4), 1)], in1=new,
                                                         op0=ALU.mult, op1=ALU.add).then_inc(state_done, 1)
                    if proj and ssd:
                        for c in range(4):
                            dve.wait_ge(p1_sum if c < 2 else p2_sum, c0 + c % 2 + 1)
                            if c == 0 and scan:
                                dve.wait_ge(feat_done, 4 * (g + G))
                            tile = 2 * g + c if c < 2 else g + 8 * c
                            for k in range(CONV):
                                src, tap = feat[:, c, k:k + T], pcol[:, 0, bass.ds(tile + 32 * k, 1)]
                                if k == 0:
                                    step(dve.tensor_scalar(ca[:, c, :], src, tap, None, ALU.mult))
                                else:
                                    ins = dve.scalar_tensor_tensor(out=ca[:, c, :], in0=src, scalar=tap, in1=ca[:, c, :],
                                                                   op0=ALU.mult, op1=ALU.add)
                                    if k < CONV - 1:
                                        step(ins)
                                    else:
                                        ins.then_inc(conv_done, 1)
                    if scan and ssd:
                        dve.wait_ge(tok_mul, 4 * g)
                        dve.wait_ge(in_mm, g)
                        y_all = yn[:, :, :].rearrange("p t n -> p (t n)")
                        hs = bass.ds((g - 1) * HPG, HPG)
                        if not first:
                            dve.wait_ge(yT_mm, g - 1 + G)
                        step(dve.tensor_tensor(y_all, ps[:, A, :], dx[:, :, :].rearrange("p t n -> p (t n)"), ALU.add))
                        dve.wait_ge(off_mm, g - 1 + G + 1)
                        for t in range(NT):
                            r = slice(CH, P) if t == 0 else slice(0, P)
                            step(dve.tensor_tensor(by_head(vs[r, t, :]), by_head(ps[r, B, t * 256:(t + 1) * 256]),
                                                   heads(dtv[r, CDEC, t, hs], r.stop - r.start), ALU.mult))
                            step(dve.tensor_tensor(yn[r, t, :], yn[r, t, :], vs[r, t, :], ALU.add))
                        dve.wait_ge(zs_done, g - 1 + G + 1)
                        dve.tensor_tensor(y_all, y_all, zs[:, :, :].rearrange("p t n -> p (t n)"), ALU.mult).then_inc(y_done, 1)
                        dve.wait_ge(y_done, g)
                        dve.wait_ge(y_sq, 2 * (g - 1 + G) + 2)
                        y = rsqrt(sm[:, 8:10], 2, 256)
                        for t in range(NT):
                            dve.tensor_scalar(yn[:, t, :], yn[:, t, :], y[:, t:t + 1], None, ALU.mult).then_inc(yn_done, 1)
                    if scan and not ssd:
                        dve.wait_ge(y_sq, 2 * (g - 1 + G) + 2)
                        y = rsqrt(sm[:, 8:10], 2, 256)
                        dve.wait_ge(zs_done, g - 1 + G + 1)
                        if not first:
                            dve.wait_ge(yT_mm, g - 1 + G)
                        for t in range(NT):
                            ins = dve.scalar_tensor_tensor(out=yn[:, t, :], in0=ps[:, A + t, 0:256], scalar=y[:, t:t + 1],
                                                           in1=zs[:, t, :], op0=ALU.mult, op1=ALU.mult)
                            ins.then_inc(yn_done, 1)
                    if proj and not ssd:
                        dve.wait_ge(p1_sum, c0 + 2)
                        q, k = ca[:, 0, :], ca[:, 1, :]
                        for o, (src, scale, e) in enumerate(((q, P ** -0.5, 0), (k, 1.0, 1), (q, P ** -0.5, 2), (k, 1.0, 3))):
                            dve.scalar_tensor_tensor(out=fm[:, o, :], in0=src, scalar=scale,
                                                     in1=exps[:, bass.ds(g * T + e * 1024, T)],
                                                     op0=ALU.mult, op1=ALU.mult).then_inc(feat_done, 1)
                    if proj:
                        if ssd:
                            if scan:
                                dve.wait_ge(zs_done, g - 1 + G + 1)
                            sums(p3_lo, c0, C, [zf[:, t, :] for t in range(2)], p3_sum)
                        else:
                            if scan:
                                dve.wait_ge(off_mm, g - 1 + G + 1)
                            sums(p3_lo, c0, C, [vs[:, t, :] for t in range(2)], p3_sum)
                    if scan:
                        lo(SLOT_O, g - 1 + n0[SLOT_O])

                body(0, True, False, False)
                body(1, True, True, False)
                per = SSD_STEPS if ssd else GLA_STEPS
                with dve.Fori(2, n) as g:
                    step.body(g, 2, per)
                    body(g, True, True, True)
                step.after(n - 2, per)
                body(n, False, True, True)
                body(n + 1, False, False, True)

            norm(0)
            lo(SLOT_GATE, 0)
            dve.wait_ge(consts, CONST_ALL)
            for ph, (kind, layer, which) in enumerate(PHASES):
                if kind == "ffn":
                    ffn(ph)
                elif kind == "gla":
                    gla_start()
                    dve.wait_ge(gla_act, 7)
                    mixer(ph, kind, GLA_H)
                else:
                    ssd_start()
                    dve.wait_ge(ssd_act, 7)
                    mixer(ph, kind, SSD_G)
                norm(ph + 1)

        @block.tensor
        def _(pe):
            def features(slot, banks):
                for c in range(2):
                    bank = ps[:, banks + c, :]
                    for k in range(KD):
                        off = k * UW + c * P
                        pe.matmul(bank, ws[:, slot, 0, off:off + P], xT[:, k, :, :].rearrange("p a t -> p (a t)"),
                                  start=(k == 0), stop=False, skip_group_check=True)
                        mm = pe.matmul(bank[:, 0:T], ws[:, slot, 1, off:off + P], xT[:, k, 0, :],
                                       start=False, stop=(k == KD - 1), skip_group_check=True)
                    mm.then_inc(tile_mm[slot], 1)

            def tokens(slot, banks):
                for t in range(NT):
                    bank = ps[:, banks + t, :]
                    for k in range(KD):
                        rhs = ws[:, slot, :, k * UW:(k + 1) * UW]
                        pe.matmul(bank.rearrange("p (a n) -> p a n", a=2), xT[:, k, 0, t * P:(t + 1) * P], rhs,
                                  start=(k == 0), stop=False, skip_group_check=True)
                        mm = pe.matmul(bank[:, 0:UW], xT[:, k, 1, t * P:(t + 1) * P], rhs[:, 0, :],
                                       start=False, stop=(k == KD - 1), skip_group_check=True)
                    mm.then_inc(tile_mm[slot], 1)

            def open_banks(ph):
                if ph == 0:
                    pe.wait_ge(consts, CONST_IDENT + 1)
                else:
                    pe.wait_ge(post_read, NT * ph)
                for b in range(4):
                    for q in range(4):
                        pe.matmul(ps[:, b, q * P:(q + 1) * P], zr[:, :], zr[:, :], start=(q == 0), stop=False,
                                  skip_group_check=True)

            def output(slot, last):
                for t in range(NT):
                    for n in range(2):
                        for j in range(2):
                            for a, b in ((0, 0), (0, 1), (1, 0)):
                                off = j * D + n * 512
                                mm = pe.matmul(ps[:, 2 * t + n, :], hT[:, j, a, t * P:(t + 1) * P],
                                               ws[:, slot, b, off:off + 512], start=False,
                                               stop=(last and j == 1 and a == 1), skip_group_check=True)
                    mm.then_inc(tile_mm[slot], 1)

            def split(slot, count):
                pe.wait_ge(lo_done[slot], count + 1)

            def norm(b):
                for t in range(NT):
                    pe.wait_ge(xn_ready, NT * b + t + 1)
                    for q in range(2):
                        for k in range(4):
                            col = (4 * q + k) * P
                            mm = pe.transpose(ps[:, A + 2 * t + q, k * P:(k + 1) * P], NORMED[:, t, col:col + P], ident[:, :])
                        mm.then_inc(xnT, 1)

            def ffn(ph):
                f = ffns_before(ph) * NF * 2
                n0 = [used_before(ph, s) for s in range(4)]
                open_banks(ph)
                pe.wait_ge(xT_lo, 2 * NT * (ph + 1))

                def body(i, first):
                    split(SLOT_GATE, i + n0[SLOT_GATE])
                    if not first:
                        pe.wait_ge(gate_sum, i * 2 + f)
                    features(SLOT_GATE, A)
                    if not first:
                        split(SLOT_DOWN, i + n0[SLOT_DOWN] - 1)
                        pe.wait_ge(hT_ready, i * 2 + f)
                        output(SLOT_DOWN, False)
                    split(SLOT_UP, i + n0[SLOT_UP])
                    if not first:
                        pe.wait_ge(up_sum, i * 2 + f)
                    features(SLOT_UP, C)
                body(0, True)
                with pe.Fori(1, NF) as i:
                    body(i, False)
                split(SLOT_DOWN, NF - 1 + n0[SLOT_DOWN])
                pe.wait_ge(hT_ready, NF * 2 + f)
                output(SLOT_DOWN, True)

            def small(width):
                for t in range(NT):
                    bank = ps[:, C + t, 0:2 * width]
                    for k in range(KD):
                        pe.matmul(bank.rearrange("p (a n) -> p a n", a=2), xT[:, k, 0, t * P:(t + 1) * P],
                                  sw[:, k, :, 0:width], start=(k == 0), stop=False, skip_group_check=True)
                        mm = pe.matmul(bank[:, 0:width], xT[:, k, 1, t * P:(t + 1) * P], sw[:, k, 0, 0:width],
                                       start=False, stop=(k == KD - 1), skip_group_check=True)
                    mm.then_inc(small_mm, 1)

            def gla_start():
                pe.wait_ge(small_lo, 1)
                small(GLA_RANK)
                pe.wait_ge(gla_dve, 1)
                for t in range(NT):
                    mm = pe.transpose(ps[0:GLA_RANK, C, t * P:(t + 1) * P], lrt[:, t, :], ident[:, :])
                mm.then_inc(gla_mm, 1)
                pe.wait_ge(gla_dve, 2)
                for h in range(GLA_H):
                    mm = pe.matmul(ps[:, C + h // 2, (h % 2) * T:(h % 2 + 1) * T], wgk[:, h * P:(h + 1) * P], lrT,
                                   start=True, stop=True, skip_group_check=True)
                mm.then_inc(gla_mm, 1)

            def ssd_start():
                pe.wait_ge(small_lo, 2)
                small(SSD_H)
                pe.wait_ge(consts, CONST_ALL)
                pe.wait_ge(ssd_dve, 2)
                for t in range(NT):
                    rhs = dtv[:, DA, t, :]
                    for o, lhs in ((0, tri[:, :]), (64, blk[:, :])):
                        pe.matmul(ps[:, C, o + t * 32:o + (t + 1) * 32], lhs, rhs, start=True, stop=True, skip_group_check=True)
                    for c in range(2):
                        o = 128 + (2 * t + c) * 32
                        mm = pe.matmul(ps[:, C, o:o + 32], half[:, c, :], rhs, start=True, stop=True, skip_group_check=True)
                mm.then_inc(ssd_mm, 1)
                pe.wait_ge(ssd_dve, 3)
                for t in range(NT):
                    pe.wait_ge(ssd_dve, SSD_WEIGHTS + 2 * t + 1)
                    for b in range(4):
                        mm = pe.matmul(ps[:, A + b, :], blk[:, :], scr[:, 0, b * 512:(b + 1) * 512], start=True, stop=True,
                                       skip_group_check=True)
                    mm.then_inc(ssd_mm, 1)
                pe.wait_ge(ssd_dve, SSD_WEIGHTS + 4)

            def mixer(ph, kind, n):
                G = groups_before(kind)
                n0 = [used_before(ph, s) for s in range(4)]
                ssd = kind == "ssd"

                def body(g, proj, scan, outp):
                    first = isinstance(g, int) and g == 1
                    last = not proj and not scan
                    c0 = g * 2 + 2 * G
                    if proj:
                        split(SLOT_P1, g + n0[SLOT_P1])
                        if scan and not first:
                            pe.wait_ge(yn_done, c0 - 2)
                        if scan:
                            pe.wait_ge(p2_sum, c0)
                        features(SLOT_P1, A)
                    if outp:
                        pe.wait_ge(yn_done, 2 * (g - 2 + G) + 2)
                        if scan:
                            pe.wait_ge(p3_sum, c0)
                        for j in range(2):
                            for t in range(NT):
                                mm = pe.transpose(ps[:, C, j * T + t * P:j * T + (t + 1) * P],
                                                  yn[:, t, j * P:(j + 1) * P], ident[:, :])
                        mm.then_inc(yT_mm, 1)
                    if scan:
                        pe.wait_ge(feat_done, 4 * (g - 1 + G) + 4)
                        pe.wait_ge(p3_sum, 2 * (g - 1 + G) + 2)
                        for t in range(NT):
                            if ssd:
                                for j in range(2):
                                    o = (2 * t + j) * P
                                    mm = pe.transpose(ps[:, E, o:o + P], fm[:, j, t * P:(t + 1) * P], ident[:, :])
                            else:
                                mm = pe.transpose(ps[:, E, t * P:(t + 1) * P], fm[:, 3, t * P:(t + 1) * P], ident[:, :])
                        mm.then_inc(tok_T, 1)
                    if proj:
                        split(SLOT_P2, g + n0[SLOT_P2])
                        pe.wait_ge(p1_sum, c0 + 2)
                        if ssd:
                            features(SLOT_P2, A)
                        else:
                            tokens(SLOT_P2, A)
                    if scan:
                        if outp:
                            pe.wait_ge(yT_lo, 2 * (g - 2 + G) + 2)
                        if ssd:
                            for t in range(NT):
                                pe.transpose(ps[:, C, t * P:(t + 1) * P], fm[:, 2, t * P:(t + 1) * P], ident[:, :])
                        for c in range(4):
                            i, o = slice(c * CH, (c + 1) * CH), (256 if ssd else 0) + (c // 2) * CH
                            kv, q = (2, 3) if ssd else (1, 0)
                            r = slice((c % 2) * CH, (c % 2 + 1) * CH)
                            mm = pe.matmul(ps[r, C, o:o + CH], fm[:, kv, i], fm[:, q, i], start=True, stop=True,
                                           skip_group_check=True)
                        mm.then_inc(e_mm, 1)
                    if outp:
                        split(SLOT_O, g - 2 + n0[SLOT_O])
                        pe.wait_ge(yT_lo, 2 * (g - 2 + G) + 2)
                        output(SLOT_O, last)
                    if scan:
                        pe.wait_ge(tok_out, g - 1 + G + 1)
                        if ssd:
                            pe.wait_ge(e_out, g)
                        pe.wait_ge(w_done, 2 * (g - 1 + G) + 2)
                        if ssd:
                            pe.wait_ge(tok_mul, 4 * (g - 1) + 2)
                        if proj:
                            pe.wait_ge(p2_sum, c0 + 2)
                        for c, (bank, o) in ((0, (E, 0)), (2, (E, 256)), (1, (C, 0))):
                            r, t = slice((c % 2) * CH, (c % 2 + 1) * CH), c // 2
                            keys = bcb[r, t * P:(t + 1) * P] if ssd else xw[r, t, 0:P]
                            vals = xw[r, t, :] if ssd else vs[r, t, :]
                            mm = pe.matmul(ps[:, bank, o:o + 256], keys, vals, start=True, stop=True, skip_group_check=True)
                            if c:
                                mm.then_inc(upd_mm, 1)
                        if ssd:
                            for t in range(NT):
                                for h in range(HPG):
                                    for c in range(2):
                                        r, o = slice(c * CH, (c + 1) * CH), t * 256 + h * HD
                                        mm = pe.matmul(ps[r, A, o:o + HD], wm[r, t, h, :], xdt[r, t, h * HD:(h + 1) * HD],
                                                       start=True, stop=True, skip_group_check=True)
                            mm.then_inc(in_mm, 1)
                        else:
                            for c in range(4):
                                r, t = slice((c % 2) * CH, (c % 2 + 1) * CH), c // 2
                                pe.matmul(ps[r, A + t, 0:256], wm[r, t, 0, :], vs[r, t, :], start=True, stop=(c == 0),
                                          skip_group_check=True)
                        for c in range(1, 4):
                            pe.wait_ge(state_done, 3 * (g - 1 + G) + c)
                            r, t = slice((c % 2) * CH, (c % 2 + 1) * CH), c // 2
                            dst = ps[r, B, t * 256:(t + 1) * 256] if ssd else ps[r, A + t, 0:256]
                            mm = pe.matmul(dst, fm[:, 3 if ssd else 2, c * CH:(c + 1) * CH], st[:, c - 1, :], start=ssd,
                                           stop=True, skip_group_check=True)
                        mm.then_inc(off_mm, 1)
                    if proj:
                        split(SLOT_P3, g + n0[SLOT_P3])
                        if not scan:
                            pe.wait_ge(p2_sum, c0 + 2)
                        if scan:
                            pe.wait_ge(state_done, 3 * (g - 1 + G) + 3)
                        tokens(SLOT_P3, C)
                open_banks(ph)
                pipeline(pe, n, body)

            pe.wait_ge(consts, CONST_IDENT)
            pe.wait_ge(params_in, 16 * 11)
            for a in range(2):
                mm = pe.transpose(ps[:, C, a * P:(a + 1) * P], prow[:, a, :], ident[:, :])
            mm.then_inc(cols_T, 1)
            pe.wait_ge(cols_done, 1)
            norm(0)
            for ph, (kind, layer, which) in enumerate(PHASES):
                if kind == "ffn":
                    ffn(ph)
                else:
                    pe.wait_ge(xT_lo, 2 * NT * (ph + 1))
                    if kind == "gla":
                        gla_start()
                        mixer(ph, kind, GLA_H)
                    else:
                        ssd_start()
                        mixer(ph, kind, SSD_G)
                if ph + 1 < NPH:
                    norm(ph + 1)


_INS = ["x", "ffn_w_gate", "ffn_w_up", "ffn_w_down", "norm_gain", "gla_w_in", "gla_w_gk2", "gla_b_gk", "gla_norm",
        "gla_w_out", "ssd_w_in", "ssd_conv_w", "ssd_conv_b", "ssd_dt_bias", "ssd_A_log", "ssd_D", "ssd_norm",
        "ssd_w_out"]


def kernel(**inputs):
    import numpy as np
    import concourse.bacc as bacc
    from concourse.bass_utils import run_bass_kernel_spmd

    nc = bacc.Bacc("TRN2", target_bir_lowering=False, num_devices=1)
    arrays, args = {}, []
    for name in _INS:
        a = np.ascontiguousarray(inputs[name])
        arrays[f"in_{name}"] = a
        args.append(nc.dram_tensor(f"in_{name}", a.shape, mybir.dt.from_np(a.dtype), kind="ExternalInput").ap())
    args.append(nc.dram_tensor("out_y", (1, T, D), F32, kind="ExternalOutput").ap())
    trunk(nc, *args)
    r = run_bass_kernel_spmd(nc, [arrays], core_ids=[0])
    return r.results[0]["out_y"]
```

```python
from contextlib import ExitStack

import concourse.bass as bass
from concourse import mybir

ALU = mybir.AluOpType
ACT = mybir.ActivationFunctionType
F32 = mybir.dt.float32
F32R = mybir.dt.float32r
I32 = mybir.dt.int32

P = 128
T = 256
NT = T // P
D = 1024
KD = D // P
D_FF = 2816
UW = 256
UNIT = KD * UW
NF = D_FF // UW
EPS = 1e-6
CH = 64
HPG = 4
HD = 64
GLA_H = 4
GLA_RANK = 16
SSD_G = 8
SSD_H = 32
DI = 2048
CONV = 4
MAGIC = float(0x5F3759DF)
SLOT_P1, SLOT_P2, SLOT_P3, SLOT_O = 0, 1, 2, 3
SLOT_GATE, SLOT_UP, SLOT_DOWN = 0, 1, 2
CONST_IDENT, CONST_EPS, CONST_ALL = 2, 4, 17
SSD_WEIGHTS = 4
SSD_STEPS, GLA_STEPS = 19, 13

PHASES = [("ffn", 0, 0), ("gla", 0, 0), ("ffn", 0, 1), ("ffn", 1, 0), ("ssd", 0, 0), ("ffn", 1, 1)]
NPH = len(PHASES)


def uses_in(kind, slot):
    if kind == "ffn":
        return NF if slot < 3 else 0
    return GLA_H if kind == "gla" else SSD_G


def used_before(phase, slot):
    return sum(uses_in(PHASES[q][0], slot) for q in range(phase))


def groups_before(kind):
    return 0 if kind == "gla" else GLA_H


def ffns_before(phase):
    return sum(PHASES[q][0] == "ffn" for q in range(phase))


def pipeline(eng, n, body):
    body(0, True, False, False)
    body(1, True, True, False)
    with eng.Fori(2, n) as g:
        body(g, True, True, True)
    body(n, False, True, True)
    body(n + 1, False, False, True)


class Links:

    def __init__(self, eng, sem):
        self.eng, self.sem, self.base, self.k = eng, sem, 0, 0

    def __call__(self, ins):
        self.start(ins)
        self.wait()

    def start(self, ins):
        self.k += 1
        ins.then_inc(self.sem, 1)

    def wait(self):
        self.eng.wait_ge(self.sem, self.base + self.k)

    def body(self, i, start, per):
        self.before = self.base + self.k
        self.base, self.k = i * per + (self.before - start * per), 0

    def after(self, n, per):
        assert self.k == per, (self.k, per)
        self.base, self.k = self.before + n * per, 0


def trunk(nc, x, ffn_w_gate, ffn_w_up, ffn_w_down, norm_gain, gla_w_in, gla_w_gk2, gla_b_gk,
          gla_norm, gla_w_out, ssd_w_in, ssd_conv_w, ssd_conv_b, ssd_dt_bias, ssd_A_log, ssd_D,
          ssd_norm, ssd_w_out, out):
    with ExitStack() as ctx:
        def sb(name, shape, dt=F32):
            return ctx.enter_context(nc.sbuf_tensor(name, shape, dt))

        def sem(name):
            return ctx.enter_context(nc.semaphore(name))

        raw = sb("raw", [P, 4, UNIT])
        ws = sb("ws", [P, 4, 2, UNIT], F32R)
        xres = sb("xres", [P, NT, D])
        xT = sb("xT", [P, KD, 2, T], F32R)
        hT = sb("hT", [P, 2, 2, T], F32R)
        exps = sb("exps", [P, 4096])
        scr = sb("scr", [P, 2, 2048])
        gpost = sb("gpost", [P, D])
        gpre = sb("gpre", [P, D])
        lo2 = sb("lo2", [P, 2, T])
        feat = sb("feat", [P, 4, CONV - 1 + T])
        ca = sb("ca", [P, 4, T])
        fm = sb("fm", [P, 4, T])
        xdt = sb("xdt", [P, NT, 256])
        xw = sb("xw", [P, NT, 256])
        dx = sb("dx", [P, NT, 256])
        wm = sb("wm", [P, NT, HPG, CH])
        zf = sb("zf", [P, NT, 256])
        zs = sb("zs", [P, NT, 256])
        vs = sb("vs", [P, NT, 256])
        yn = sb("yn", [P, NT, 256])
        dtw = sb("dtw", [P, KD, SSD_H])
        sw = sb("sw", [P, KD, 2, SSD_H], F32R)
        ident = sb("ident", [P, P])
        tri = sb("tri", [P, P])
        blk = sb("blk", [P, P])
        half = sb("half", [P, 2, P])
        mask = sb("mask", [P, CH])
        zr = sb("zr", [P, P], F32R)
        pcol = sb("pcol", [P, 2, P])
        xtok = scr[:, 0, 0:512].rearrange("p (t n) -> p t n", t=NT)
        st = scr[:, 0, 512:1280].rearrange("p (c n) -> p c n", c=3)
        bcb = scr[:, 0, 1280:1664]
        prow = zs[:, 0, 0:2 * P].rearrange("p (a n) -> p a n", a=2)
        lrw = exps[:, 0:KD * GLA_RANK].rearrange("p (k n) -> p k n", k=KD)
        wgk = xdt[0:GLA_RANK, :, :].rearrange("p t n -> p (t n)")
        lrT = dx[0:GLA_RANK, 0, :]
        lrt = sb("lrt", [P, NT, GLA_RANK])
        hb = sb("hb", [P, 3, SSD_H])
        dtv = sb("dtv", [P, 8, NT, SSD_H])
        edl = sb("edl", [P, 4, SSD_H])
        sm = sb("sm", [P, 32])
        ps = ctx.enter_context(nc.psum_tensor("ps", [P, 8, 512], F32))

        JUNK = scr[:, 1, 0:D]
        NORMED = scr[:, 0, :].rearrange("p (t d) -> p t d", t=NT)
        EPS_COL, DUMMY = sm[:, 30:31], sm[:, 29:30]
        T1 = scr[:, 1, D:2 * D]
        DT, DA, CS, CSL, WST, CDEC, TA, TB = range(8)
        A, B, C, E = 4, 5, 6, 7
        CW0, CB0 = 0, 0
        GG0, GS0, GB0 = 32, 40, 56

        loaded = [sem(f"loaded{s}") for s in range(4)]
        hi_done = [sem(f"hi_done{s}") for s in range(4)]
        lo_done = [sem(f"lo_done{s}") for s in range(4)]
        tile_mm = [sem(f"tile_mm{s}") for s in range(4)]
        params_in, x_in = sem("params_in"), sem("x_in")
        gpre_in, gpost_in = sem("gpre_in"), sem("gpost_in")
        stored = sem("stored")
        consts = sem("consts")
        cols_T, cols_done = sem("cols_T"), sem("cols_done")
        dve_step = sem("dve_step")
        sq_post, sq_pre = sem("sq_post"), sem("sq_pre")
        root_post, root_pre = sem("root_post"), sem("root_pre")
        sqrt_ready = sem("sqrt_ready")
        xg_done = sem("xg_done")
        post_read = sem("post_read")
        x_ready, xn_ready = sem("x_ready"), sem("xn_ready")
        xnT = sem("xnT")
        xT_hi, xT_lo = sem("xT_hi"), sem("xT_lo")
        gate_lo, up_lo = sem("gate_lo"), sem("up_lo")
        gate_sum, silu_g, h_done, h_hi, hT_ready = (sem(n) for n in (
            "gate_sum", "silu_g", "h_done", "h_hi", "hT_ready"))
        up_sum = sem("up_sum")
        small_hi, small_lo, small_mm, small_lo_out = (sem(n) for n in (
            "small_hi", "small_lo", "small_mm", "small_lo_out"))
        gla_mm, gla_dve, gla_act = sem("gla_mm"), sem("gla_dve"), sem("gla_act")
        ssd_mm, ssd_dve, ssd_act, ssd_r = sem("ssd_mm"), sem("ssd_dve"), sem("ssd_act"), sem("ssd_r")
        p1_out, p2_out, p3_out = sem("p1_out"), sem("p2_out"), sem("p3_out")
        conv_step, feat_done = sem("conv_step"), sem("feat_done")
        tok_T, tok_out, tok_mul = sem("tok_T"), sem("tok_out"), sem("tok_mul")
        e_mm, e_out, w_done = sem("e_mm"), sem("e_out"), sem("w_done")
        upd_mm, state_done = sem("upd_mm"), sem("state_done")
        in_mm, off_mm = sem("in_mm"), sem("off_mm")
        y_done, y_sq, y_out, yn_done = sem("y_done"), sem("y_sq"), sem("y_out"), sem("yn_done")
        zs_done = sem("zs_done")
        yT_mm, yT_hi, yT_lo = sem("yT_mm"), sem("yT_hi"), sem("yT_lo")

        def gain_row(j):
            return norm_gain.rearrange("l n d -> (l n) d")[j:j + 1, :].broadcast_to([P, D])

        block = ctx.enter_context(nc.Block())

        @block.sync
        def _(sp):
            def at(value):
                return value if isinstance(value, int) else sp.snap(value)

            def cols(w, col, n=UW):
                return w.rearrange("(k p) n -> p k n", p=P)[:, :, bass.ds(col, n)]

            def load_cols(slot, w, col, count):
                dst = raw[:, slot, :].rearrange("p (k n) -> p k n", k=KD)
                src = cols(w, at(col))
                if count is not None:
                    sp.wait_ge(lo_done[slot], count)
                for h in (1, 0):
                    ks = slice(h * KD // 2, (h + 1) * KD // 2)
                    sp.dma_start(dst[:, ks, :], src[:, ks, :]).then_inc(loaded[slot], 16)

            def load_two(slot, w, col0, col1, count):
                dst = raw[:, slot, :].rearrange("p (k c n) -> p k c n", k=KD, c=2)
                starts = at(col0), at(col1)
                sp.wait_ge(lo_done[slot], count)
                for c, col in enumerate(starts):
                    sp.dma_start(dst[:, :, c, :], cols(w, col, P)).then_inc(loaded[slot], 16)

            def load_rows(slot, w, row, count):
                dst = raw[:, slot, :].rearrange("p (j n) -> p j n", j=2)
                starts = at(row), at(row + P)
                if count is not None:
                    sp.wait_ge(lo_done[slot], count)
                for j in (1, 0):
                    sp.dma_start(dst[:, j, :], w[bass.ds(starts[j], P), :]).then_inc(loaded[slot], 16)

            for t in range(NT):
                sp.dma_start(xres[:, t, :], x[0, t * P:(t + 1) * P, :]).then_inc(x_in, 16)

            def load_first(ph):
                if ph == NPH:
                    return
                kind, layer, which = PHASES[ph]
                n0, n1 = (used_before(ph, s) for s in (0, 1)) if ph else (None, None)
                if kind == "ffn":
                    load_cols(SLOT_GATE, ffn_w_gate[layer, which], 0, n0)
                    load_cols(SLOT_UP, ffn_w_up[layer, which], 0, n1)
                elif kind == "gla":
                    load_two(SLOT_P1, gla_w_in[0], 0, 512, n0)
                    load_cols(SLOT_P2, gla_w_in[0], 2048, n1)
                else:
                    load_cols(SLOT_P1, ssd_w_in[0], DI, n0)
                    load_two(SLOT_P2, ssd_w_in[0], 2 * DI, 2 * DI + 1024, n1)

            load_first(0)
            for ph, (kind, layer, which) in enumerate(PHASES):
                n0 = [used_before(ph, s) for s in range(4)]
                if kind == "ffn":
                    wg, wu, wd = (w[layer, which] for w in (ffn_w_gate, ffn_w_up, ffn_w_down))

                    def load_ffn(i, fresh=False):
                        load_cols(SLOT_GATE, wg, i * UW + UW, i + n0[SLOT_GATE] + 1)
                        load_rows(SLOT_DOWN, wd, i * UW, None if fresh else i + n0[SLOT_DOWN])
                        load_cols(SLOT_UP, wu, i * UW + UW, i + n0[SLOT_UP] + 1)
                    if ph == 0:
                        load_ffn(0, True)
                    with sp.Fori(1 if ph == 0 else 0, NF - 1) as i:
                        load_ffn(i)
                    load_rows(SLOT_DOWN, wd, (NF - 1) * UW, NF - 1 + n0[SLOT_DOWN])
                    load_first(ph + 1)
                else:
                    ssd = kind == "ssd"
                    n = SSD_G if ssd else GLA_H
                    w, wo = (ssd_w_in[0], ssd_w_out[0]) if ssd else (gla_w_in[0], gla_w_out[0])

                    def load_p3(g):
                        load_cols(SLOT_P3, w, g * UW if ssd else g * UW + 1024, g + n0[SLOT_P3])

                    def load_p12(g):
                        if ssd:
                            load_cols(SLOT_P1, w, g * UW + DI, g + n0[SLOT_P1])
                            load_two(SLOT_P2, w, g * P + 2 * DI, g * P + 2 * DI + 1024, g + n0[SLOT_P2])
                        else:
                            load_two(SLOT_P1, w, g * P, g * P + 512, g + n0[SLOT_P1])
                            load_cols(SLOT_P2, w, g * UW + 2048, g + n0[SLOT_P2])

                    def load_out(g):
                        fresh = isinstance(g, int) and g + n0[SLOT_O] == 0
                        load_rows(SLOT_O, wo, g * UW, None if fresh else g + n0[SLOT_O])
                    load_p3(0)
                    load_p12(1)
                    load_p3(1)
                    load_p12(2)
                    load_out(0)
                    with sp.Fori(2, n - 1) as g:
                        load_p3(g)
                        load_p12(g + 1)
                        load_out(g - 1)
                    load_p3(n - 1)
                    load_first(ph + 1)
                    load_out(n - 2)
                    load_out(n - 1)
            for t in range(NT):
                sp.wait_ge(x_ready, NPH * NT - NT + t + 1)
                sp.dma_start(out[0, t * P:(t + 1) * P, :], xres[:, t, :]).then_inc(stored, 16)
            sp.wait_ge(stored, 16 * NT)

        @block.gpsimd
        def _(pool):
            step = Links(pool, consts)

            def norm_gain_product(b):
                if b == 0:
                    pool.wait_ge(x_in, 16 * NT)
                else:
                    pool.wait_ge(x_ready, NT * (b - 1) + 1)
                pool.wait_ge(gpre_in, 16 * (b + 1))
                pool.tensor_tensor(out=NORMED[:, 0, :], in0=xres[:, 0, :], in1=gpre[:, :], op=ALU.mult).then_inc(xg_done, 1)

            pool.dma_start(gpre[:, :], gain_row(0)).then_inc(gpre_in, 16)
            step(pool.memset(ident[:, :], 0.0))
            step(pool.affine_select(out=ident[:, :], in_=ident[:, :], compare_op=ALU.not_equal, fill=1.0, base=0,
                                    pattern=[[-1, P]], channel_multiplier=1))
            assert step.k == CONST_IDENT
            step(pool.memset(zr[:, :].bitcast(F32), 0.0))
            step(pool.memset(EPS_COL, EPS))
            assert step.k == CONST_EPS
            norm_gain_product(0)
            pool.dma_start(gpost[:, :], gain_row(1)).then_inc(gpost_in, 16)
            step(pool.memset(prow[:, 1, :], 0.0))
            rows = "(t c) -> t c"
            for dst, src in (
                    (prow[:, 0, :], ssd_conv_w[0].rearrange("k (t c) -> (k t) c", c=P)),
                    (prow[0:32, 1, :], ssd_conv_b[0].rearrange(rows, c=P)),
                    (prow[GG0:GG0 + 8, 1, :], gla_norm[0].rearrange(rows, c=P)),
                    (prow[GS0:GS0 + 16, 1, :], ssd_norm[0].rearrange(rows, c=P)),
                    (prow[GB0:GB0 + 4, 1, :], gla_b_gk[0].rearrange(rows, c=P)),
                    (hb[:, 0, :], ssd_A_log.broadcast_to([P, SSD_H])),
                    (hb[:, 1, :], ssd_D.broadcast_to([P, SSD_H])),
                    (hb[:, 2, :], ssd_dt_bias.broadcast_to([P, SSD_H])),
                    (wgk, gla_w_gk2[0]),
                    (lrw[:, :, :], gla_w_in[0].rearrange("(k p) n -> p k n", p=P)[:, :, 3072:3072 + GLA_RANK]),
                    (dtw[:, :, :], ssd_w_in[0].rearrange("(k p) n -> p k n", p=P)[:, :, 6144:6144 + SSD_H])):
                pool.dma_start(dst, src).then_inc(params_in, 16)
            step(pool.memset(tri[:, :], 1.0))
            step(pool.affine_select(out=tri[:, :], in_=tri[:, :], compare_op=ALU.is_ge, fill=0.0, base=0,
                                    pattern=[[1, P]], channel_multiplier=-1))
            step(pool.memset(tri[0:CH, CH:P], 0.0))
            step(pool.memset(blk[:, :], 0.0))
            step(pool.memset(half[:, :, :], 0.0))
            for c in range(2):
                r = slice(c * CH, (c + 1) * CH)
                step(pool.tensor_copy(mask[r, :], tri[r, r]))
                step(pool.memset(blk[r, r], 1.0))
                step(pool.memset(half[r, c, :], 1.0))
            step(pool.memset(feat[:, :, 0:CONV - 1], 0.0))
            assert step.k == CONST_ALL

            def side_products(g, proj, scan, outp):
                if not scan:
                    return
                G = groups_before("ssd")
                hs = bass.ds((g - 1) * HPG, HPG)

                def heads(ap, n):
                    return ap.rearrange("p t (h o) -> p t h o", o=1).broadcast_to([P, n, HPG, HD])

                def by_head(buf):
                    return buf[:, :, :].rearrange("p t (h d) -> p t h d", h=HPG)
                pool.wait_ge(tok_out, g - 1 + G + 1)
                pool.tensor_tensor(out=by_head(xw), in0=by_head(xtok), in1=heads(dtv[:, WST, :, hs], NT),
                                   op=ALU.mult).then_inc(tok_mul, 1)
                pool.tensor_tensor(out=by_head(xdt), in0=by_head(xtok), in1=heads(dtv[:, DT, :, hs], NT),
                                   op=ALU.mult).then_inc(tok_mul, 1)
                if not (isinstance(g, int) and g == 1):
                    pool.wait_ge(y_out, 2 * (g - 1 + G))
                for t in range(NT):
                    pool.tensor_tensor(out=by_head(dx)[:, t], in0=by_head(xtok)[:, t],
                                       in1=hb[:, 1, hs].rearrange("p (h o) -> p h o", o=1).broadcast_to([P, HPG, HD]),
                                       op=ALU.mult).then_inc(tok_mul, 1)

            for b in range(NPH):
                if b > 0:
                    norm_gain_product(b)
                pool.wait_ge(xn_ready, NT * (b + 1))
                if b > 0:
                    pool.dma_start(gpost[:, :], gain_row(2 * b + 1)).then_inc(gpost_in, 16)
                if b + 1 < NPH:
                    pool.dma_start(gpre[:, :], gain_row(2 * b + 2)).then_inc(gpre_in, 16)
                if PHASES[b][0] == "ssd":
                    pool.wait_ge(ssd_dve, 2)
                    for t in range(NT):
                        if t:
                            pool.wait_ge(ssd_mm, 3)
                        pool.tensor_tensor(
                            out=scr[:, 0, :].rearrange("p (h i) -> p h i", i=CH),
                            in0=dtv[:, DA, t, :].rearrange("p (h i) -> p h i", i=1).broadcast_to([P, SSD_H, CH]),
                            in1=mask[:, :].rearrange("p (h i) -> p h i", h=1).broadcast_to([P, SSD_H, CH]),
                            op=ALU.mult).then_inc(ssd_r, 1)
                    pool.wait_ge(ssd_dve, SSD_WEIGHTS)
                    pool.wait_ge(ssd_mm, 5)
                    pipeline(pool, SSD_G, side_products)

        @block.scalar
        def _(act):
            def hi(slot, count):
                act.wait_ge(loaded[slot], (count + 1) * 32)
                if not (isinstance(count, int) and count == 0):
                    act.wait_ge(tile_mm[slot], count * 2)
                act.activation(ws[:, slot, 0, :], raw[:, slot, :], ACT.Copy).then_inc(hi_done[slot], 1)

            def low_halves(slot, count, banks, done):
                for c in range(2):
                    act.wait_ge(tile_mm[slot], count * 2 + c + 1)
                    act.activation(lo2[:, c, :], ps[:, banks + c, T:2 * T], ACT.Copy).then_inc(done, 1)

            def tiles_out(slot, count, banks, outs, done):
                for c in range(2):
                    act.wait_ge(tile_mm[slot], count * 2 + c + 1)
                    act.activation(outs[c], ps[:, banks + c, 0:T], ACT.Copy).then_inc(done, 1)

            def norm(b):
                if b > 0:
                    act.wait_ge(sqrt_ready, b)
                act.activation(DUMMY, EPS_COL, ACT.Sqrt).then_inc(sqrt_ready, 1)

                def mean_root(src, col, squares, roots, count):
                    act.activation(JUNK, src, ACT.Square, accum_out=sm[:, col:col + 1]).then_inc(squares, 1)
                    act.wait_ge(squares, count)
                    act.activation(sm[:, col + 4:col + 5], sm[:, col:col + 1], ACT.Sqrt, scale=1.0 / D,
                                   bias=EPS_COL).then_inc(roots, 1)
                if b > 0:
                    slot = SLOT_DOWN if PHASES[b - 1][0] == "ffn" else SLOT_O
                    for t in range(NT):
                        act.wait_ge(tile_mm[slot], 2 * used_before(b, slot) - 1 + t)
                        mean_root(ps[:, 2 * t:2 * t + 2, :].rearrange("p b n -> p (b n)"), t, sq_post, root_post,
                                  NT * (b - 1) + t + 1)
                if b == NPH:
                    return
                for t in range(NT):
                    if b == 0:
                        act.wait_ge(x_in, 16 * NT)
                    else:
                        act.wait_ge(x_ready, NT * (b - 1) + t + 1)
                    mean_root(xres[:, t, :], 2 + t, sq_pre, root_pre, NT * b + t + 1)
                for t in range(NT):
                    for q in range(2):
                        act.wait_ge(xnT, 2 * NT * b + 2 * t + q + 1)
                        act.activation(xT[:, 4 * q:4 * q + 4, 0, t * P:(t + 1) * P],
                                       ps[:, A + 2 * t + q, :].rearrange("p (k n) -> p k n", k=4),
                                       ACT.Copy).then_inc(xT_hi, 1)

            def ffn(ph):
                f = ffns_before(ph) * NF * 2
                n0 = [used_before(ph, s) for s in range(4)]
                last = ph == NPH - 1

                def body(i, split_next):
                    low_halves(SLOT_GATE, i + n0[SLOT_GATE], A, gate_lo)
                    if split_next:
                        hi(SLOT_GATE, i + n0[SLOT_GATE] + 1)
                    for c in range(2):
                        act.wait_ge(gate_sum, i * 2 + f + c + 1)
                        act.activation(fm[:, c, :], ca[:, c, :], ACT.Silu).then_inc(silu_g, 1)
                    hi(SLOT_DOWN, i + n0[SLOT_DOWN])
                    low_halves(SLOT_UP, i + n0[SLOT_UP], C, up_lo)
                    for c in range(2):
                        act.wait_ge(h_done, i * 2 + f + c + 1)
                        act.activation(hT[:, c, 0, :], fm[:, 2 + c, :], ACT.Copy).then_inc(h_hi, 1)
                    if split_next:
                        hi(SLOT_UP, i + n0[SLOT_UP] + 1)
                if ph == 0:
                    body(0, True)
                with act.Fori(1 if ph == 0 else 0, NF - 1 if last else NF) as i:
                    body(i, True)
                if last:
                    body(NF - 1, False)

            def gla_start(n0):
                act.wait_ge(params_in, 16 * 11)
                act.activation(sw[:, :, 0, 0:GLA_RANK], lrw[:, :, :], ACT.Copy).then_inc(small_hi, 1)
                act.wait_ge(cols_T, 1)
                act.activation(pcol[:, :, :].rearrange("p a n -> p (a n)"), ps[:, B, 0:256], ACT.Copy).then_inc(cols_done, 1)
                act.wait_ge(small_mm, 2)
                act.activation(lrt[:, :, :], ps[:, C:E + 1, GLA_RANK:2 * GLA_RANK], ACT.Copy).then_inc(small_lo_out, 1)
                tiles_out(SLOT_P1, n0[SLOT_P1], A, [ca[:, c, :] for c in range(2)], p1_out)
                hi(SLOT_P3, n0[SLOT_P3])
                et = scr[:, 0, 1024:2048]
                act.wait_ge(gla_dve, 3)
                act.activation(et, et, ACT.Exp, scale=-1.0).then_inc(gla_act, 1)
                act.wait_ge(gla_act, 1)
                act.activation(et, et, ACT.Ln, bias=1.0).then_inc(gla_act, 1)
                tiles_out(SLOT_P2, n0[SLOT_P2], A, [zf[:, t, :] for t in range(2)], p2_out)
                hi(SLOT_P1, n0[SLOT_P1] + 1)
                b16, dm, de = scr[:, 0, 0:1024], scr[:, 0, 1024:2048], scr[:, 1, 0:1024]
                act.wait_ge(gla_dve, 7)
                nrm = 1.0 / 16.0
                act.activation(exps[:, 1024:2048], dm, ACT.Exp, scale=-nrm).then_inc(gla_act, 1)
                act.activation(exps[:, 3072:4096], de, ACT.Exp, scale=nrm).then_inc(gla_act, 1)
                act.activation(exps[:, 0:1024], dm, ACT.Exp, scale=nrm).then_inc(gla_act, 1)
                act.activation(exps[:, 2048:3072], b16, ACT.Exp, scale=nrm).then_inc(gla_act, 1)
                act.activation(edl[:, 0, 0:16], b16.rearrange("p (n i) -> p n i", i=CH)[:, :, CH - 1], ACT.Exp,
                               scale=nrm).then_inc(gla_act, 1)
                hi(SLOT_P2, n0[SLOT_P2] + 1)
                tiles_out(SLOT_P3, n0[SLOT_P3], C, [vs[:, t, :] for t in range(2)], p3_out)

            def ssd_start(n0):
                act.activation(sw[:, :, 0, :], dtw[:, :, :], ACT.Copy).then_inc(small_hi, 1)
                act.activation(hb[:, 0, :], hb[:, 0, :], ACT.Exp).then_inc(ssd_act, 1)
                act.wait_ge(small_mm, 4)
                act.activation(dtv[:, TA, :, :], ps[:, C:E + 1, SSD_H:2 * SSD_H], ACT.Copy).then_inc(small_lo_out, 1)
                act.wait_ge(ssd_dve, 1)
                act.activation(dtv[:, TB, :, :], dtv[:, TB, :, :], ACT.Exp, scale=-1.0).then_inc(ssd_act, 1)
                tiles_out(SLOT_P1, n0[SLOT_P1], A, [feat[:, c, CONV - 1:] for c in range(2)], p1_out)
                hi(SLOT_P3, n0[SLOT_P3])
                act.wait_ge(ssd_dve, 3)
                act.activation(dtv[:, CDEC, :, :], dtv[:, CS, :, :], ACT.Exp).then_inc(ssd_act, 1)
                act.activation(dtv[:, TB, :, :], dtv[:, TA, :, :], ACT.Exp).then_inc(ssd_act, 1)
                act.activation(edl[:, :, :], edl[:, :, :], ACT.Exp).then_inc(ssd_act, 1)
                tiles_out(SLOT_P2, n0[SLOT_P2], A, [feat[:, 2 + c, CONV - 1:] for c in range(2)], p2_out)
                for k in range(4):
                    act.wait_ge(ssd_dve, SSD_WEIGHTS + k + 1)
                    act.activation(exps[:, k * 1024:(k + 1) * 1024], scr[:, 1, (k % 2) * 1024:(k % 2 + 1) * 1024],
                                   ACT.Exp).then_inc(ssd_act, 1)
                    if k == 0:
                        hi(SLOT_P1, n0[SLOT_P1] + 1)
                    if k == 1:
                        hi(SLOT_P2, n0[SLOT_P2] + 1)
                for c in range(4):
                    act.wait_ge(conv_step, 16 if c > 1 else 8)
                    tile = c if c < 2 else 8 * c
                    act.activation(fm[:, c, :], ca[:, c, :], ACT.Silu, bias=pcol[:, 1, tile:tile + 1]).then_inc(feat_done, 1)
                tiles_out(SLOT_P3, n0[SLOT_P3], C, [zf[:, t, :] for t in range(2)], p3_out)

            def mixer(ph, kind, n):
                G = groups_before(kind)
                n0 = [used_before(ph, s) for s in range(4)]
                ssd = kind == "ssd"
                gain0 = GS0 if ssd else GG0

                def body(g, proj, scan, outp):
                    if not scan and not outp:
                        return
                    first = isinstance(g, int) and g == 1
                    if scan:
                        if not first:
                            if ssd:
                                act.wait_ge(y_done, g - 1)
                            else:
                                act.wait_ge(y_out, 2 * (g - 1 + G))
                        act.wait_ge(p3_out if ssd else p2_out, 2 * (g - 1 + G) + 2)
                        act.activation(zs[:, :, :], zf[:, :, :], ACT.Silu).then_inc(zs_done, 1)
                    if proj:
                        if not ssd:
                            act.wait_ge(feat_done, 4 * (g + G))
                        tiles_out(SLOT_P1, g + n0[SLOT_P1], A,
                                  [feat[:, c, CONV - 1:] if ssd else ca[:, c, :] for c in range(2)], p1_out)
                    if outp:
                        act.wait_ge(yT_mm, g - 2 + G + 1)
                        for j in range(2):
                            act.activation(hT[:, j, 0, :], ps[:, C, j * T:(j + 1) * T], ACT.Copy,
                                           scale=pcol[:, 1, bass.ds(2 * g + (gain0 - 4 + j), 1)]).then_inc(yT_hi, 1)
                    if scan:
                        act.wait_ge(tok_T, g - 1 + G + 1)
                        if ssd:
                            if not first:
                                act.wait_ge(tok_mul, 4 * (g - 1))
                            act.activation(xtok[:, :, :].rearrange("p t n -> p (t n)"), ps[:, E, :],
                                           ACT.Copy).then_inc(tok_out, 1)
                        else:
                            act.activation(xw[:, :, 0:P], ps[:, E, 0:2 * P].rearrange("p (t n) -> p t n", t=2),
                                           ACT.Copy).then_inc(tok_out, 1)
                    if proj:
                        hi(SLOT_P3, g + n0[SLOT_P3])
                        tiles_out(SLOT_P2, g + n0[SLOT_P2], A,
                                  [feat[:, 2 + c, CONV - 1:] if ssd else zf[:, c, :] for c in range(2)], p2_out)
                    if scan and ssd:
                        act.wait_ge(e_mm, g - 1 + G + 1)
                        act.activation(bcb[:, :], ps[:, C, 0:384], ACT.Copy).then_inc(e_out, 1)
                    if proj:
                        hi(SLOT_P1, g + n0[SLOT_P1] + 1)
                        hi(SLOT_P2, g + n0[SLOT_P2] + 1)

                    def feature(c):
                        act.wait_ge(conv_step, 16 * g + (16 if c > 1 else 8))
                        tile = 2 * g + c if c < 2 else g + 8 * c
                        act.activation(fm[:, c, :], ca[:, c, :], ACT.Silu,
                                       bias=pcol[:, 1, bass.ds(tile, 1)]).then_inc(feat_done, 1)
                    if proj and ssd:
                        for c in range(3):
                            feature(c)
                    if scan:
                        hi(SLOT_O, g - 1 + n0[SLOT_O])
                        act.wait_ge(off_mm, g - 1 + G + 1)
                    if proj and ssd:
                        feature(3)
                    if scan:
                        if ssd:
                            act.wait_ge(y_done, g)
                        for t in range(NT):
                            act.activation(JUNK[:, t * 256:(t + 1) * 256], yn[:, t, :] if ssd else ps[:, A + t, 0:256],
                                           ACT.Square, accum_out=sm[:, 8 + t:9 + t]).then_inc(y_sq, 1)
                    if proj:
                        tiles_out(SLOT_P3, g + n0[SLOT_P3], C, [(zf if ssd else vs)[:, t, :] for t in range(2)], p3_out)
                pipeline(act, n, body)

            act.wait_ge(consts, CONST_EPS)
            norm(0)
            hi(SLOT_GATE, 0)
            hi(SLOT_UP, 0)
            for ph, (kind, layer, which) in enumerate(PHASES):
                if kind == "ffn":
                    ffn(ph)
                elif kind == "gla":
                    gla_start([used_before(ph, s) for s in range(4)])
                    mixer(ph, kind, GLA_H)
                else:
                    ssd_start([used_before(ph, s) for s in range(4)])
                    mixer(ph, kind, SSD_G)
                norm(ph + 1)

        @block.vector
        def _(dve):
            step = Links(dve, dve_step)

            def lo(slot, count):
                dve.wait_ge(hi_done[slot], count + 1)
                dve.tensor_tensor(ws[:, slot, 1, :], raw[:, slot, :], ws[:, slot, 0, :].bitcast(F32),
                                  ALU.subtract).then_inc(lo_done[slot], 1)

            def sums(low, count, banks, outs, done):
                for c in range(2):
                    dve.wait_ge(low, count + c + 1)
                    dve.tensor_tensor(outs[c], ps[:, banks + c, 0:T], lo2[:, c, :], ALU.add).then_inc(done, 1)

            def rsqrt2(ss, width):
                m, y, a, mh = (sm[:, o:o + 2] for o in (16, 18, 20, 22))
                step(dve.tensor_scalar(m, ss, 1.0 / width, EPS, ALU.mult, ALU.add))
                step.start(dve.tensor_scalar(mh, m, -0.5, None, ALU.mult))
                step(dve.tensor_scalar(y.bitcast(I32), m.bitcast(I32), 1, None, ALU.logical_shift_right))
                step(dve.tensor_scalar(y.bitcast(I32), y.bitcast(I32), -1.0, MAGIC, ALU.mult, ALU.add))
                for _ in range(3):
                    for o, wait in ((0, step.start), (1, step)):
                        c = slice(o, o + 1)
                        wait(dve.scalar_tensor_tensor(out=a[:, c], in0=y[:, c], scalar=mh[:, c], in1=y[:, c],
                                                      op0=ALU.mult, op1=ALU.mult))
                    step(dve.scalar_tensor_tensor(out=y, in0=a, scalar=1.5, in1=y, op0=ALU.add, op1=ALU.mult))
                return y

            def inverse_root(col, squares, roots, count):
                ss, root = sm[:, col:col + 1], sm[:, col + 4:col + 5]
                first = 13 if col == 3 else 10
                mh, y, a = (sm[:, o:o + 1] for o in range(first, first + 3))
                dve.wait_ge(squares, count)
                step.start(dve.tensor_scalar(mh, ss, -0.5 / D, -0.5 * EPS, ALU.mult, ALU.add))
                dve.wait_ge(roots, count)
                step(dve.reciprocal(y, root))
                step(dve.scalar_tensor_tensor(out=a, in0=y, scalar=mh, in1=y, op0=ALU.mult, op1=ALU.mult))
                step(dve.scalar_tensor_tensor(out=y, in0=a, scalar=1.5, in1=y, op0=ALU.add, op1=ALU.mult))
                return y

            def norm(b):
                if b > 0:
                    weight = 0.5 if PHASES[b - 1][0] == "ffn" else 1.0
                    dve.wait_ge(gpost_in, 16 * b)
                    for t in range(NT):
                        r = inverse_root(t, sq_post, root_post, NT * (b - 1) + t + 1)
                        dve.scalar_tensor_tensor(out=T1, in0=ps[:, 2 * t:2 * t + 2, :].rearrange("p b n -> p (b n)"),
                                                 scalar=r, in1=gpost[:, :], op0=ALU.mult, op1=ALU.mult).then_inc(post_read, 1)
                        dve.wait_ge(post_read, NT * (b - 1) + t + 1)
                        dve.scalar_tensor_tensor(out=xres[:, t, :], in0=T1, scalar=weight, in1=xres[:, t, :],
                                                 op0=ALU.mult, op1=ALU.add).then_inc(x_ready, 1)
                if b == NPH:
                    return
                if b == 0:
                    dve.wait_ge(x_in, 16 * NT)
                else:
                    dve.wait_ge(x_ready, NT * b)
                dve.wait_ge(gpre_in, 16 * (b + 1))
                step(dve.tensor_tensor(NORMED[:, 1, :], xres[:, 1, :], gpre[:, :], ALU.mult))
                for t in range(NT):
                    r = inverse_root(2 + t, sq_pre, root_pre, NT * b + t + 1)
                    if t == 0:
                        dve.wait_ge(xg_done, b + 1)
                    dve.tensor_scalar(NORMED[:, t, :], NORMED[:, t, :], r, None, ALU.mult).then_inc(xn_ready, 1)
                for t in range(NT):
                    for q in range(2):
                        dve.wait_ge(xT_hi, 2 * NT * b + 2 * t + q + 1)
                        dve.tensor_tensor(xT[:, 4 * q:4 * q + 4, 1, t * P:(t + 1) * P],
                                          ps[:, A + 2 * t + q, :].rearrange("p (k n) -> p k n", k=4),
                                          xT[:, 4 * q:4 * q + 4, 0, t * P:(t + 1) * P].bitcast(F32),
                                          ALU.subtract).then_inc(xT_lo, 1)

            def ffn(ph):
                f = ffns_before(ph) * NF * 2
                n0 = [used_before(ph, s) for s in range(4)]
                last = ph == NPH - 1

                def body(i, split_next):
                    sums(gate_lo, i * 2 + f, A, [ca[:, c, :] for c in range(2)], gate_sum)
                    if split_next:
                        lo(SLOT_GATE, i + n0[SLOT_GATE] + 1)
                    lo(SLOT_DOWN, i + n0[SLOT_DOWN])
                    sums(up_lo, i * 2 + f, C, [ca[:, 2 + c, :] for c in range(2)], up_sum)
                    for c in range(2):
                        dve.wait_ge(up_sum, i * 2 + f + c + 1)
                        dve.wait_ge(silu_g, i * 2 + f + c + 1)
                        dve.tensor_tensor(fm[:, 2 + c, :], fm[:, c, :], ca[:, 2 + c, :], ALU.mult).then_inc(h_done, 1)
                    for c in range(2):
                        dve.wait_ge(h_hi, i * 2 + f + c + 1)
                        dve.tensor_tensor(hT[:, c, 1, :], fm[:, 2 + c, :], hT[:, c, 0, :].bitcast(F32),
                                          ALU.subtract).then_inc(hT_ready, 1)
                    if split_next:
                        lo(SLOT_UP, i + n0[SLOT_UP] + 1)
                with dve.Fori(0, NF - 1 if last else NF) as i:
                    body(i, True)
                if last:
                    body(NF - 1, False)

            def gla_start(n0):
                dve.wait_ge(small_hi, 1)
                dve.tensor_tensor(sw[:, :, 1, 0:GLA_RANK], lrw[:, :, :], sw[:, :, 0, 0:GLA_RANK].bitcast(F32),
                                  ALU.subtract).then_inc(small_lo, 1)
                reset = scr[:, 1, 1024:2048]
                dve.wait_ge(xT_lo, 8)
                step(dve.memset(reset, 1.0))
                dve.memset(reset.rearrange("p (n i) -> p n i", i=CH)[:, :, 0:1], 0.0)
                dve.wait_ge(small_lo_out, 1)
                dve.tensor_tensor(lrt[:, :, :], lrt[:, :, :], ps[:, C:E + 1, 0:GLA_RANK], ALU.add).then_inc(gla_dve, 1)
                dve.wait_ge(gla_mm, 1)
                dve.tensor_copy(lrT, ps[0:GLA_RANK, C, 0:T]).then_inc(gla_dve, 1)
                z, et, g16 = scr[:, 0, 0:1024], scr[:, 0, 1024:2048], scr[:, 1, 0:1024]
                dve.wait_ge(gla_mm, 2)
                dve.wait_ge(cols_done, 1)
                for h in range(GLA_H):
                    step(dve.tensor_scalar(z[:, h * T:(h + 1) * T], ps[:, C + h // 2, (h % 2) * T:(h % 2 + 1) * T],
                                           pcol[:, 1, GB0 + h:GB0 + h + 1], None, ALU.add))
                dve.scalar_tensor_tensor(out=et, in0=z, scalar=-1.0, in1=z, op0=ALU.mult, op1=ALU.max).then_inc(gla_dve, 1)
                lo(SLOT_P3, n0[SLOT_P3])
                dve.wait_ge(gla_act, 2)
                dve.scalar_tensor_tensor(out=g16, in0=z, scalar=0.0, in1=et, op0=ALU.min, op1=ALU.subtract).then_inc(gla_dve, 1)
                dve.wait_ge(gla_dve, 4)
                dve.tensor_tensor_scan(out=z, data0=reset, data1=g16, initial=0.0, op0=ALU.mult,
                                       op1=ALU.add).then_inc(gla_dve, 1)
                dve.wait_ge(gla_dve, 5)

                def chunks(ap):
                    return ap.rearrange("p (n i) -> p n i", i=CH)
                dve.tensor_tensor(chunks(et), chunks(z), chunks(z)[:, :, CH // 2:CH // 2 + 1].broadcast_to([P, 16, CH]),
                                  ALU.subtract).then_inc(gla_dve, 1)
                dve.tensor_tensor(chunks(g16), chunks(z)[:, :, CH - 1:CH].broadcast_to([P, 16, CH]), chunks(z),
                                  ALU.subtract).then_inc(gla_dve, 1)
                lo(SLOT_P1, n0[SLOT_P1] + 1)
                dve.wait_ge(gla_act, 6)
                decayed(0, 0, (1, 3, 0, 2))
                lo(SLOT_P2, n0[SLOT_P2] + 1)

            def decayed(g, count, which):
                dve.wait_ge(p1_out, count + 2)
                for o in which:
                    dve.scalar_tensor_tensor(out=fm[:, o, :], in0=ca[:, o % 2, :], scalar=1.0 if o % 2 else P ** -0.5,
                                             in1=exps[:, bass.ds(g * T + o * 1024, T)],
                                             op0=ALU.mult, op1=ALU.mult).then_inc(feat_done, 1)

            def convolution(g, c0):
                for k in range(CONV):
                    for j in range(2):
                        c = c0 + j
                        tile = 2 * g + c if c < 2 else g + 8 * c
                        src, tap = feat[:, c, k:k + T], pcol[:, 0, bass.ds(tile + 32 * k, 1)]
                        if k == 0:
                            ins = dve.tensor_scalar(ca[:, c, :], src, tap, None, ALU.mult)
                        else:
                            dve.wait_ge(conv_step, 16 * g + (4 * c0 + 2 * k + j - 1))
                            ins = dve.scalar_tensor_tensor(out=ca[:, c, :], in0=src, scalar=tap, in1=ca[:, c, :],
                                                           op0=ALU.mult, op1=ALU.add)
                        ins.then_inc(conv_step, 1)

            def ssd_start(n0):
                dve.wait_ge(small_hi, 2)
                dve.tensor_tensor(sw[:, :, 1, :], dtw[:, :, :], sw[:, :, 0, :].bitcast(F32),
                                  ALU.subtract).then_inc(small_lo, 1)
                v = [dtv[:, r, :, :] for r in range(8)]

                def over_t(ap):
                    return ap.rearrange("p (t h) -> p t h", t=1).broadcast_to([P, NT, SSD_H])
                dve.wait_ge(small_lo_out, 2)
                step(dve.tensor_tensor(v[TA], v[TA], ps[:, C:E + 1, 0:SSD_H], ALU.add))
                step(dve.tensor_tensor(v[TA], v[TA], over_t(hb[:, 2, :]), ALU.add))
                dve.scalar_tensor_tensor(out=v[TB], in0=v[TA], scalar=-1.0, in1=v[TA], op0=ALU.mult, op1=ALU.max).then_inc(ssd_dve, 1)
                e, den, s, s2, q = v[TB], v[DT], v[CS], v[CSL], v[WST]
                dve.wait_ge(ssd_act, 2)
                step(dve.tensor_scalar(den, e, 2.0, None, ALU.add))
                step(dve.reciprocal(den, den))
                step(dve.tensor_tensor(s, e, den, ALU.mult))
                step(dve.tensor_tensor(s2, s, s, ALU.mult))
                step(dve.tensor_scalar(q, s2, 1.0 / 15, None, ALU.mult))
                for c in (13, 11, 9, 7, 5, 3):
                    step(dve.scalar_tensor_tensor(out=q, in0=q, scalar=1.0 / c, in1=s2, op0=ALU.add, op1=ALU.mult))
                step(dve.scalar_tensor_tensor(out=q, in0=q, scalar=1.0, in1=s, op0=ALU.add, op1=ALU.mult))
                step(dve.tensor_scalar(v[TA], v[TA], 0.0, None, ALU.max))
                step(dve.scalar_tensor_tensor(out=v[DT], in0=q, scalar=2.0, in1=v[TA], op0=ALU.mult, op1=ALU.add))
                dve.scalar_tensor_tensor(out=v[DA], in0=v[DT], scalar=-1.0, in1=over_t(hb[:, 0, :]), op0=ALU.mult,
                                         op1=ALU.mult).then_inc(ssd_dve, 1)
                lo(SLOT_P3, n0[SLOT_P3])
                dve.wait_ge(ssd_mm, 1)
                step(dve.tensor_copy(dtv[:, CS:CSL + 1, :, :].rearrange("p a t h -> p (a t h)"), ps[:, C, 0:128]))
                step(dve.tensor_copy(edl[:, :, :].rearrange("p c h -> p (c h)"), ps[:, C, 128:256]))
                dve.tensor_tensor(v[TA], v[CSL], v[CS], ALU.subtract).then_inc(ssd_dve, 1)
                G = groups_before("ssd")
                dve.wait_ge(p1_out, 2 * G + 2)
                convolution(0, 0)
                dve.wait_ge(ssd_act, 5)
                dve.tensor_tensor(v[WST], v[TB], v[DT], ALU.mult).then_inc(ssd_dve, 1)
                for k in range(4):
                    t, h = k // 2, k % 2
                    seg = scr[:, 1, h * 1024:(h + 1) * 1024].rearrange("p (h i) -> p h i", i=CH)
                    bank = A if h else C
                    dve.wait_ge(ssd_mm, 2 + k)
                    if t:
                        dve.wait_ge(ssd_act, 6 + h)
                    step(dve.tensor_tensor(seg, ps[:, bank:bank + 2, :].rearrange("p b (h i) -> p (b h) i", i=CH),
                                           dtv[:, CS, t, h * 16:(h + 1) * 16].rearrange("p (h i) -> p h i", i=1).broadcast_to([P, 16, CH]),
                                           ALU.subtract))
                    dve.tensor_scalar(seg, seg, 0.0, None, ALU.min).then_inc(ssd_dve, 1)
                    if k == 0:
                        lo(SLOT_P1, n0[SLOT_P1] + 1)
                    if k == 1:
                        lo(SLOT_P2, n0[SLOT_P2] + 1)
                dve.wait_ge(p2_out, 2 * G + 2)
                convolution(0, 2)

            def mixer(ph, kind, n):
                G = groups_before(kind)
                n0 = [used_before(ph, s) for s in range(4)]
                ssd = kind == "ssd"
                gain0 = GS0 if ssd else GG0

                def by_head(ap):
                    return ap.rearrange("p (h d) -> p h d", h=HPG)

                def heads(ap, rows=P):
                    return ap.rearrange("p (h d) -> p h d", d=1).broadcast_to([rows, HPG, HD])

                def body(g, proj, scan, outp):
                    if not scan and not outp:
                        return
                    first = isinstance(g, int) and g == 1
                    c0 = g * 2 + 2 * G
                    if outp:
                        for j in range(2):
                            dve.wait_ge(yT_hi, 2 * (g - 2 + G) + 2)
                            dve.scalar_tensor_tensor(out=hT[:, j, 1, :], in0=ps[:, C, j * T:(j + 1) * T],
                                                     scalar=pcol[:, 1, bass.ds(2 * g + (gain0 - 4 + j), 1)],
                                                     in1=hT[:, j, 0, :].bitcast(F32), op0=ALU.mult,
                                                     op1=ALU.subtract).then_inc(yT_lo, 1)
                    if proj:
                        lo(SLOT_P3, g + n0[SLOT_P3])
                        if ssd:
                            dve.wait_ge(p1_out, c0 + 2)
                            dve.wait_ge(feat_done, 4 * (g + G))
                            convolution(g, 0)
                    if scan:
                        mk = mask[:, :].rearrange("p (t i) -> p t i", t=1).broadcast_to([P, NT, CH])
                        if ssd:
                            dve.wait_ge(e_out, g)
                            cb = bcb[:, 256:384].rearrange("p (t i) -> p t i", t=2)
                            step(dve.tensor_tensor(cb, cb, mk, ALU.mult))
                            for t in range(NT):
                                dve.tensor_tensor(
                                    wm[:, t, :, :],
                                    exps[:, bass.ds(g * HPG * CH + (t * 2048 - HPG * CH), HPG * CH)].rearrange("p (h i) -> p h i", h=HPG),
                                    cb[:, t, :].rearrange("p (h i) -> p h i", h=1).broadcast_to([P, HPG, CH]),
                                    ALU.mult).then_inc(w_done, 1)
                        else:
                            dve.wait_ge(e_mm, g - 1 + G + 1)
                            dve.tensor_tensor(wm[:, :, 0, :], ps[:, C, 0:P].rearrange("p (t i) -> p t i", t=2), mk,
                                              ALU.mult).then_inc(w_done, 2)
                    if proj:
                        lo(SLOT_P1, g + n0[SLOT_P1] + 1)
                        if ssd:
                            dve.wait_ge(p2_out, c0 + 2)
                            convolution(g, 2)
                        else:
                            decayed(g, c0, (1, 3, 0))
                    if scan:
                        bank = [(E, 0), (C, 0), (E, 256)]
                        for c in range(3):
                            dve.wait_ge(upd_mm, 2 * (g - 1 + G) + (1 if c == 0 else 2))
                            new = ps[:, bank[c][0], bank[c][1]:bank[c][1] + 256]
                            if c == 0:
                                dve.tensor_copy(st[:, 0, :], new).then_inc(state_done, 1)
                                continue
                            dve.wait_ge(state_done, 3 * (g - 1 + G) + c)
                            if ssd:
                                step(dve.tensor_tensor(by_head(st[:, c, :]), by_head(st[:, c - 1, :]),
                                                       heads(edl[:, c, bass.ds((g - 1) * HPG, HPG)]), ALU.mult))
                                dve.tensor_tensor(st[:, c, :], st[:, c, :], new, ALU.add).then_inc(state_done, 1)
                            else:
                                dve.scalar_tensor_tensor(out=st[:, c, :], in0=st[:, c - 1, :],
                                                         scalar=edl[:, 0, bass.ds(4 * g + (c - 4), 1)], in1=new,
                                                         op0=ALU.mult, op1=ALU.add).then_inc(state_done, 1)
                    if proj:
                        lo(SLOT_P2, g + n0[SLOT_P2] + 1)
                    if scan:
                        if not first:
                            dve.wait_ge(yT_mm, g - 1 + G)
                        if ssd:
                            dve.wait_ge(tok_mul, 4 * g)
                            dve.wait_ge(in_mm, g)
                            y_all = yn[:, :, :].rearrange("p t n -> p (t n)")
                            hs = bass.ds((g - 1) * HPG, HPG)
                            step(dve.tensor_tensor(y_all, ps[:, A, :], dx[:, :, :].rearrange("p t n -> p (t n)"), ALU.add))
                            dve.wait_ge(off_mm, g - 1 + G + 1)
                            for t in range(NT):
                                r = slice(CH, P) if t == 0 else slice(0, P)
                                dve.tensor_tensor(by_head(vs[r, t, :]), by_head(ps[r, B, t * 256:(t + 1) * 256]),
                                                  heads(dtv[r, CDEC, t, hs], r.stop - r.start), ALU.mult).then_inc(y_out, 1)
                            for t in range(NT):
                                r = slice(CH, P) if t == 0 else slice(0, P)
                                dve.wait_ge(y_out, 2 * (g - 1 + G) + t + 1)
                                step.start(dve.tensor_tensor(yn[r, t, :], yn[r, t, :], vs[r, t, :], ALU.add))
                            step.wait()
                            dve.wait_ge(zs_done, g - 1 + G + 1)
                            dve.tensor_tensor(y_all, y_all, zs[:, :, :].rearrange("p t n -> p (t n)"), ALU.mult).then_inc(y_done, 1)
                        else:
                            dve.wait_ge(zs_done, g - 1 + G + 1)
                            for t in range(NT):
                                dve.wait_ge(y_sq, 2 * (g - 1 + G) + t + 1)
                                dve.tensor_tensor(yn[:, t, :], ps[:, A + t, 0:256], zs[:, t, :], ALU.mult).then_inc(y_out, 1)
                            if proj:
                                decayed(g, c0, (2,))
                        lo(SLOT_O, g - 1 + n0[SLOT_O])
                        dve.wait_ge(y_sq, 2 * (g - 1 + G) + 2)
                        y = rsqrt2(sm[:, 8:10], 256)
                        if ssd:
                            dve.wait_ge(y_done, g)
                        else:
                            dve.wait_ge(y_out, 2 * (g - 1 + G) + 2)
                        for t in range(NT):
                            dve.tensor_scalar(yn[:, t, :], yn[:, t, :], y[:, t:t + 1], None, ALU.mult).then_inc(yn_done, 1)

                body(0, True, False, False)
                body(1, True, True, False)
                per = SSD_STEPS if ssd else GLA_STEPS
                with dve.Fori(2, n) as g:
                    step.body(g, 2, per)
                    body(g, True, True, True)
                step.after(n - 2, per)
                body(n, False, True, True)
                body(n + 1, False, False, True)

            norm(0)
            lo(SLOT_GATE, 0)
            lo(SLOT_UP, 0)
            dve.wait_ge(consts, CONST_ALL)
            for ph, (kind, layer, which) in enumerate(PHASES):
                if kind == "ffn":
                    ffn(ph)
                elif kind == "gla":
                    gla_start([used_before(ph, s) for s in range(4)])
                    dve.wait_ge(gla_act, 7)
                    mixer(ph, kind, GLA_H)
                else:
                    ssd_start([used_before(ph, s) for s in range(4)])
                    dve.wait_ge(ssd_act, 9)
                    mixer(ph, kind, SSD_G)
                norm(ph + 1)

        @block.tensor
        def _(pe):
            def features(slot, banks):
                for c in range(2):
                    bank = ps[:, banks + c, :]
                    for k in range(KD):
                        off = k * UW + c * P
                        pe.matmul(bank, ws[:, slot, 0, off:off + P], xT[:, k, :, :].rearrange("p a t -> p (a t)"),
                                  start=(k == 0), stop=False, skip_group_check=True)
                        mm = pe.matmul(bank[:, 0:T], ws[:, slot, 1, off:off + P], xT[:, k, 0, :],
                                       start=False, stop=(k == KD - 1), skip_group_check=True)
                    mm.then_inc(tile_mm[slot], 1)

            def feature_tiles(slot, banks):
                for c in range(2):
                    for k in range(KD):
                        off = k * UW + c * P
                        for a, b in ((0, 0), (0, 1), (1, 0)):
                            mm = pe.matmul(ps[:, banks + c, 0:T], ws[:, slot, a, off:off + P], xT[:, k, b, :],
                                           start=(k == 0 and a + b == 0), stop=(k == KD - 1 and a == 1),
                                           skip_group_check=True)
                    mm.then_inc(tile_mm[slot], 1)

            def token_tiles(slot, banks):
                for t in range(NT):
                    for k in range(KD):
                        for a, b in ((0, 0), (0, 1), (1, 0)):
                            mm = pe.matmul(ps[:, banks + t, 0:UW], xT[:, k, a, t * P:(t + 1) * P],
                                           ws[:, slot, b, k * UW:(k + 1) * UW],
                                           start=(k == 0 and a + b == 0), stop=(k == KD - 1 and a == 1),
                                           skip_group_check=True)
                    mm.then_inc(tile_mm[slot], 1)

            def open_banks(ph):
                if ph == 0:
                    pe.wait_ge(consts, CONST_EPS)
                else:
                    pe.wait_ge(post_read, NT * ph)
                for b in range(4):
                    for q in range(4):
                        pe.matmul(ps[:, b, q * P:(q + 1) * P], zr[:, :], zr[:, :], start=(q == 0), stop=False,
                                  skip_group_check=True)

            def output(slot, last):
                for t in range(NT):
                    for n in range(2):
                        for j in range(2):
                            for a, b in ((0, 0), (0, 1), (1, 0)):
                                off = j * D + n * 512
                                mm = pe.matmul(ps[:, 2 * t + n, :], hT[:, j, a, t * P:(t + 1) * P],
                                               ws[:, slot, b, off:off + 512], start=False,
                                               stop=(last and j == 1 and a == 1), skip_group_check=True)
                    mm.then_inc(tile_mm[slot], 1)

            def split(slot, count):
                pe.wait_ge(lo_done[slot], count + 1)

            def norm(b):
                open_banks(b)
                for t in range(NT):
                    pe.wait_ge(xn_ready, NT * b + t + 1)
                    for q in range(2):
                        for k in range(4):
                            col = (4 * q + k) * P
                            mm = pe.transpose(ps[:, A + 2 * t + q, k * P:(k + 1) * P], NORMED[:, t, col:col + P], ident[:, :])
                        mm.then_inc(xnT, 1)

            def ffn(ph):
                f = ffns_before(ph) * NF * 2
                n0 = [used_before(ph, s) for s in range(4)]
                pe.wait_ge(xT_lo, 2 * NT * (ph + 1))

                def body(i, first):
                    split(SLOT_GATE, i + n0[SLOT_GATE])
                    if not first:
                        pe.wait_ge(gate_sum, i * 2 + f)
                    features(SLOT_GATE, A)
                    if not first:
                        split(SLOT_DOWN, i + n0[SLOT_DOWN] - 1)
                        pe.wait_ge(hT_ready, i * 2 + f)
                        output(SLOT_DOWN, False)
                    split(SLOT_UP, i + n0[SLOT_UP])
                    if not first:
                        pe.wait_ge(up_sum, i * 2 + f)
                    features(SLOT_UP, C)
                body(0, True)
                with pe.Fori(1, NF) as i:
                    body(i, False)
                split(SLOT_DOWN, NF - 1 + n0[SLOT_DOWN])
                pe.wait_ge(hT_ready, NF * 2 + f)
                output(SLOT_DOWN, True)

            def small(width):
                for t in range(NT):
                    bank = ps[:, C + t, 0:2 * width]
                    for k in range(KD):
                        pe.matmul(bank.rearrange("p (a n) -> p a n", a=2), xT[:, k, 0, t * P:(t + 1) * P],
                                  sw[:, k, :, 0:width], start=(k == 0), stop=False, skip_group_check=True)
                        mm = pe.matmul(bank[:, 0:width], xT[:, k, 1, t * P:(t + 1) * P], sw[:, k, 0, 0:width],
                                       start=False, stop=(k == KD - 1), skip_group_check=True)
                    mm.then_inc(small_mm, 1)

            def gla_start(n0):
                pe.wait_ge(params_in, 16 * 11)
                for a in range(2):
                    mm = pe.transpose(ps[:, B, a * P:(a + 1) * P], prow[:, a, :], ident[:, :])
                mm.then_inc(cols_T, 1)
                pe.wait_ge(small_lo, 1)
                small(GLA_RANK)
                split(SLOT_P1, n0[SLOT_P1])
                pe.wait_ge(cols_done, 1)
                feature_tiles(SLOT_P1, A)
                pe.wait_ge(gla_dve, 1)
                for t in range(NT):
                    mm = pe.transpose(ps[0:GLA_RANK, C, t * P:(t + 1) * P], lrt[:, t, :], ident[:, :])
                mm.then_inc(gla_mm, 1)
                pe.wait_ge(gla_dve, 2)
                for h in range(GLA_H):
                    mm = pe.matmul(ps[:, C + h // 2, (h % 2) * T:(h % 2 + 1) * T], wgk[:, h * P:(h + 1) * P], lrT,
                                   start=True, stop=True, skip_group_check=True)
                mm.then_inc(gla_mm, 1)
                split(SLOT_P2, n0[SLOT_P2])
                pe.wait_ge(p1_out, 2)
                token_tiles(SLOT_P2, A)
                split(SLOT_P3, n0[SLOT_P3])
                pe.wait_ge(gla_dve, 3)
                token_tiles(SLOT_P3, C)

            def ssd_start(n0):
                G = groups_before("ssd")
                pe.wait_ge(small_lo, 2)
                small(SSD_H)
                split(SLOT_P1, n0[SLOT_P1])
                feature_tiles(SLOT_P1, A)
                pe.wait_ge(consts, CONST_ALL)
                pe.wait_ge(ssd_dve, 2)
                for t in range(NT):
                    rhs = dtv[:, DA, t, :]
                    for o, lhs in ((0, tri[:, :]), (64, blk[:, :])):
                        pe.matmul(ps[:, C, o + t * 32:o + (t + 1) * 32], lhs, rhs, start=True, stop=True, skip_group_check=True)
                    for c in range(2):
                        o = 128 + (2 * t + c) * 32
                        mm = pe.matmul(ps[:, C, o:o + 32], half[:, c, :], rhs, start=True, stop=True, skip_group_check=True)
                mm.then_inc(ssd_mm, 1)
                split(SLOT_P2, n0[SLOT_P2])
                pe.wait_ge(p1_out, 2 * G + 2)
                feature_tiles(SLOT_P2, A)
                pe.wait_ge(ssd_dve, 3)
                for k in range(4):
                    t, h = k // 2, k % 2
                    if h == 0:
                        pe.wait_ge(ssd_r, t + 1)
                    if k == 1:
                        pe.wait_ge(p2_out, 2 * G + 2)
                    if t:
                        pe.wait_ge(ssd_dve, SSD_WEIGHTS + h + 1)
                    for b in range(2):
                        mm = pe.matmul(ps[:, (A if h else C) + b, :], blk[:, :],
                                       scr[:, 0, (2 * h + b) * 512:(2 * h + b + 1) * 512], start=True, stop=True,
                                       skip_group_check=True)
                    mm.then_inc(ssd_mm, 1)
                split(SLOT_P3, n0[SLOT_P3])
                pe.wait_ge(ssd_dve, SSD_WEIGHTS + 3)
                token_tiles(SLOT_P3, C)
                pe.wait_ge(ssd_dve, SSD_WEIGHTS + 4)

            def mixer(ph, kind, n):
                G = groups_before(kind)
                n0 = [used_before(ph, s) for s in range(4)]
                ssd = kind == "ssd"

                def body(g, proj, scan, outp):
                    if not scan and not outp:
                        return
                    first = isinstance(g, int) and g == 1
                    last = not proj and not scan
                    c0 = g * 2 + 2 * G
                    if proj:
                        split(SLOT_P1, g + n0[SLOT_P1])
                        if scan and not first:
                            pe.wait_ge(y_out, c0 - 2)
                        if scan:
                            pe.wait_ge(p2_out, c0)
                        feature_tiles(SLOT_P1, A)
                    if outp:
                        pe.wait_ge(yn_done, 2 * (g - 2 + G) + 2)
                        if scan:
                            pe.wait_ge(p3_out, c0)
                        for j in range(2):
                            for t in range(NT):
                                mm = pe.transpose(ps[:, C, j * T + t * P:j * T + (t + 1) * P],
                                                  yn[:, t, j * P:(j + 1) * P], ident[:, :])
                        mm.then_inc(yT_mm, 1)
                    if scan:
                        pe.wait_ge(feat_done, 4 * (g - 1 + G) + 4)
                        pe.wait_ge(p3_out, 2 * (g - 1 + G) + 2)
                        for t in range(NT):
                            if ssd:
                                for j in range(2):
                                    o = (2 * t + j) * P
                                    mm = pe.transpose(ps[:, E, o:o + P], fm[:, j, t * P:(t + 1) * P], ident[:, :])
                            else:
                                mm = pe.transpose(ps[:, E, t * P:(t + 1) * P], fm[:, 3, t * P:(t + 1) * P], ident[:, :])
                        mm.then_inc(tok_T, 1)
                    if proj:
                        split(SLOT_P2, g + n0[SLOT_P2])
                        pe.wait_ge(p1_out, c0 + 2)
                        if ssd:
                            feature_tiles(SLOT_P2, A)
                        else:
                            token_tiles(SLOT_P2, A)
                    if scan:
                        if outp:
                            pe.wait_ge(yT_lo, 2 * (g - 2 + G) + 2)
                        if ssd:
                            for t in range(NT):
                                pe.transpose(ps[:, C, t * P:(t + 1) * P], fm[:, 2, t * P:(t + 1) * P], ident[:, :])
                        for c in range(4):
                            i, o = slice(c * CH, (c + 1) * CH), (256 if ssd else 0) + (c // 2) * CH
                            kv, q = (2, 3) if ssd else (1, 0)
                            r = slice((c % 2) * CH, (c % 2 + 1) * CH)
                            mm = pe.matmul(ps[r, C, o:o + CH], fm[:, kv, i], fm[:, q, i], start=True, stop=True,
                                           skip_group_check=True)
                        mm.then_inc(e_mm, 1)
                    if outp:
                        split(SLOT_O, g - 2 + n0[SLOT_O])
                        pe.wait_ge(yT_lo, 2 * (g - 2 + G) + 2)
                        output(SLOT_O, last)
                    if scan:
                        pe.wait_ge(tok_out, g - 1 + G + 1)
                        if ssd:
                            pe.wait_ge(e_out, g)
                        pe.wait_ge(w_done, 2 * (g - 1 + G) + 2)
                        if ssd:
                            pe.wait_ge(tok_mul, 4 * (g - 1) + 2)
                        if proj:
                            pe.wait_ge(p2_out, c0 + 2)
                        for c, (bank, o) in ((0, (E, 0)), (2, (E, 256)), (1, (C, 0))):
                            r, t = slice((c % 2) * CH, (c % 2 + 1) * CH), c // 2
                            keys = bcb[r, t * P:(t + 1) * P] if ssd else xw[r, t, 0:P]
                            vals = xw[r, t, :] if ssd else vs[r, t, :]
                            mm = pe.matmul(ps[:, bank, o:o + 256], keys, vals, start=True, stop=True, skip_group_check=True)
                            if c:
                                mm.then_inc(upd_mm, 1)
                        if ssd:
                            for t in range(NT):
                                for h in range(HPG):
                                    for c in range(2):
                                        r, o = slice(c * CH, (c + 1) * CH), t * 256 + h * HD
                                        mm = pe.matmul(ps[r, A, o:o + HD], wm[r, t, h, :], xdt[r, t, h * HD:(h + 1) * HD],
                                                       start=True, stop=True, skip_group_check=True)
                            mm.then_inc(in_mm, 1)
                        else:
                            for c in range(4):
                                r, t = slice((c % 2) * CH, (c % 2 + 1) * CH), c // 2
                                pe.matmul(ps[r, A + t, 0:256], wm[r, t, 0, :], vs[r, t, :], start=True, stop=(c == 0),
                                          skip_group_check=True)
                        for c in range(1, 4):
                            pe.wait_ge(state_done, 3 * (g - 1 + G) + c)
                            r, t = slice((c % 2) * CH, (c % 2 + 1) * CH), c // 2
                            dst = ps[r, B, t * 256:(t + 1) * 256] if ssd else ps[r, A + t, 0:256]
                            mm = pe.matmul(dst, fm[:, 3 if ssd else 2, c * CH:(c + 1) * CH], st[:, c - 1, :], start=ssd,
                                           stop=True, skip_group_check=True)
                        mm.then_inc(off_mm, 1)
                    if proj:
                        split(SLOT_P3, g + n0[SLOT_P3])
                        if scan:
                            pe.wait_ge(state_done, 3 * (g - 1 + G) + 3)
                        token_tiles(SLOT_P3, C)
                pipeline(pe, n, body)

            norm(0)
            for ph, (kind, layer, which) in enumerate(PHASES):
                if kind == "ffn":
                    ffn(ph)
                else:
                    n0 = [used_before(ph, s) for s in range(4)]
                    pe.wait_ge(xT_lo, 2 * NT * (ph + 1))
                    if kind == "gla":
                        gla_start(n0)
                        mixer(ph, kind, GLA_H)
                    else:
                        ssd_start(n0)
                        mixer(ph, kind, SSD_G)
                if ph + 1 < NPH:
                    norm(ph + 1)


_INS = ["x", "ffn_w_gate", "ffn_w_up", "ffn_w_down", "norm_gain", "gla_w_in", "gla_w_gk2", "gla_b_gk", "gla_norm",
        "gla_w_out", "ssd_w_in", "ssd_conv_w", "ssd_conv_b", "ssd_dt_bias", "ssd_A_log", "ssd_D", "ssd_norm",
        "ssd_w_out"]


def kernel(**inputs):
    import numpy as np
    import concourse.bacc as bacc
    from concourse.bass_utils import run_bass_kernel_spmd

    nc = bacc.Bacc("TRN2", target_bir_lowering=False, num_devices=1)
    arrays, args = {}, []
    for name in _INS:
        a = np.ascontiguousarray(inputs[name])
        arrays[f"in_{name}"] = a
        args.append(nc.dram_tensor(f"in_{name}", a.shape, mybir.dt.from_np(a.dtype), kind="ExternalInput").ap())
    args.append(nc.dram_tensor("out_y", (1, T, D), F32, kind="ExternalOutput").ap())
    trunk(nc, *args)
    r = run_bass_kernel_spmd(nc, [arrays], core_ids=[0])
    return r.results[0]["out_y"]
```

```python
from contextlib import ExitStack

import concourse.bass as bass
from concourse import mybir

ALU = mybir.AluOpType
ACT = mybir.ActivationFunctionType
F32 = mybir.dt.float32
F32R = mybir.dt.float32r
I32 = mybir.dt.int32

P = 128
T = 256
NT = T // P
D = 1024
KD = D // P
D_FF = 2816
UW = 256
UNIT = KD * UW
NF = D_FF // UW
EPS = 1e-6
CH = 64
HPG = 4
HD = 64
GLA_H = 4
GLA_RANK = 16
SSD_G = 8
SSD_H = 32
DI = 2048
CONV = 4
KEEP_WARM = 3
MAGIC = float(0x5F3759DF)
SLOT_P1, SLOT_P2, SLOT_P3, SLOT_O = 0, 1, 2, 3
SLOT_GATE, SLOT_UP, SLOT_DOWN = 0, 1, 2
CONST_IDENT, CONST_EPS, CONST_ALL = 2, 5, 18
SSD_WEIGHTS = 4
SSD_STEPS, GLA_STEPS = 19, 13

PHASES = [("ffn", 0, 0), ("gla", 0, 0), ("ffn", 0, 1), ("ffn", 1, 0), ("ssd", 0, 0), ("ffn", 1, 1)]
NPH = len(PHASES)


def uses_in(kind, slot):
    if kind == "ffn":
        return NF if slot < 3 else 0
    return (GLA_H if kind == "gla" else SSD_G) + (0, 0, 1, -1)[slot]


def out_unit(g, n, n0):
    if isinstance(g, int) and g == n - 1:
        return SLOT_P3, n + n0[SLOT_P3]
    return SLOT_O, g + n0[SLOT_O]


def used_before(phase, slot):
    return sum(uses_in(PHASES[q][0], slot) for q in range(phase))


def groups_before(kind):
    return 0 if kind == "gla" else GLA_H


def weight_of(phase):
    return 0.5 if PHASES[phase][0] == "ffn" else 1.0


def ffns_before(phase):
    return sum(PHASES[q][0] == "ffn" for q in range(phase))


def pipeline(eng, n, body):
    body(0, True, False, False)
    body(1, True, True, False)
    with eng.Fori(2, n) as g:
        body(g, True, True, True)
    body(n, False, True, True)
    body(n + 1, False, False, True)


class Links:

    def __init__(self, eng, sem):
        self.eng, self.sem, self.base, self.k = eng, sem, 0, 0

    def __call__(self, ins):
        self.start(ins)
        self.wait()

    def start(self, ins):
        self.k += 1
        ins.then_inc(self.sem, 1)

    def wait(self):
        self.eng.wait_ge(self.sem, self.base + self.k)

    def body(self, i, start, per):
        self.before = self.base + self.k
        self.base, self.k = i * per + (self.before - start * per), 0

    def after(self, n, per):
        assert self.k == per, (self.k, per)
        self.base, self.k = self.before + n * per, 0


def trunk(nc, x, ffn_w_gate, ffn_w_up, ffn_w_down, norm_gain, gla_w_in, gla_w_gk2, gla_b_gk,
          gla_norm, gla_w_out, ssd_w_in, ssd_conv_w, ssd_conv_b, ssd_dt_bias, ssd_A_log, ssd_D,
          ssd_norm, ssd_w_out, out):
    with ExitStack() as ctx:
        def sb(name, shape, dt=F32):
            return ctx.enter_context(nc.sbuf_tensor(name, shape, dt))

        def sem(name):
            return ctx.enter_context(nc.semaphore(name))

        raw = sb("raw", [P, 4, UNIT])
        ws = sb("ws", [P, 4, 2, UNIT], F32R)
        xres = sb("xres", [P, NT, D])
        xT = sb("xT", [P, KD, 2, T], F32R)
        hT = sb("hT", [P, 2, 2, T], F32R)
        exps = sb("exps", [P, 4096])
        scr = sb("scr", [P, 2, 2048])
        gpost = sb("gpost", [P, D])
        gpre = sb("gpre", [P, D])
        lo2 = sb("lo2", [P, 2, T])
        feat = sb("feat", [P, 4, CONV - 1 + T])
        ca = sb("ca", [P, 4, T])
        fm = sb("fm", [P, 4, T])
        xdt = sb("xdt", [P, NT, 256])
        xw = sb("xw", [P, NT, 256])
        dx = sb("dx", [P, NT, 256])
        wm = sb("wm", [P, NT, HPG, CH])
        zf = sb("zf", [P, NT, 256])
        zs = sb("zs", [P, NT, 256])
        vs = sb("vs", [P, NT, 256])
        yn = sb("yn", [P, NT, 256])
        dtw = sb("dtw", [P, KD, SSD_H])
        sw = sb("sw", [P, KD, 2, SSD_H], F32R)
        ident = sb("ident", [P, P])
        tri = sb("tri", [P, P])
        blk = sb("blk", [P, P])
        half = sb("half", [P, 2, P])
        mask = sb("mask", [P, CH])
        zr = sb("zr", [P, P], F32R)
        pcol = sb("pcol", [P, 2, P])
        xtok = scr[:, 0, 0:512].rearrange("p (t n) -> p t n", t=NT)
        st = scr[:, 0, 512:1280].rearrange("p (c n) -> p c n", c=3)
        bcb = scr[:, 0, 1280:1664]
        prow = zs[:, 0, 0:2 * P].rearrange("p (a n) -> p a n", a=2)
        lrw = exps[:, 0:KD * GLA_RANK].rearrange("p (k n) -> p k n", k=KD)
        wgk = xdt[0:GLA_RANK, :, :].rearrange("p t n -> p (t n)")
        lrT = dx[0:GLA_RANK, 0, :]
        dtT = xw[0:SSD_H, 0, :]
        hb = sb("hb", [P, 3, SSD_H])
        dtv = sb("dtv", [P, 8, NT, SSD_H])
        edl = sb("edl", [P, 4, SSD_H])
        sm = sb("sm", [P, 44])
        ps = ctx.enter_context(nc.psum_tensor("ps", [P, 8, 512], F32))

        JUNK = scr[:, 1, 0:D]
        NORMED = scr[:, 0, :].rearrange("p (t d) -> p t d", t=NT)
        EPS_COL = {1.0: sm[:, 30:31], 0.5: sm[:, 31:32]}
        DUMMY = sm[:, 29:30]
        GAINED = scr[:, 1, D:2 * D], scr[:, 0, D:2 * D]
        R_ROWS = scr[:, 0, :], exps[:, 2048:4096]
        DT, DA, CS, CSL, WST, CDEC, TA, TB = range(8)
        A, B, C, E = 4, 5, 6, 7
        CW0, CB0 = 0, 0
        GG0, GS0, GB0 = 32, 40, 56

        loaded = [sem(f"loaded{s}") for s in range(4)]
        hi_done = [sem(f"hi_done{s}") for s in range(4)]
        lo_done = [sem(f"lo_done{s}") for s in range(4)]
        tile_mm = [sem(f"tile_mm{s}") for s in range(4)]
        params_in, x_in = sem("params_in"), [sem("x0_in"), sem("x1_in")]
        gpre_in, gpost_in = sem("gpre_in"), sem("gpost_in")
        stored = sem("stored")
        consts = sem("consts")
        cols_T, cols_done = sem("cols_T"), sem("cols_done")
        dve_step = sem("dve_step")
        sq_post, sq_pre = sem("sq_post"), sem("sq_pre")
        root_post, root_pre = sem("root_post"), sem("root_pre")
        sqrt_ready = sem("sqrt_ready")
        xg_done = sem("xg_done")
        post_read = sem("post_read")
        x_ready, xn_ready = sem("x_ready"), sem("xn_ready")
        xnT = sem("xnT")
        xT_hi, xT_lo = sem("xT_hi"), sem("xT_lo")
        gate_lo, up_lo = sem("gate_lo"), sem("up_lo")
        gate_sum, silu_g, h_done, h_hi, hT_ready = (sem(n) for n in (
            "gate_sum", "silu_g", "h_done", "h_hi", "hT_ready"))
        up_sum = sem("up_sum")
        small_hi, small_lo, small_mm, small_out, dt_T = (sem(n) for n in (
            "small_hi", "small_lo", "small_mm", "small_out", "dt_T"))
        gla_mm, gla_dve, gla_act = sem("gla_mm"), sem("gla_dve"), sem("gla_act")
        ssd_mm, ssd_dve, ssd_act, ssd_r = sem("ssd_mm"), sem("ssd_dve"), sem("ssd_act"), sem("ssd_r")
        p1_out, p2_out, p3_out = sem("p1_out"), sem("p2_out"), sem("p3_out")
        conv_step, feat_done = sem("conv_step"), sem("feat_done")
        tok_T, tok_out, tok_mul = sem("tok_T"), sem("tok_out"), sem("tok_mul")
        e_mm, e_out, w_done = sem("e_mm"), sem("e_out"), sem("w_done")
        upd_mm, state_done = sem("upd_mm"), sem("state_done")
        in_mm, off_mm = sem("in_mm"), sem("off_mm")
        y_done, y_sq, y_out, yn_done = sem("y_done"), sem("y_sq"), sem("y_out"), sem("yn_done")
        zs_done = sem("zs_done")
        yT_mm, yT_hi, yT_lo = sem("yT_mm"), sem("yT_hi"), sem("yT_lo")

        def gain_row(j):
            return norm_gain.rearrange("l n d -> (l n) d")[j:j + 1, :].broadcast_to([P, D])

        block = ctx.enter_context(nc.Block())

        @block.sync
        def _(sp):
            def at(value):
                return value if isinstance(value, int) else sp.snap(value)

            def cols(w, col, n=UW):
                return w.rearrange("(k p) n -> p k n", p=P)[:, :, bass.ds(col, n)]

            def load_cols(slot, w, col, count):
                dst = raw[:, slot, :].rearrange("p (k n) -> p k n", k=KD)
                src = cols(w, at(col))
                if count is not None:
                    sp.wait_ge(lo_done[slot], count)
                for h in (1, 0):
                    ks = slice(h * KD // 2, (h + 1) * KD // 2)
                    sp.dma_start(dst[:, ks, :], src[:, ks, :]).then_inc(loaded[slot], 16)

            def load_two(slot, w, col0, col1, count):
                dst = raw[:, slot, :].rearrange("p (k c n) -> p k c n", k=KD, c=2)
                starts = at(col0), at(col1)
                sp.wait_ge(lo_done[slot], count)
                for c, col in enumerate(starts):
                    sp.dma_start(dst[:, :, c, :], cols(w, col, P)).then_inc(loaded[slot], 16)

            def load_rows(slot, w, row, count):
                dst = raw[:, slot, :].rearrange("p (j n) -> p j n", j=2)
                starts = at(row), at(row + P)
                if count is not None:
                    sp.wait_ge(lo_done[slot], count)
                for j in (1, 0):
                    sp.dma_start(dst[:, j, :], w[bass.ds(starts[j], P), :]).then_inc(loaded[slot], 16)

            for t in range(NT):
                sp.dma_start(xres[:, t, :], x[0, t * P:(t + 1) * P, :]).then_inc(x_in[t], 16)

            def load_first(ph, slot):
                if ph == NPH:
                    return
                kind, layer, which = PHASES[ph]
                count = used_before(ph, slot) if ph else None
                if kind == "ffn":
                    load_cols(slot, (ffn_w_gate, ffn_w_up)[slot][layer, which], 0, count)
                elif kind == "gla":
                    if slot == SLOT_P1:
                        load_two(slot, gla_w_in[0], 0, 512, count)
                    else:
                        load_cols(slot, gla_w_in[0], 2048, count)
                elif slot == SLOT_P1:
                    load_cols(slot, ssd_w_in[0], DI, count)
                else:
                    load_two(slot, ssd_w_in[0], 2 * DI, 2 * DI + 1024, count)

            load_first(0, 0)
            load_first(0, 1)
            for ph, (kind, layer, which) in enumerate(PHASES):
                n0 = [used_before(ph, s) for s in range(4)]
                if kind == "ffn":
                    wg, wu, wd = (w[layer, which] for w in (ffn_w_gate, ffn_w_up, ffn_w_down))

                    def load_ffn(i, fresh=False):
                        load_cols(SLOT_GATE, wg, i * UW + UW, i + n0[SLOT_GATE] + 1)
                        load_rows(SLOT_DOWN, wd, i * UW, None if fresh else i + n0[SLOT_DOWN])
                        load_cols(SLOT_UP, wu, i * UW + UW, i + n0[SLOT_UP] + 1)
                    if ph == 0:
                        load_ffn(0, True)
                    with sp.Fori(1 if ph == 0 else 0, NF - 1) as i:
                        load_ffn(i)
                    load_first(ph + 1, 0)
                    load_rows(SLOT_DOWN, wd, (NF - 1) * UW, NF - 1 + n0[SLOT_DOWN])
                    load_first(ph + 1, 1)
                else:
                    ssd = kind == "ssd"
                    n = SSD_G if ssd else GLA_H
                    w, wo = (ssd_w_in[0], ssd_w_out[0]) if ssd else (gla_w_in[0], gla_w_out[0])

                    def load_p3(g):
                        load_cols(SLOT_P3, w, g * UW if ssd else g * UW + 1024, g + n0[SLOT_P3])

                    def load_p12(g):
                        if ssd:
                            load_cols(SLOT_P1, w, g * UW + DI, g + n0[SLOT_P1])
                            load_two(SLOT_P2, w, g * P + 2 * DI, g * P + 2 * DI + 1024, g + n0[SLOT_P2])
                        else:
                            load_two(SLOT_P1, w, g * P, g * P + 512, g + n0[SLOT_P1])
                            load_cols(SLOT_P2, w, g * UW + 2048, g + n0[SLOT_P2])

                    def load_out(g):
                        slot, count = out_unit(g, n, n0)
                        fresh = isinstance(count, int) and count == 0
                        load_rows(slot, wo, g * UW, None if fresh else count)
                    load_p3(0)
                    load_p12(1)
                    load_p3(1)
                    load_p12(2)
                    load_out(0)
                    with sp.Fori(2, n - 1) as g:
                        load_p3(g)
                        load_p12(g + 1)
                        load_out(g - 1)
                    load_p3(n - 1)
                    load_first(ph + 1, 0)
                    load_first(ph + 1, 1)
                    load_out(n - 2)
                    load_out(n - 1)
            for t in range(NT):
                sp.wait_ge(x_ready, NPH * NT - NT + t + 1)
                sp.dma_start(out[0, t * P:(t + 1) * P, :], xres[:, t, :]).then_inc(stored, 16)
            sp.wait_ge(stored, 16 * NT)

        @block.gpsimd
        def _(pool):
            step = Links(pool, consts)

            def norm_gain_product(b):
                if b == 0:
                    pool.wait_ge(x_in[0], 16)
                else:
                    pool.wait_ge(x_ready, NT * (b - 1) + 1)
                pool.wait_ge(gpre_in, 16 * (b + 1))
                pool.tensor_tensor(out=NORMED[:, 0, :], in0=xres[:, 0, :], in1=gpre[:, :], op=ALU.mult).then_inc(xg_done, 1)

            pool.dma_start(gpre[:, :], gain_row(0)).then_inc(gpre_in, 16)
            step(pool.memset(ident[:, :], 0.0))
            step(pool.affine_select(out=ident[:, :], in_=ident[:, :], compare_op=ALU.not_equal, fill=1.0, base=0,
                                    pattern=[[-1, P]], channel_multiplier=1))
            assert step.k == CONST_IDENT
            step(pool.memset(zr[:, :].bitcast(F32), 0.0))
            for weight, col in EPS_COL.items():
                step(pool.memset(col, EPS / weight ** 2))
            assert step.k == CONST_EPS
            norm_gain_product(0)
            pool.dma_start(gpost[:, :], gain_row(1)).then_inc(gpost_in, 16)
            step(pool.memset(prow[:, 1, :], 0.0))
            rows = "(t c) -> t c"
            for dst, src in (
                    (prow[:, 0, :], ssd_conv_w[0].rearrange("k (t c) -> (k t) c", c=P)),
                    (prow[0:32, 1, :], ssd_conv_b[0].rearrange(rows, c=P)),
                    (prow[GG0:GG0 + 8, 1, :], gla_norm[0].rearrange(rows, c=P)),
                    (prow[GS0:GS0 + 16, 1, :], ssd_norm[0].rearrange(rows, c=P)),
                    (prow[GB0:GB0 + 4, 1, :], gla_b_gk[0].rearrange(rows, c=P)),
                    (hb[:, 0, :], ssd_A_log.broadcast_to([P, SSD_H])),
                    (hb[:, 1, :], ssd_D.broadcast_to([P, SSD_H])),
                    (hb[:, 2, :], ssd_dt_bias.broadcast_to([P, SSD_H])),
                    (wgk, gla_w_gk2[0]),
                    (lrw[:, :, :], gla_w_in[0].rearrange("(k p) n -> p k n", p=P)[:, :, 3072:3072 + GLA_RANK]),
                    (dtw[:, :, :], ssd_w_in[0].rearrange("(k p) n -> p k n", p=P)[:, :, 6144:6144 + SSD_H])):
                pool.dma_start(dst, src).then_inc(params_in, 16)
            step(pool.memset(tri[:, :], 1.0))
            step(pool.affine_select(out=tri[:, :], in_=tri[:, :], compare_op=ALU.is_ge, fill=0.0, base=0,
                                    pattern=[[1, P]], channel_multiplier=-1))
            step(pool.memset(tri[0:CH, CH:P], 0.0))
            step(pool.memset(blk[:, :], 0.0))
            step(pool.memset(half[:, :, :], 0.0))
            for c in range(2):
                r = slice(c * CH, (c + 1) * CH)
                step(pool.tensor_copy(mask[r, :], tri[r, r]))
                step(pool.memset(blk[r, r], 1.0))
                step(pool.memset(half[r, c, :], 1.0))
            step(pool.memset(feat[:, :, 0:CONV - 1], 0.0))
            assert step.k == CONST_ALL

            def side_products(g, proj, scan, outp):
                if not scan:
                    return
                G = groups_before("ssd")
                hs = bass.ds((g - 1) * HPG, HPG)

                def heads(ap, n):
                    return ap.rearrange("p t (h o) -> p t h o", o=1).broadcast_to([P, n, HPG, HD])

                def by_head(buf):
                    return buf[:, :, :].rearrange("p t (h d) -> p t h d", h=HPG)
                pool.wait_ge(tok_out, g - 1 + G + 1)
                pool.tensor_tensor(out=by_head(xw), in0=by_head(xtok), in1=heads(dtv[:, WST, :, hs], NT),
                                   op=ALU.mult).then_inc(tok_mul, 1)
                pool.tensor_tensor(out=by_head(xdt), in0=by_head(xtok), in1=heads(dtv[:, DT, :, hs], NT),
                                   op=ALU.mult).then_inc(tok_mul, 1)
                if not (isinstance(g, int) and g == 1):
                    pool.wait_ge(y_out, 2 * (g - 1 + G))
                for t in range(NT):
                    pool.tensor_tensor(out=by_head(dx)[:, t], in0=by_head(xtok)[:, t],
                                       in1=hb[:, 1, hs].rearrange("p (h o) -> p h o", o=1).broadcast_to([P, HPG, HD]),
                                       op=ALU.mult).then_inc(tok_mul, 1)

            for b in range(NPH):
                if b > 0:
                    norm_gain_product(b)
                pool.wait_ge(xn_ready, NT * (b + 1))
                if b > 0:
                    pool.dma_start(gpost[:, :], gain_row(2 * b + 1)).then_inc(gpost_in, 16)
                if b + 1 < NPH:
                    pool.dma_start(gpre[:, :], gain_row(2 * b + 2)).then_inc(gpre_in, 16)
                if PHASES[b][0] == "ssd":
                    pool.wait_ge(ssd_dve, 2)
                    for t in range(NT):
                        pool.tensor_tensor(
                            out=R_ROWS[t].rearrange("p (h i) -> p h i", i=CH),
                            in0=dtv[:, DA, t, :].rearrange("p (h i) -> p h i", i=1).broadcast_to([P, SSD_H, CH]),
                            in1=mask[:, :].rearrange("p (h i) -> p h i", h=1).broadcast_to([P, SSD_H, CH]),
                            op=ALU.mult).then_inc(ssd_r, 1)
                    pool.wait_ge(ssd_dve, SSD_WEIGHTS)
                    pool.wait_ge(ssd_mm, 5)
                    pipeline(pool, SSD_G, side_products)

        @block.scalar
        def _(act):
            def hi(slot, count):
                act.wait_ge(loaded[slot], (count + 1) * 32)
                if not (isinstance(count, int) and count == 0):
                    act.wait_ge(tile_mm[slot], count * 2)
                act.activation(ws[:, slot, 0, :], raw[:, slot, :], ACT.Copy).then_inc(hi_done[slot], 1)

            def low_halves(slot, count, banks, done, tiles=(0, 1)):
                for c in tiles:
                    act.wait_ge(tile_mm[slot], count * 2 + c + 1)
                    act.activation(lo2[:, c, :], ps[:, banks + c, T:2 * T], ACT.Copy).then_inc(done, 1)

            def tiles_out(slot, count, banks, outs, done):
                for c in range(2):
                    act.wait_ge(tile_mm[slot], count * 2 + c + 1)
                    act.activation(outs[c], ps[:, banks + c, 0:T], ACT.Copy).then_inc(done, 1)

            def norm(b):
                if b > 0:
                    act.wait_ge(sqrt_ready, b)
                act.activation(DUMMY, EPS_COL[1.0], ACT.Sqrt).then_inc(sqrt_ready, 1)

                def mean_root(src, col, squares, roots, count, weight=1.0):
                    act.activation(JUNK, src, ACT.Square, accum_out=sm[:, col:col + 1]).then_inc(squares, 1)
                    act.wait_ge(squares, count)
                    act.activation(sm[:, col + 4:col + 5], sm[:, col:col + 1], ACT.Sqrt,
                                   scale=1.0 / (D * weight ** 2), bias=EPS_COL[weight]).then_inc(roots, 1)
                if b > 0:
                    for t in range(NT):
                        act.wait_ge(tile_mm[SLOT_DOWN], 2 * used_before(b, SLOT_DOWN) - 1 + t)
                        mean_root(ps[:, 2 * t:2 * t + 2, :].rearrange("p b n -> p (b n)"), t, sq_post, root_post,
                                  NT * (b - 1) + t + 1, weight_of(b - 1))
                if b == NPH:
                    return
                for t in range(NT):
                    if b == 0:
                        act.wait_ge(x_in[t], 16)
                    else:
                        act.wait_ge(x_ready, NT * (b - 1) + t + 1)
                    mean_root(xres[:, t, :], 2 + t, sq_pre, root_pre, NT * b + t + 1)
                if b == 0:
                    hi(SLOT_GATE, 0)
                if PHASES[b][0] == "gla":
                    act.wait_ge(params_in, 16 * 11)
                    act.activation(sw[:, :, 0, 0:GLA_RANK], lrw[:, :, :], ACT.Copy).then_inc(small_hi, 1)
                if PHASES[b][0] == "ssd":
                    act.activation(sw[:, :, 0, :], dtw[:, :, :], ACT.Copy).then_inc(small_hi, 1)
                for t in range(NT):
                    for q in range(2):
                        act.wait_ge(xnT, 2 * NT * b + 2 * t + q + 1)
                        act.activation(xT[:, 4 * q:4 * q + 4, 0, t * P:(t + 1) * P],
                                       ps[:, A + 2 * t + q, :].rearrange("p (k n) -> p k n", k=4),
                                       ACT.Copy).then_inc(xT_hi, 1)

            def ffn(ph):
                f = ffns_before(ph) * NF * 2
                n0 = [used_before(ph, s) for s in range(4)]
                last = ph == NPH - 1

                def gate(i, split_next):
                    low_halves(SLOT_GATE, i + n0[SLOT_GATE], A, gate_lo)
                    if split_next:
                        hi(SLOT_GATE, i + n0[SLOT_GATE] + 1)

                def body(i, split_next, split_after):
                    for c in range(2):
                        act.wait_ge(gate_sum, i * 2 + f + c + 1)
                        act.activation(fm[:, c, :], ca[:, c, :], ACT.Silu).then_inc(silu_g, 1)
                    hi(SLOT_DOWN, i + n0[SLOT_DOWN])
                    for c in range(2):
                        low_halves(SLOT_UP, i + n0[SLOT_UP], C, up_lo, (c,))
                        act.wait_ge(h_done, i * 2 + f + c + 1)
                        act.activation(hT[:, c, 0, :], fm[:, 2 + c, :], ACT.Copy).then_inc(h_hi, 1)
                    if split_next:
                        hi(SLOT_UP, i + n0[SLOT_UP] + 1)
                    if split_after is not None:
                        gate(i + 1, split_after)
                gate(0, True)
                if ph == 0:
                    body(0, True, True)
                with act.Fori(1 if ph == 0 else 0, NF - 2 if last else NF - 1) as i:
                    body(i, True, True)
                if last:
                    body(NF - 2, True, False)
                body(NF - 1, not last, None)

            def gla_start(n0):
                act.wait_ge(cols_T, 1)
                act.activation(pcol[:, :, :].rearrange("p a n -> p (a n)"), ps[:, B, 0:256], ACT.Copy).then_inc(cols_done, 1)
                act.wait_ge(small_mm, 1)
                act.activation(lrT, ps[0:GLA_RANK, C, 0:T], ACT.Copy).then_inc(small_out, 1)
                hi(SLOT_P3, n0[SLOT_P3])
                et = scr[:, 0, 1024:2048]
                act.wait_ge(gla_dve, 1)
                act.activation(et, et, ACT.Exp, scale=-1.0).then_inc(gla_act, 1)
                tiles_out(SLOT_P1, n0[SLOT_P1], A, [ca[:, c, :] for c in range(2)], p1_out)
                act.wait_ge(gla_act, 1)
                act.activation(et, et, ACT.Ln, bias=1.0).then_inc(gla_act, 1)
                tiles_out(SLOT_P2, n0[SLOT_P2], A, [zf[:, t, :] for t in range(2)], p2_out)
                hi(SLOT_P1, n0[SLOT_P1] + 1)
                b16, dm, de = scr[:, 0, 0:1024], scr[:, 0, 1024:2048], scr[:, 1, 0:1024]
                nrm = 1.0 / 16.0
                act.wait_ge(gla_dve, 3)
                act.activation(exps[:, 2048:3072], b16, ACT.Exp, scale=nrm).then_inc(gla_act, 1)
                act.activation(edl[:, 0, 0:16], b16.rearrange("p (n i) -> p n i", i=CH)[:, :, CH - 1], ACT.Exp,
                               scale=nrm).then_inc(gla_act, 1)
                act.wait_ge(gla_dve, 4)
                act.activation(exps[:, 0:1024], dm, ACT.Exp, scale=nrm).then_inc(gla_act, 1)
                act.activation(exps[:, 1024:2048], dm, ACT.Exp, scale=-nrm).then_inc(gla_act, 1)
                act.wait_ge(gla_dve, 5)
                act.activation(exps[:, 3072:4096], de, ACT.Exp, scale=nrm).then_inc(gla_act, 1)
                hi(SLOT_P2, n0[SLOT_P2] + 1)
                tiles_out(SLOT_P3, n0[SLOT_P3], C, [vs[:, t, :] for t in range(2)], p3_out)

            def ssd_start(n0):
                act.activation(hb[:, 0, :], hb[:, 0, :], ACT.Exp).then_inc(ssd_act, 1)
                act.wait_ge(small_mm, 2)
                act.activation(dtT, ps[0:SSD_H, C, 0:T], ACT.Copy).then_inc(small_out, 1)
                act.wait_ge(ssd_dve, 1)
                act.activation(dtv[:, TB, :, :], dtv[:, TB, :, :], ACT.Exp, scale=-1.0).then_inc(ssd_act, 1)
                tiles_out(SLOT_P1, n0[SLOT_P1], A, [feat[:, c, CONV - 1:] for c in range(2)], p1_out)
                hi(SLOT_P3, n0[SLOT_P3])
                act.wait_ge(ssd_dve, 3)
                act.activation(dtv[:, CDEC, :, :], dtv[:, CS, :, :], ACT.Exp).then_inc(ssd_act, 1)
                act.activation(dtv[:, TB, :, :], dtv[:, TA, :, :], ACT.Exp).then_inc(ssd_act, 1)
                act.activation(edl[:, :, :], edl[:, :, :], ACT.Exp).then_inc(ssd_act, 1)
                tiles_out(SLOT_P2, n0[SLOT_P2], A, [feat[:, 2 + c, CONV - 1:] for c in range(2)], p2_out)
                for k in range(4):
                    act.wait_ge(ssd_dve, SSD_WEIGHTS + k + 1)
                    act.activation(exps[:, k * 1024:(k + 1) * 1024], scr[:, 1, (k % 2) * 1024:(k % 2 + 1) * 1024],
                                   ACT.Exp).then_inc(ssd_act, 1)
                    if k == 0:
                        hi(SLOT_P1, n0[SLOT_P1] + 1)
                    if k == 3:
                        hi(SLOT_P2, n0[SLOT_P2] + 1)
                for c in range(4):
                    act.wait_ge(conv_step, 16 if c > 1 else 8)
                    tile = c if c < 2 else 8 * c
                    act.activation(fm[:, c, :], ca[:, c, :], ACT.Silu, bias=pcol[:, 1, tile:tile + 1]).then_inc(feat_done, 1)
                tiles_out(SLOT_P3, n0[SLOT_P3], C, [zf[:, t, :] for t in range(2)], p3_out)

            def mixer(ph, kind, n):
                G = groups_before(kind)
                n0 = [used_before(ph, s) for s in range(4)]
                ssd = kind == "ssd"
                gain0 = GS0 if ssd else GG0

                def body(g, proj, scan, outp):
                    if not scan and not outp:
                        return
                    first = isinstance(g, int) and g == 1
                    if scan:
                        if not first:
                            if ssd:
                                act.wait_ge(y_done, g - 1)
                            else:
                                act.wait_ge(y_out, 2 * (g - 1 + G))
                        act.wait_ge(p3_out if ssd else p2_out, 2 * (g - 1 + G) + 2)
                        act.activation(zs[:, :, :], zf[:, :, :], ACT.Silu).then_inc(zs_done, 1)
                    if proj:
                        if not ssd:
                            act.wait_ge(feat_done, 4 * (g + G))
                        tiles_out(SLOT_P1, g + n0[SLOT_P1], A,
                                  [feat[:, c, CONV - 1:] if ssd else ca[:, c, :] for c in range(2)], p1_out)

                    def transposed(bank):
                        act.wait_ge(yT_mm, g - 2 + G + 1)
                        for j in range(2):
                            act.activation(hT[:, j, 0, :], ps[:, bank, j * T:(j + 1) * T], ACT.Copy,
                                           scale=pcol[:, 1, bass.ds(2 * g + (gain0 - 4 + j), 1)]).then_inc(yT_hi, 1)
                    if outp and (proj or not scan):
                        transposed(C)
                    if scan:
                        act.wait_ge(tok_T, g - 1 + G + 1)
                        if ssd:
                            if not first:
                                act.wait_ge(tok_mul, 4 * (g - 1))
                            act.activation(xtok[:, :, :].rearrange("p t n -> p (t n)"), ps[:, E, :],
                                           ACT.Copy).then_inc(tok_out, 1)
                        else:
                            act.activation(xw[:, :, 0:P], ps[:, E, 0:2 * P].rearrange("p (t n) -> p t n", t=2),
                                           ACT.Copy).then_inc(tok_out, 1)
                    if proj:
                        hi(SLOT_P3, g + n0[SLOT_P3])
                        tiles_out(SLOT_P2, g + n0[SLOT_P2], A,
                                  [feat[:, 2 + c, CONV - 1:] if ssd else zf[:, c, :] for c in range(2)], p2_out)
                    if scan and ssd:
                        act.wait_ge(e_mm, g - 1 + G + 1)
                        act.activation(bcb[:, :], ps[:, C, 0:384], ACT.Copy).then_inc(e_out, 1)
                    if scan and not proj:
                        transposed(A)
                    if proj:
                        hi(SLOT_P1, g + n0[SLOT_P1] + 1)
                        hi(SLOT_P2, g + n0[SLOT_P2] + 1)

                    def feature(c):
                        act.wait_ge(conv_step, 16 * g + (16 if c > 1 else 8))
                        tile = 2 * g + c if c < 2 else g + 8 * c
                        act.activation(fm[:, c, :], ca[:, c, :], ACT.Silu,
                                       bias=pcol[:, 1, bass.ds(tile, 1)]).then_inc(feat_done, 1)
                    if proj and ssd:
                        for c in range(2):
                            feature(c)
                    if scan:
                        hi(*out_unit(g - 1, n, n0))
                    if proj and ssd:
                        feature(2)
                    if scan:
                        act.wait_ge(off_mm, g - 1 + G + 1)
                    if proj and ssd:
                        feature(3)
                    if scan:
                        if ssd:
                            act.wait_ge(y_done, g)
                        for t in range(NT):
                            act.activation(JUNK[:, t * 256:(t + 1) * 256], yn[:, t, :] if ssd else ps[:, A + t, 0:256],
                                           ACT.Square, accum_out=sm[:, 8 + t:9 + t]).then_inc(y_sq, 1)
                    if proj:
                        tiles_out(SLOT_P3, g + n0[SLOT_P3], C, [(zf if ssd else vs)[:, t, :] for t in range(2)], p3_out)
                pipeline(act, n, body)

            act.wait_ge(consts, CONST_EPS)
            norm(0)
            hi(SLOT_UP, 0)
            for ph, (kind, layer, which) in enumerate(PHASES):
                if kind == "ffn":
                    ffn(ph)
                elif kind == "gla":
                    gla_start([used_before(ph, s) for s in range(4)])
                    mixer(ph, kind, GLA_H)
                else:
                    ssd_start([used_before(ph, s) for s in range(4)])
                    mixer(ph, kind, SSD_G)
                norm(ph + 1)

        @block.vector
        def _(dve):
            step = Links(dve, dve_step)

            def lo(slot, count):
                dve.wait_ge(hi_done[slot], count + 1)
                low_part(slot, slice(0, UNIT)).then_inc(lo_done[slot], 1)

            def low_part(slot, cols):
                return dve.tensor_tensor(ws[:, slot, 1, cols], raw[:, slot, cols], ws[:, slot, 0, cols].bitcast(F32),
                                         ALU.subtract)

            def sums(low, count, banks, outs, done, tiles=(0, 1)):
                for c in tiles:
                    dve.wait_ge(low, count + c + 1)
                    dve.tensor_tensor(outs[c], ps[:, banks + c, 0:T], lo2[:, c, :], ALU.add).then_inc(done, 1)

            def rsqrt2(ss, width):
                m, y, a, mh = (sm[:, o:o + 2] for o in (16, 18, 20, 22))
                step(dve.tensor_scalar(m, ss, 1.0 / width, EPS, ALU.mult, ALU.add))
                step.start(dve.tensor_scalar(mh, m, -0.5, None, ALU.mult))
                step(dve.tensor_scalar(y.bitcast(I32), m.bitcast(I32), 1, None, ALU.logical_shift_right))
                step(dve.tensor_scalar(y.bitcast(I32), y.bitcast(I32), -1.0, MAGIC, ALU.mult, ALU.add))
                for _ in range(3):
                    for o, wait in ((0, step.start), (1, step)):
                        c = slice(o, o + 1)
                        wait(dve.scalar_tensor_tensor(out=a[:, c], in0=y[:, c], scalar=mh[:, c], in1=y[:, c],
                                                      op0=ALU.mult, op1=ALU.mult))
                    step(dve.scalar_tensor_tensor(out=y, in0=a, scalar=1.5, in1=y, op0=ALU.add, op1=ALU.mult))
                return y

            def inverse_roots(col, squares, roots, count, weight=1.0):
                ss, root = sm[:, col:col + 2], sm[:, col + 4:col + 6]
                mh, y, a = (sm[:, o:o + 2] for o in range(32 + 3 * col, 38 + 3 * col, 2))
                dve.wait_ge(squares, count)
                step.start(dve.tensor_scalar(mh, ss, -0.5 / (D * weight ** 2), -0.5 * EPS / weight ** 2, ALU.mult, ALU.add))
                dve.wait_ge(roots, count)
                step(dve.reciprocal(y, root))
                for c, wait in ((slice(0, 1), step.start), (slice(1, 2), step)):
                    wait(dve.scalar_tensor_tensor(out=a[:, c], in0=y[:, c], scalar=mh[:, c], in1=y[:, c],
                                                  op0=ALU.mult, op1=ALU.mult))
                step(dve.scalar_tensor_tensor(out=y, in0=a, scalar=1.5, in1=y, op0=ALU.add, op1=ALU.mult))
                return y

            def norm(b):
                if b > 0:
                    dve.wait_ge(gpost_in, 16 * b)
                    for t in range(NT):
                        dve.wait_ge(sq_post, NT * (b - 1) + t + 1)
                        dve.tensor_tensor(GAINED[t], ps[:, 2 * t:2 * t + 2, :].rearrange("p b n -> p (b n)"), gpost[:, :],
                                          ALU.mult).then_inc(post_read, 1)
                    r = inverse_roots(0, sq_post, root_post, NT * b, weight_of(b - 1))
                    dve.wait_ge(post_read, NT * b)
                    for t in range(NT):
                        dve.scalar_tensor_tensor(out=xres[:, t, :], in0=GAINED[t], scalar=r[:, t:t + 1],
                                                 in1=xres[:, t, :], op0=ALU.mult, op1=ALU.add).then_inc(x_ready, 1)
                if b == NPH:
                    return
                if b == 0:
                    dve.wait_ge(x_in[1], 16)
                else:
                    dve.wait_ge(x_ready, NT * b)
                dve.wait_ge(gpre_in, 16 * (b + 1))
                step.start(dve.tensor_tensor(NORMED[:, 1, :], xres[:, 1, :], gpre[:, :], ALU.mult))
                r = inverse_roots(2, sq_pre, root_pre, NT * (b + 1))
                for t in range(NT):
                    if t == 0:
                        dve.wait_ge(xg_done, b + 1)
                    dve.tensor_scalar(NORMED[:, t, :], NORMED[:, t, :], r[:, t:t + 1], None, ALU.mult).then_inc(xn_ready, 1)
                if PHASES[b][0] == "gla":
                    dve.wait_ge(small_hi, 1)
                    dve.tensor_tensor(sw[:, :, 1, 0:GLA_RANK], lrw[:, :, :], sw[:, :, 0, 0:GLA_RANK].bitcast(F32),
                                      ALU.subtract).then_inc(small_lo, 1)
                if PHASES[b][0] == "ssd":
                    dve.wait_ge(small_hi, 2)
                    dve.tensor_tensor(sw[:, :, 1, :], dtw[:, :, :], sw[:, :, 0, :].bitcast(F32),
                                      ALU.subtract).then_inc(small_lo, 1)
                for t in range(NT):
                    for q in range(2):
                        dve.wait_ge(xT_hi, 2 * NT * b + 2 * t + q + 1)
                        dve.tensor_tensor(xT[:, 4 * q:4 * q + 4, 1, t * P:(t + 1) * P],
                                          ps[:, A + 2 * t + q, :].rearrange("p (k n) -> p k n", k=4),
                                          xT[:, 4 * q:4 * q + 4, 0, t * P:(t + 1) * P].bitcast(F32),
                                          ALU.subtract).then_inc(xT_lo, 1)

            def ffn(ph):
                f = ffns_before(ph) * NF * 2
                n0 = [used_before(ph, s) for s in range(4)]
                last = ph == NPH - 1

                def body(i, split_next):
                    sums(gate_lo, i * 2 + f, A, [ca[:, c, :] for c in range(2)], gate_sum)
                    if split_next:
                        lo(SLOT_GATE, i + n0[SLOT_GATE] + 1)
                    for c in range(2):
                        if c == 0:
                            dve.wait_ge(hi_done[SLOT_DOWN], i + n0[SLOT_DOWN] + 1)
                            down = low_part(SLOT_DOWN, slice(0, D))
                        else:
                            down = low_part(SLOT_DOWN, slice(D, 2 * D))
                            down.then_inc(lo_done[SLOT_DOWN], 1)
                        sums(up_lo, i * 2 + f, C, [ca[:, 2 + c, :] for c in range(2)], up_sum, (c,))
                        dve.wait_ge(up_sum, i * 2 + f + c + 1)
                        dve.wait_ge(silu_g, i * 2 + f + c + 1)
                        dve.tensor_tensor(fm[:, 2 + c, :], fm[:, c, :], ca[:, 2 + c, :], ALU.mult).then_inc(h_done, 1)
                        dve.wait_ge(h_hi, i * 2 + f + c + 1)
                        dve.tensor_tensor(hT[:, c, 1, :], fm[:, 2 + c, :], hT[:, c, 0, :].bitcast(F32),
                                          ALU.subtract).then_inc(hT_ready, 1)
                    if split_next:
                        lo(SLOT_UP, i + n0[SLOT_UP] + 1)
                with dve.Fori(0, NF - 1 if last else NF) as i:
                    body(i, True)
                if last:
                    body(NF - 1, False)

            def gla_start(n0):
                reset = scr[:, 1, 1024:2048]
                dve.wait_ge(xT_lo, 8)
                step(dve.memset(reset, 1.0))
                dve.memset(reset.rearrange("p (n i) -> p n i", i=CH)[:, :, 0:1], 0.0)
                z, et, g16 = scr[:, 0, 0:1024], scr[:, 0, 1024:2048], scr[:, 1, 0:1024]
                dve.wait_ge(gla_mm, 1)
                dve.wait_ge(cols_done, 1)
                for h in range(GLA_H):
                    step.start(dve.tensor_scalar(z[:, h * T:(h + 1) * T], ps[:, C + h // 2, (h % 2) * T:(h % 2 + 1) * T],
                                                 pcol[:, 1, GB0 + h:GB0 + h + 1], None, ALU.add))
                step.wait()
                dve.scalar_tensor_tensor(out=et, in0=z, scalar=-1.0, in1=z, op0=ALU.mult, op1=ALU.max).then_inc(gla_dve, 1)
                lo(SLOT_P3, n0[SLOT_P3])
                dve.wait_ge(gla_act, 2)
                dve.scalar_tensor_tensor(out=g16, in0=z, scalar=0.0, in1=et, op0=ALU.min, op1=ALU.subtract).then_inc(gla_dve, 1)
                dve.wait_ge(gla_dve, 2)
                dve.tensor_tensor_scan(out=z, data0=reset, data1=g16, initial=0.0, op0=ALU.mult,
                                       op1=ALU.add).then_inc(gla_dve, 1)
                dve.wait_ge(gla_dve, 3)

                def chunks(ap):
                    return ap.rearrange("p (n i) -> p n i", i=CH)
                dve.tensor_tensor(chunks(et), chunks(z), chunks(z)[:, :, CH // 2:CH // 2 + 1].broadcast_to([P, 16, CH]),
                                  ALU.subtract).then_inc(gla_dve, 1)
                lo(SLOT_P1, n0[SLOT_P1] + 1)
                dve.tensor_tensor(chunks(g16), chunks(z)[:, :, CH - 1:CH].broadcast_to([P, 16, CH]), chunks(z),
                                  ALU.subtract).then_inc(gla_dve, 1)
                dve.wait_ge(gla_act, 7)
                decayed(0, 0, (2, 0, 1, 3))
                lo(SLOT_P2, n0[SLOT_P2] + 1)

            def decayed(g, count, which):
                dve.wait_ge(p1_out, count + 2)
                for o in which:
                    dve.scalar_tensor_tensor(out=fm[:, o, :], in0=ca[:, o % 2, :], scalar=1.0 if o % 2 else P ** -0.5,
                                             in1=exps[:, bass.ds(g * T + o * 1024, T)],
                                             op0=ALU.mult, op1=ALU.mult).then_inc(feat_done, 1)

            def convolution(g, c0):
                for k in range(CONV):
                    for j in range(2):
                        c = c0 + j
                        tile = 2 * g + c if c < 2 else g + 8 * c
                        src, tap = feat[:, c, k:k + T], pcol[:, 0, bass.ds(tile + 32 * k, 1)]
                        if k == 0:
                            ins = dve.tensor_scalar(ca[:, c, :], src, tap, None, ALU.mult)
                        else:
                            dve.wait_ge(conv_step, 16 * g + (4 * c0 + 2 * k + j - 1))
                            ins = dve.scalar_tensor_tensor(out=ca[:, c, :], in0=src, scalar=tap, in1=ca[:, c, :],
                                                           op0=ALU.mult, op1=ALU.add)
                        ins.then_inc(conv_step, 1)

            def ssd_start(n0):
                v = [dtv[:, r, :, :] for r in range(8)]

                def over_t(ap):
                    return ap.rearrange("p (t h) -> p t h", t=1).broadcast_to([P, NT, SSD_H])
                dve.wait_ge(dt_T, 1)
                step(dve.tensor_tensor(v[TA], ps[:, E, 0:NT * SSD_H].rearrange("p (t h) -> p t h", t=NT),
                                       over_t(hb[:, 2, :]), ALU.add))
                dve.scalar_tensor_tensor(out=v[TB], in0=v[TA], scalar=-1.0, in1=v[TA], op0=ALU.mult, op1=ALU.max).then_inc(ssd_dve, 1)
                e, den, s, s2, q = v[TB], v[DT], v[CS], v[CSL], v[WST]
                dve.wait_ge(ssd_act, 2)
                step(dve.tensor_scalar(den, e, 2.0, None, ALU.add))
                step(dve.reciprocal(den, den))
                step(dve.tensor_tensor(s, e, den, ALU.mult))
                step(dve.tensor_tensor(s2, s, s, ALU.mult))
                step(dve.tensor_scalar(q, s2, 1.0 / 15, None, ALU.mult))
                for c in (13, 11, 9, 7, 5, 3):
                    step(dve.scalar_tensor_tensor(out=q, in0=q, scalar=1.0 / c, in1=s2, op0=ALU.add, op1=ALU.mult))
                step(dve.scalar_tensor_tensor(out=q, in0=q, scalar=1.0, in1=s, op0=ALU.add, op1=ALU.mult))
                step(dve.tensor_scalar(v[TA], v[TA], 0.0, None, ALU.max))
                step(dve.scalar_tensor_tensor(out=v[DT], in0=q, scalar=2.0, in1=v[TA], op0=ALU.mult, op1=ALU.add))
                dve.scalar_tensor_tensor(out=v[DA], in0=v[DT], scalar=-1.0, in1=over_t(hb[:, 0, :]), op0=ALU.mult,
                                         op1=ALU.mult).then_inc(ssd_dve, 1)
                lo(SLOT_P3, n0[SLOT_P3])
                dve.wait_ge(ssd_mm, 1)
                step(dve.tensor_copy(dtv[:, CS:CSL + 1, :, :].rearrange("p a t h -> p (a t h)"), ps[:, C, 0:128]))
                step(dve.tensor_copy(edl[:, :, :].rearrange("p c h -> p (c h)"), ps[:, C, 128:256]))
                dve.tensor_tensor(v[TA], v[CSL], v[CS], ALU.subtract).then_inc(ssd_dve, 1)
                G = groups_before("ssd")
                dve.wait_ge(p1_out, 2 * G + 2)
                convolution(0, 0)
                dve.wait_ge(ssd_act, 5)
                dve.tensor_tensor(v[WST], v[TB], v[DT], ALU.mult).then_inc(ssd_dve, 1)
                for k in range(4):
                    t, h = k // 2, k % 2
                    seg = scr[:, 1, h * 1024:(h + 1) * 1024].rearrange("p (h i) -> p h i", i=CH)
                    bank = A if h else C
                    dve.wait_ge(ssd_mm, 2 + k)
                    if t:
                        dve.wait_ge(ssd_act, 6 + h)
                    step(dve.tensor_tensor(seg, ps[:, bank:bank + 2, :].rearrange("p b (h i) -> p (b h) i", i=CH),
                                           dtv[:, CS, t, h * 16:(h + 1) * 16].rearrange("p (h i) -> p h i", i=1).broadcast_to([P, 16, CH]),
                                           ALU.subtract))
                    dve.tensor_scalar(seg, seg, 0.0, None, ALU.min).then_inc(ssd_dve, 1)
                lo(SLOT_P1, n0[SLOT_P1] + 1)
                dve.wait_ge(p2_out, 2 * G + 2)
                convolution(0, 2)
                lo(SLOT_P2, n0[SLOT_P2] + 1)

            def mixer(ph, kind, n):
                G = groups_before(kind)
                n0 = [used_before(ph, s) for s in range(4)]
                ssd = kind == "ssd"
                gain0 = GS0 if ssd else GG0

                def by_head(ap):
                    return ap.rearrange("p (h d) -> p h d", h=HPG)

                def heads(ap, rows=P):
                    return ap.rearrange("p (h d) -> p h d", d=1).broadcast_to([rows, HPG, HD])

                def body(g, proj, scan, outp):
                    if not scan and not outp:
                        return
                    first = isinstance(g, int) and g == 1
                    c0 = g * 2 + 2 * G

                    def transposed(bank):
                        for j in range(2):
                            dve.wait_ge(yT_hi, 2 * (g - 2 + G) + 2)
                            dve.scalar_tensor_tensor(out=hT[:, j, 1, :], in0=ps[:, bank, j * T:(j + 1) * T],
                                                     scalar=pcol[:, 1, bass.ds(2 * g + (gain0 - 4 + j), 1)],
                                                     in1=hT[:, j, 0, :].bitcast(F32), op0=ALU.mult,
                                                     op1=ALU.subtract).then_inc(yT_lo, 1)
                    if outp and (proj or not scan):
                        transposed(C)
                    if proj:
                        if ssd:
                            dve.wait_ge(p1_out, c0 + 2)
                            dve.wait_ge(feat_done, 4 * (g + G))
                            convolution(g, 0)
                        lo(SLOT_P3, g + n0[SLOT_P3])
                    if scan:
                        mk = mask[:, :].rearrange("p (t i) -> p t i", t=1).broadcast_to([P, NT, CH])
                        if ssd:
                            dve.wait_ge(e_out, g)
                            cb = bcb[:, 256:384].rearrange("p (t i) -> p t i", t=2)
                            step(dve.tensor_tensor(cb, cb, mk, ALU.mult))
                            for t in range(NT):
                                dve.tensor_tensor(
                                    wm[:, t, :, :],
                                    exps[:, bass.ds(g * HPG * CH + (t * 2048 - HPG * CH), HPG * CH)].rearrange("p (h i) -> p h i", h=HPG),
                                    cb[:, t, :].rearrange("p (h i) -> p h i", h=1).broadcast_to([P, HPG, CH]),
                                    ALU.mult).then_inc(w_done, 1)
                        else:
                            dve.wait_ge(e_mm, g - 1 + G + 1)
                            dve.tensor_tensor(wm[:, :, 0, :], ps[:, C, 0:P].rearrange("p (t i) -> p t i", t=2), mk,
                                              ALU.mult).then_inc(w_done, 2)
                    if scan and not proj:
                        transposed(A)
                    if proj:
                        lo(SLOT_P1, g + n0[SLOT_P1] + 1)
                    if scan:
                        bank = [(E, 0), (C, 0), (E, 256)]
                        for c in range(3):
                            dve.wait_ge(upd_mm, 2 * (g - 1 + G) + (1 if c == 0 else 2))
                            new = ps[:, bank[c][0], bank[c][1]:bank[c][1] + 256]
                            if c == 0:
                                dve.tensor_copy(st[:, 0, :], new).then_inc(state_done, 1)
                                continue
                            dve.wait_ge(state_done, 3 * (g - 1 + G) + c)
                            if ssd:
                                step(dve.tensor_tensor(by_head(st[:, c, :]), by_head(st[:, c - 1, :]),
                                                       heads(edl[:, c, bass.ds((g - 1) * HPG, HPG)]), ALU.mult))
                                dve.tensor_tensor(st[:, c, :], st[:, c, :], new, ALU.add).then_inc(state_done, 1)
                            else:
                                dve.scalar_tensor_tensor(out=st[:, c, :], in0=st[:, c - 1, :],
                                                         scalar=edl[:, 0, bass.ds(4 * g + (c - 4), 1)], in1=new,
                                                         op0=ALU.mult, op1=ALU.add).then_inc(state_done, 1)
                    if proj:
                        if ssd:
                            dve.wait_ge(p2_out, c0 + 2)
                            convolution(g, 2)
                        else:
                            decayed(g, c0, (1, 3, 0))
                    if scan:
                        if not first:
                            dve.wait_ge(yT_mm, g - 1 + G)
                        if ssd:
                            dve.wait_ge(tok_mul, 4 * g)
                            dve.wait_ge(in_mm, g)
                            y_all = yn[:, :, :].rearrange("p t n -> p (t n)")
                            hs = bass.ds((g - 1) * HPG, HPG)
                            step(dve.tensor_tensor(y_all, ps[:, A, :], dx[:, :, :].rearrange("p t n -> p (t n)"), ALU.add))
                            dve.wait_ge(off_mm, g - 1 + G + 1)
                            for t in range(NT):
                                r = slice(CH, P) if t == 0 else slice(0, P)
                                dve.tensor_tensor(by_head(vs[r, t, :]), by_head(ps[r, B, t * 256:(t + 1) * 256]),
                                                  heads(dtv[r, CDEC, t, hs], r.stop - r.start), ALU.mult).then_inc(y_out, 1)
                            for t in range(NT):
                                r = slice(CH, P) if t == 0 else slice(0, P)
                                dve.wait_ge(y_out, 2 * (g - 1 + G) + t + 1)
                                step.start(dve.tensor_tensor(yn[r, t, :], yn[r, t, :], vs[r, t, :], ALU.add))
                            step.wait()
                            dve.wait_ge(zs_done, g - 1 + G + 1)
                            dve.tensor_tensor(y_all, y_all, zs[:, :, :].rearrange("p t n -> p (t n)"), ALU.mult).then_inc(y_done, 1)
                        else:
                            dve.wait_ge(zs_done, g - 1 + G + 1)
                            for t in range(NT):
                                dve.wait_ge(y_sq, 2 * (g - 1 + G) + t + 1)
                                dve.tensor_tensor(yn[:, t, :], ps[:, A + t, 0:256], zs[:, t, :], ALU.mult).then_inc(y_out, 1)
                            if proj:
                                decayed(g, c0, (2,))
                    if proj:
                        lo(SLOT_P2, g + n0[SLOT_P2] + 1)
                    elif scan:
                        lo(*out_unit(g - 1, n, n0))
                    if scan:
                        dve.wait_ge(y_sq, 2 * (g - 1 + G) + 2)
                        y = rsqrt2(sm[:, 8:10], 256)
                        if ssd:
                            dve.wait_ge(y_done, g)
                        else:
                            dve.wait_ge(y_out, 2 * (g - 1 + G) + 2)
                        for t in range(NT):
                            dve.tensor_scalar(yn[:, t, :], yn[:, t, :], y[:, t:t + 1], None, ALU.mult).then_inc(yn_done, 1)
                    if scan and proj:
                        lo(*out_unit(g - 1, n, n0))

                body(0, True, False, False)
                body(1, True, True, False)
                per = SSD_STEPS if ssd else GLA_STEPS
                with dve.Fori(2, n) as g:
                    step.body(g, 2, per)
                    body(g, True, True, True)
                step.after(n - 2, per)
                body(n, False, True, True)
                body(n + 1, False, False, True)

            norm(0)
            lo(SLOT_GATE, 0)
            lo(SLOT_UP, 0)
            dve.wait_ge(consts, CONST_ALL)
            for ph, (kind, layer, which) in enumerate(PHASES):
                if kind == "ffn":
                    ffn(ph)
                elif kind == "gla":
                    gla_start([used_before(ph, s) for s in range(4)])
                    dve.wait_ge(gla_act, 7)
                    mixer(ph, kind, GLA_H)
                else:
                    ssd_start([used_before(ph, s) for s in range(4)])
                    dve.wait_ge(ssd_act, 9)
                    mixer(ph, kind, SSD_G)
                norm(ph + 1)

        @block.tensor
        def _(pe):
            def features(slot, banks, norm=None):
                for c in range(2):
                    bank = ps[:, banks + c, :]
                    for k in range(KD):
                        off = k * UW + c * P
                        if norm is not None and (c, k) == (0, KD // 2):
                            pe.wait_ge(xT_lo, 2 * NT * (norm + 1))
                        pe.matmul(bank, ws[:, slot, 0, off:off + P], xT[:, k, :, :].rearrange("p a t -> p (a t)"),
                                  start=(k == 0), stop=False, skip_group_check=True)
                        mm = pe.matmul(bank[:, 0:T], ws[:, slot, 1, off:off + P], xT[:, k, 0, :],
                                       start=False, stop=(k == KD - 1), skip_group_check=True)
                    mm.then_inc(tile_mm[slot], 1)

            def feature_tiles(slot, banks):
                for c in range(2):
                    for k in range(KD):
                        off = k * UW + c * P
                        for a, b in ((0, 0), (0, 1), (1, 0)):
                            mm = pe.matmul(ps[:, banks + c, 0:T], ws[:, slot, a, off:off + P], xT[:, k, b, :],
                                           start=(k == 0 and a + b == 0), stop=(k == KD - 1 and a == 1),
                                           skip_group_check=True)
                    mm.then_inc(tile_mm[slot], 1)

            def token_tiles(slot, banks):
                for t in range(NT):
                    for k in range(KD):
                        for a, b in ((0, 0), (0, 1), (1, 0)):
                            mm = pe.matmul(ps[:, banks + t, 0:UW], xT[:, k, a, t * P:(t + 1) * P],
                                           ws[:, slot, b, k * UW:(k + 1) * UW],
                                           start=(k == 0 and a + b == 0), stop=(k == KD - 1 and a == 1),
                                           skip_group_check=True)
                    mm.then_inc(tile_mm[slot], 1)

            def open_banks(ph):
                if ph == 0:
                    pe.wait_ge(consts, CONST_EPS)
                else:
                    pe.wait_ge(post_read, NT * ph)
                zeros = zr[:, :].rearrange("p (o n) -> p o n", o=1).broadcast_to([P, 4, P])
                for rnd in range(1 + KEEP_WARM * (ph > 0)):
                    for b in range(4):
                        pe.matmul(ps[:, b, :].rearrange("p (o n) -> p o n", o=4), zr[:, :], zeros, start=(rnd == 0),
                                  stop=False, skip_group_check=True)

            def output(slot, last, rows=(0, 1)):
                for t in range(NT):
                    for n in range(2):
                        for j in rows:
                            for a, b in ((0, 0), (0, 1), (1, 0)):
                                off = j * D + n * 512
                                mm = pe.matmul(ps[:, 2 * t + n, :], hT[:, j, a, t * P:(t + 1) * P],
                                               ws[:, slot, b, off:off + 512], start=False,
                                               stop=(last and j == 1 and a == 1), skip_group_check=True)
                    if 1 in rows:
                        mm.then_inc(tile_mm[slot], 1)

            def split(slot, count):
                pe.wait_ge(lo_done[slot], count + 1)

            def norm(b):
                open_banks(b)
                for t in range(NT):
                    pe.wait_ge(xn_ready, NT * b + t + 1)
                    for q in range(2):
                        for k in range(4):
                            col = (4 * q + k) * P
                            mm = pe.transpose(ps[:, A + 2 * t + q, k * P:(k + 1) * P], NORMED[:, t, col:col + P], ident[:, :])
                        mm.then_inc(xnT, 1)

            def ffn(ph):
                f = ffns_before(ph) * NF * 2
                n0 = [used_before(ph, s) for s in range(4)]
                pe.wait_ge(xT_lo, 2 * NT * (ph + 1) - 1)

                def down(i, last):
                    split(SLOT_DOWN, i + n0[SLOT_DOWN])
                    for j in range(2):
                        pe.wait_ge(hT_ready, i * 2 + f + j + 1)
                        output(SLOT_DOWN, last, (j,))

                def body(i, first):
                    split(SLOT_GATE, i + n0[SLOT_GATE])
                    if not first:
                        pe.wait_ge(gate_sum, i * 2 + f)
                    features(SLOT_GATE, A, ph if first else None)
                    if not first:
                        down(i - 1, False)
                    split(SLOT_UP, i + n0[SLOT_UP])
                    if not first:
                        pe.wait_ge(up_sum, i * 2 + f)
                    features(SLOT_UP, C)
                body(0, True)
                with pe.Fori(1, NF) as i:
                    body(i, False)
                down(NF - 1, True)

            def small(width, norm):
                pe.wait_ge(xT_lo, 2 * NT * (norm + 1) - 1)
                for k in range(KD):
                    if k == KD // 2:
                        pe.wait_ge(xT_lo, 2 * NT * (norm + 1))
                    for a, b in ((0, 0), (0, 1), (1, 0)):
                        mm = pe.matmul(ps[0:width, C, 0:T], sw[:, k, a, 0:width], xT[:, k, b, :],
                                       start=(k == 0 and a + b == 0), stop=(k == KD - 1 and a == 1),
                                       skip_group_check=True)
                mm.then_inc(small_mm, 1)

            def gla_start(ph, n0):
                pe.wait_ge(params_in, 16 * 11)
                pe.wait_ge(xT_lo, 2 * NT * ph + 2)
                for a in range(2):
                    mm = pe.transpose(ps[:, B, a * P:(a + 1) * P], prow[:, a, :], ident[:, :])
                mm.then_inc(cols_T, 1)
                pe.wait_ge(small_lo, 1)
                small(GLA_RANK, ph)
                pe.wait_ge(small_out, 1)
                for h in range(GLA_H):
                    mm = pe.matmul(ps[:, C + h // 2, (h % 2) * T:(h % 2 + 1) * T], wgk[:, h * P:(h + 1) * P], lrT,
                                   start=True, stop=True, skip_group_check=True)
                mm.then_inc(gla_mm, 1)
                split(SLOT_P1, n0[SLOT_P1])
                pe.wait_ge(cols_done, 1)
                feature_tiles(SLOT_P1, A)
                split(SLOT_P2, n0[SLOT_P2])
                pe.wait_ge(p1_out, 2)
                token_tiles(SLOT_P2, A)
                split(SLOT_P3, n0[SLOT_P3])
                pe.wait_ge(gla_dve, 1)
                token_tiles(SLOT_P3, C)

            def ssd_start(ph, n0):
                G = groups_before("ssd")
                pe.wait_ge(small_lo, 2)
                small(SSD_H, ph)
                pe.wait_ge(small_out, 2)
                for t in range(NT):
                    mm = pe.transpose(ps[:, E, t * SSD_H:(t + 1) * SSD_H], dtT[:, t * P:(t + 1) * P], ident[0:SSD_H, 0:SSD_H])
                mm.then_inc(dt_T, 1)
                split(SLOT_P1, n0[SLOT_P1])
                feature_tiles(SLOT_P1, A)
                pe.wait_ge(consts, CONST_ALL)
                pe.wait_ge(ssd_dve, 2)
                for t in range(NT):
                    rhs = dtv[:, DA, t, :]
                    for o, lhs in ((0, tri[:, :]), (64, blk[:, :])):
                        pe.matmul(ps[:, C, o + t * 32:o + (t + 1) * 32], lhs, rhs, start=True, stop=True, skip_group_check=True)
                    for c in range(2):
                        o = 128 + (2 * t + c) * 32
                        mm = pe.matmul(ps[:, C, o:o + 32], half[:, c, :], rhs, start=True, stop=True, skip_group_check=True)
                mm.then_inc(ssd_mm, 1)
                split(SLOT_P2, n0[SLOT_P2])
                pe.wait_ge(p1_out, 2 * G + 2)
                feature_tiles(SLOT_P2, A)
                pe.wait_ge(ssd_dve, 3)
                for k in range(4):
                    t, h = k // 2, k % 2
                    if h == 0:
                        pe.wait_ge(ssd_r, t + 1)
                    if k == 1:
                        pe.wait_ge(p2_out, 2 * G + 2)
                    if t:
                        pe.wait_ge(ssd_dve, SSD_WEIGHTS + h + 1)
                    for b in range(2):
                        mm = pe.matmul(ps[:, (A if h else C) + b, :], blk[:, :],
                                       R_ROWS[t][:, (2 * h + b) * 512:(2 * h + b + 1) * 512], start=True, stop=True,
                                       skip_group_check=True)
                    mm.then_inc(ssd_mm, 1)
                split(SLOT_P3, n0[SLOT_P3])
                pe.wait_ge(ssd_dve, SSD_WEIGHTS + 3)
                token_tiles(SLOT_P3, C)
                pe.wait_ge(ssd_dve, SSD_WEIGHTS + 4)

            def mixer(ph, kind, n):
                G = groups_before(kind)
                n0 = [used_before(ph, s) for s in range(4)]
                ssd = kind == "ssd"

                def body(g, proj, scan, outp):
                    if not scan and not outp:
                        return
                    first = isinstance(g, int) and g == 1
                    last = not proj and not scan
                    c0 = g * 2 + 2 * G
                    if proj:
                        split(SLOT_P1, g + n0[SLOT_P1])
                        if scan and not first:
                            pe.wait_ge(y_out, c0 - 2)
                        if scan:
                            pe.wait_ge(p2_out, c0)
                        feature_tiles(SLOT_P1, A)

                    def transpose_rows(bank):
                        pe.wait_ge(yn_done, 2 * (g - 2 + G) + 2)
                        for j in range(2):
                            for t in range(NT):
                                mm = pe.transpose(ps[:, bank, j * T + t * P:j * T + (t + 1) * P],
                                                  yn[:, t, j * P:(j + 1) * P], ident[:, :])
                        mm.then_inc(yT_mm, 1)

                    def add_output():
                        split(*out_unit(g - 2, n, n0))
                        pe.wait_ge(yT_lo, 2 * (g - 2 + G) + 2)
                        output(out_unit(g - 2, n, n0)[0], last)
                    if outp and (proj or not scan):
                        if scan:
                            pe.wait_ge(p3_out, c0)
                        transpose_rows(C)
                    if scan:
                        pe.wait_ge(feat_done, 4 * (g - 1 + G) + (2 if ssd else 4))
                        pe.wait_ge(p3_out, 2 * (g - 1 + G) + 2)
                        for t in range(NT):
                            if ssd:
                                for j in range(2):
                                    o = (2 * t + j) * P
                                    mm = pe.transpose(ps[:, E, o:o + P], fm[:, j, t * P:(t + 1) * P], ident[:, :])
                            else:
                                mm = pe.transpose(ps[:, E, t * P:(t + 1) * P], fm[:, 3, t * P:(t + 1) * P], ident[:, :])
                        mm.then_inc(tok_T, 1)
                    if proj:
                        split(SLOT_P2, g + n0[SLOT_P2])
                        pe.wait_ge(p1_out, c0 + 2)
                        if ssd:
                            feature_tiles(SLOT_P2, A)
                        else:
                            token_tiles(SLOT_P2, A)
                    if scan:
                        if outp and proj:
                            pe.wait_ge(yT_lo, 2 * (g - 2 + G) + 2)
                        pe.wait_ge(feat_done, 4 * (g - 1 + G) + 4)
                        if ssd:
                            for t in range(NT):
                                pe.transpose(ps[:, C, t * P:(t + 1) * P], fm[:, 2, t * P:(t + 1) * P], ident[:, :])
                        for c in range(4):
                            i, o = slice(c * CH, (c + 1) * CH), (256 if ssd else 0) + (c // 2) * CH
                            kv, q = (2, 3) if ssd else (1, 0)
                            r = slice((c % 2) * CH, (c % 2 + 1) * CH)
                            mm = pe.matmul(ps[r, C, o:o + CH], fm[:, kv, i], fm[:, q, i], start=True, stop=True,
                                           skip_group_check=True)
                        mm.then_inc(e_mm, 1)
                    if outp and proj or last:
                        add_output()
                    if scan and not proj:
                        transpose_rows(A)
                    if scan:
                        pe.wait_ge(tok_out, g - 1 + G + 1)
                        if ssd:
                            pe.wait_ge(e_out, g)
                        if not ssd:
                            pe.wait_ge(w_done, 2 * (g - 1 + G) + 2)
                        if ssd:
                            pe.wait_ge(tok_mul, 4 * (g - 1) + 2)
                        if proj:
                            pe.wait_ge(p2_out, c0 + 2)
                        for c, (bank, o) in ((0, (E, 0)), (2, (E, 256)), (1, (C, 0))):
                            r, t = slice((c % 2) * CH, (c % 2 + 1) * CH), c // 2
                            keys = bcb[r, t * P:(t + 1) * P] if ssd else xw[r, t, 0:P]
                            vals = xw[r, t, :] if ssd else vs[r, t, :]
                            if ssd and c == 1:
                                pe.wait_ge(w_done, 2 * (g - 1 + G) + 2)
                            mm = pe.matmul(ps[:, bank, o:o + 256], keys, vals, start=True, stop=True, skip_group_check=True)
                            if c:
                                mm.then_inc(upd_mm, 1)
                        if not proj:
                            pe.wait_ge(yT_lo, 2 * (g - 2 + G) + 2)
                        if ssd:
                            for t in range(NT):
                                for h in range(HPG):
                                    for c in range(2):
                                        r, o = slice(c * CH, (c + 1) * CH), t * 256 + h * HD
                                        mm = pe.matmul(ps[r, A, o:o + HD], wm[r, t, h, :], xdt[r, t, h * HD:(h + 1) * HD],
                                                       start=True, stop=True, skip_group_check=True)
                            mm.then_inc(in_mm, 1)
                        else:
                            for c in range(4):
                                r, t = slice((c % 2) * CH, (c % 2 + 1) * CH), c // 2
                                pe.matmul(ps[r, A + t, 0:256], wm[r, t, 0, :], vs[r, t, :], start=True, stop=(c == 0),
                                          skip_group_check=True)
                        for c in range(1, 4):
                            pe.wait_ge(state_done, 3 * (g - 1 + G) + c)
                            r, t = slice((c % 2) * CH, (c % 2 + 1) * CH), c // 2
                            dst = ps[r, B, t * 256:(t + 1) * 256] if ssd else ps[r, A + t, 0:256]
                            mm = pe.matmul(dst, fm[:, 3 if ssd else 2, c * CH:(c + 1) * CH], st[:, c - 1, :], start=ssd,
                                           stop=True, skip_group_check=True)
                        mm.then_inc(off_mm, 1)
                    if scan and not proj:
                        add_output()
                    if proj:
                        split(SLOT_P3, g + n0[SLOT_P3])
                        if scan:
                            pe.wait_ge(state_done, 3 * (g - 1 + G) + 3)
                        token_tiles(SLOT_P3, C)
                pipeline(pe, n, body)

            norm(0)
            for ph, (kind, layer, which) in enumerate(PHASES):
                if kind == "ffn":
                    ffn(ph)
                else:
                    n0 = [used_before(ph, s) for s in range(4)]
                    if kind == "gla":
                        gla_start(ph, n0)
                        mixer(ph, kind, GLA_H)
                    else:
                        ssd_start(ph, n0)
                        mixer(ph, kind, SSD_G)
                if ph + 1 < NPH:
                    norm(ph + 1)


_INS = ["x", "ffn_w_gate", "ffn_w_up", "ffn_w_down", "norm_gain", "gla_w_in", "gla_w_gk2", "gla_b_gk", "gla_norm",
        "gla_w_out", "ssd_w_in", "ssd_conv_w", "ssd_conv_b", "ssd_dt_bias", "ssd_A_log", "ssd_D", "ssd_norm",
        "ssd_w_out"]


def kernel(**inputs):
    import numpy as np
    import concourse.bacc as bacc
    from concourse.bass_utils import run_bass_kernel_spmd

    nc = bacc.Bacc("TRN2", target_bir_lowering=False, num_devices=1)
    arrays, args = {}, []
    for name in _INS:
        a = np.ascontiguousarray(inputs[name])
        arrays[f"in_{name}"] = a
        args.append(nc.dram_tensor(f"in_{name}", a.shape, mybir.dt.from_np(a.dtype), kind="ExternalInput").ap())
    args.append(nc.dram_tensor("out_y", (1, T, D), F32, kind="ExternalOutput").ap())
    trunk(nc, *args)
    r = run_bass_kernel_spmd(nc, [arrays], core_ids=[0])
    return r.results[0]["out_y"]
```
